# Optimizing a Trainium2 kernel written in Bass

```python
import jax
import jax.numpy as jnp
from jax import lax
import numpy as np

D_MODEL = 1024
BATCH = 1
SEQ = 512
DEPTH = 1

GRID_W = 64
CTX_LEN = 256
N_MOD = 6
EPS = 1e-6
SGU_WIDTH = 1024
SGU_GROUPS = 8
SGU_GROUP_DIM = SGU_WIDTH // SGU_GROUPS
CHUNK = 128
MLA_HEADS = 8
QK_NOPE = 128
QK_ROPE = 64
V_DIM = 128
Q_RANK = 256
KV_RANK = 128
ROPE_THETA = 10000.0
Q_BLOCK = 128
PEER_HEADS = 8
N_KEYS = 128
N_EXPERTS = N_KEYS * N_KEYS
PEER_QK = 256
PEER_HALF = PEER_QK // 2
TOPK_HALF = 16
PEER_TOPK = 16
PEER_BLOCK = 128
OFF_U = 0
OFF_V = OFF_U + SGU_WIDTH
OFF_Q = OFF_V + SGU_WIDTH
OFF_KV = OFF_Q + Q_RANK
OFF_KR = OFF_KV + KV_RANK
OFF_GA = OFF_KR + QK_ROPE
OFF_GB = OFF_GA + D_MODEL
IN_WIDTH = OFF_GB + D_MODEL

kernel_name = 'hybrid_sgu_mla_peer_dit_layer'

def rms_norm(x, g):
    xf = x.astype(jnp.float32)
    y = xf * lax.rsqrt(jnp.mean(xf * xf, axis=-1, keepdims=True) + EPS)
    return (y * g.astype(jnp.float32)).astype(x.dtype)

def modulate(h, shift, scale):
    return h * (1 + scale) + shift

def rope_1d(x, pos):
    quarter = x.shape[-1] // 2
    freqs = ROPE_THETA ** (-jnp.arange(quarter, dtype=jnp.float32) / quarter)
    ang = pos.astype(jnp.float32)[:, None] * freqs[None, :]
    shape = (x.shape[1],) + (1,) * (x.ndim - 3) + (quarter,)
    cos = jnp.cos(ang).reshape(shape).astype(x.dtype)
    sin = jnp.sin(ang).reshape(shape).astype(x.dtype)
    x1, x2 = x[..., :quarter], x[..., quarter:]
    return jnp.concatenate([x1 * cos - x2 * sin, x1 * sin + x2 * cos], axis=-1)

def axial_rope(x, rows, cols):
    half = x.shape[-1] // 2
    return jnp.concatenate([rope_1d(x[..., :half], rows), rope_1d(x[..., half:], cols)], axis=-1)

def mla_q(cq, g_q, w_uq):
    b, t, _ = cq.shape
    q = (rms_norm(cq, g_q) @ w_uq).reshape(b, t, MLA_HEADS, QK_NOPE + QK_ROPE)
    return q[..., :QK_NOPE], q[..., QK_NOPE:]

def mla_kv(ckv, g_kv, w_ukv):
    b, t, _ = ckv.shape
    kv = (rms_norm(ckv, g_kv) @ w_ukv).reshape(b, t, MLA_HEADS, QK_NOPE + V_DIM)
    return kv[..., :QK_NOPE], kv[..., QK_NOPE:]

def attend(qn, qr, kn, kr, v):
    b, t, h, _ = qn.shape
    nb = t // Q_BLOCK
    scale = (QK_NOPE + QK_ROPE) ** -0.5

    def block(args):
        qn_b, qr_b = args
        s = jnp.einsum('bqhd,bkhd->bhqk', qn_b, kn) + jnp.einsum('bqhr,bkr->bhqk', qr_b, kr)
        p = jax.nn.softmax(s.astype(jnp.float32) * scale, axis=-1).astype(v.dtype)
        return jnp.einsum('bhqk,bkhd->bqhd', p, v)

    qn_b = qn.reshape(b, nb, Q_BLOCK, h, QK_NOPE).swapaxes(0, 1)
    qr_b = qr.reshape(b, nb, Q_BLOCK, h, QK_ROPE).swapaxes(0, 1)
    o = lax.map(block, (qn_b, qr_b))
    return o.swapaxes(0, 1).reshape(b, t, h * V_DIM)

def chunk_sgu(u, v, g_sgu, w_s, b_s):
    b, t, _ = u.shape
    v = rms_norm(jax.nn.gelu(v), g_sgu).reshape(b, t // CHUNK, CHUNK, SGU_GROUPS, SGU_GROUP_DIM)
    sv = jnp.einsum('gpq,bnqgc->bnpgc', w_s, v) + b_s.T[:, :, None]
    return jax.nn.gelu(u) * sv.reshape(b, t, SGU_WIDTH)

def merge(o_a, o_b, g_a, g_b, w_pa, w_pb, w_o):
    return (jax.nn.sigmoid(g_a) * (o_a @ w_pa) + jax.nn.sigmoid(g_b) * (o_b @ w_pb)) @ w_o

def peer(h, w_pq, k1, k2, u_exp, v_exp):
    b, t, d = h.shape
    blocks = h.reshape(-1, PEER_BLOCK, d)

    def block(xb):
        q = (xb @ w_pq).reshape(PEER_BLOCK, PEER_HEADS, PEER_QK)
        s1 = jnp.einsum('thd,kd->thk', q[..., :PEER_HALF], k1).astype(jnp.float32)
        s2 = jnp.einsum('thd,kd->thk', q[..., PEER_HALF:], k2).astype(jnp.float32)
        s1t, i1 = lax.top_k(s1, TOPK_HALF)
        s2t, i2 = lax.top_k(s2, TOPK_HALF)
        n_cand = TOPK_HALF * TOPK_HALF
        cand = (s1t[..., :, None] + s2t[..., None, :]).reshape(PEER_BLOCK, PEER_HEADS, n_cand)
        cidx = (i1[..., :, None] * N_KEYS + i2[..., None, :]).reshape(PEER_BLOCK, PEER_HEADS, n_cand)
        top_s, pos = lax.top_k(cand, PEER_TOPK)
        idx = jnp.take_along_axis(cidx, pos, axis=-1)
        gw = jax.nn.softmax(top_s, axis=-1).astype(xb.dtype)
        act = jax.nn.gelu(jnp.einsum('thkd,td->thk', u_exp[idx], xb))
        return jnp.einsum('thk,thkd->td', gw * act, v_exp[idx])

    return lax.map(block, blocks).reshape(b, t, d)

def setup_inputs(seed: int = 0) -> dict:
    key = jax.random.key(seed)
    ks = jax.random.split(key, 26)
    L, D = DEPTH, D_MODEL

    def nrm(k, shape, scale):
        return jax.random.normal(k, shape, jnp.float32) * scale

    def gain(k, shape):
        return 1.0 + 0.05 * jax.random.normal(k, shape, jnp.float32)

    return {
        'x': nrm(ks[0], (BATCH, SEQ, D), 1.0),
        'c': nrm(ks[1], (BATCH, D), 1.0),
        'ctx': nrm(ks[2], (BATCH, CTX_LEN, D), 1.0),
        'c_ctx': nrm(ks[3], (D,), 1.0),
        'w_mod': nrm(ks[4], (L, D, N_MOD * D), 0.5 * D ** -0.5),
        'b_mod': nrm(ks[5], (L, N_MOD * D), 0.02),
        'g_pre1': gain(ks[6], (L, D)),
        'g_post1': gain(ks[7], (L, D)),
        'g_pre2': gain(ks[8], (L, D)),
        'g_post2': gain(ks[9], (L, D)),
        'w_in': nrm(ks[10], (L, D, IN_WIDTH), D ** -0.5),
        'g_q': gain(ks[11], (L, Q_RANK)),
        'g_kv': gain(ks[12], (L, KV_RANK)),
        'w_uq': nrm(ks[13], (L, Q_RANK, MLA_HEADS * (QK_NOPE + QK_ROPE)), Q_RANK ** -0.5),
        'w_ukv': nrm(ks[14], (L, KV_RANK, MLA_HEADS * (QK_NOPE + V_DIM)), KV_RANK ** -0.5),
        'g_sgu': gain(ks[15], (L, SGU_WIDTH)),
        'w_s': nrm(ks[16], (L, SGU_GROUPS, CHUNK, CHUNK), CHUNK ** -0.5),
        'b_s': nrm(ks[17], (L, SGU_GROUPS, CHUNK), 0.02),
        'w_pa': nrm(ks[18], (L, SGU_WIDTH, D), SGU_WIDTH ** -0.5),
        'w_pb': nrm(ks[19], (L, MLA_HEADS * V_DIM, D), (MLA_HEADS * V_DIM) ** -0.5),
        'w_o': nrm(ks[20], (L, D, D), D ** -0.5),
        'w_pq': nrm(ks[21], (L, D, PEER_HEADS * PEER_QK), D ** -0.5),
        'k1': nrm(ks[22], (L, N_KEYS, PEER_HALF), PEER_HALF ** -0.5),
        'k2': nrm(ks[23], (L, N_KEYS, PEER_HALF), PEER_HALF ** -0.5),
        'u_exp': nrm(ks[24], (L, N_EXPERTS, D), D ** -0.5),
        'v_exp': nrm(ks[25], (L, N_EXPERTS, D), D ** -0.5),
    }

def reference(x, c, ctx, c_ctx, w_mod, b_mod, g_pre1, g_post1, g_pre2, g_post2, w_in, g_q, g_kv,
              w_uq, w_ukv, g_sgu, w_s, b_s, w_pa, w_pb, w_o, w_pq, k1, k2, u_exp, v_exp):
    seq_len = x.shape[1]
    n_rows = seq_len // GRID_W
    rr, cc = jnp.meshgrid(jnp.arange(n_rows), jnp.arange(GRID_W), indexing='ij')
    rows, cols = rr.reshape(-1), cc.reshape(-1)
    for l in range(DEPTH):
        update_ctx = l < DEPTH - 1
        sh1x, sc1x, gt1x, sh2x, sc2x, gt2x = jnp.split(
            (jax.nn.silu(c) @ w_mod[l] + b_mod[l])[:, None, :], N_MOD, axis=-1)
        sh1c, sc1c, gt1c, sh2c, sc2c, gt2c = jnp.split(
            (jax.nn.silu(c_ctx) @ w_mod[l] + b_mod[l])[None, None, :], N_MOD, axis=-1)

        hx = modulate(rms_norm(x, g_pre1[l]), sh1x, sc1x)
        hc = modulate(rms_norm(ctx, g_pre1[l]), sh1c, sc1c)
        zx = hx @ w_in[l]
        zc_kv = hc @ w_in[l][:, OFF_KV:OFF_GA]
        kn_c, v_c = mla_kv(zc_kv[..., :KV_RANK], g_kv[l], w_ukv[l])
        kr_c = zc_kv[..., KV_RANK:]
        qn_x, qr_x = mla_q(zx[..., OFF_Q:OFF_KV], g_q[l], w_uq[l])
        qr_x = axial_rope(qr_x, rows, cols)
        kn_x, v_x = mla_kv(zx[..., OFF_KV:OFF_KR], g_kv[l], w_ukv[l])
        kr_x = axial_rope(zx[..., OFF_KR:OFF_GA], rows, cols)
        o_b = attend(qn_x, qr_x,
                     jnp.concatenate([kn_x, kn_c], axis=1),
                     jnp.concatenate([kr_x, kr_c], axis=1),
                     jnp.concatenate([v_x, v_c], axis=1))
        o_a = chunk_sgu(zx[..., OFF_U:OFF_V], zx[..., OFF_V:OFF_Q], g_sgu[l], w_s[l], b_s[l])
        y = merge(o_a, o_b, zx[..., OFF_GA:OFF_GB], zx[..., OFF_GB:], w_pa[l], w_pb[l], w_o[l])
        x = x + gt1x * rms_norm(y, g_post1[l])
        if update_ctx:
            zc = hc @ w_in[l][:, :OFF_KV]
            gc = hc @ w_in[l][:, OFF_GA:]
            qn_c, qr_c = mla_q(zc[..., OFF_Q:OFF_KV], g_q[l], w_uq[l])
            o_bc = attend(qn_c, qr_c, kn_c, kr_c, v_c)
            o_ac = chunk_sgu(zc[..., OFF_U:OFF_V], zc[..., OFF_V:OFF_Q], g_sgu[l], w_s[l], b_s[l])
            yc = merge(o_ac, o_bc, gc[..., :D_MODEL], gc[..., D_MODEL:], w_pa[l], w_pb[l], w_o[l])
            ctx = ctx + gt1c * rms_norm(yc, g_post1[l])

        hx2 = modulate(rms_norm(x, g_pre2[l]), sh2x, sc2x)
        x = x + gt2x * rms_norm(peer(hx2, w_pq[l], k1[l], k2[l], u_exp[l], v_exp[l]), g_post2[l])
        if update_ctx:
            hc2 = modulate(rms_norm(ctx, g_pre2[l]), sh2c, sc2c)
            ctx = ctx + gt2c * rms_norm(peer(hc2, w_pq[l], k1[l], k2[l], u_exp[l], v_exp[l]), g_post2[l])
    return x


_drawn_inputs = setup_inputs


def setup_inputs(seed=0):
    import zlib

    import numpy as np

    out = dict(_drawn_inputs(seed))
    spreads = {}
    factors = {'g_post2': 3.786, 'g_q': 3.999}
    for name, (base, spread) in spreads.items():
        noise = np.random.default_rng([zlib.crc32(name.encode()), seed]).standard_normal(out[name].shape)
        drawn = base * np.exp(spread * noise) if base else spread * noise
        out[name] = jnp.asarray(drawn.astype(out[name].dtype))
    for name, factor in factors.items():
        out[name] = (out[name] * factor).astype(out[name].dtype)
    return out
```

```python
from contextlib import ExitStack, contextmanager

import numpy as np

import concourse.bass as bass
from concourse import mybir

F32 = mybir.dt.float32
U32 = mybir.dt.uint32
I32 = mybir.dt.int32
ACT = mybir.ActivationFunctionType
ALU = mybir.AluOpType
AX = mybir.AxisListType

P = 128
D = 1024
KD = D // P
SEQ = 512
CTX = 256
NT = SEQ // P
NC = CTX // P
KEYS = SEQ + CTX
NKT = KEYS // P
GRID_W = 64
EPS = 1e-6
GROUPS = 8
HEADS = 8
NOPE, ROPE, VD = 128, 64, 128
Q_RANK, KV_RANK = 256, 128
SCALE = (NOPE + ROPE) ** -0.5
OFF_U, OFF_V = 0, 1024
OFF_Q = 2048
OFF_GA = OFF_Q + Q_RANK + KV_RANK + ROPE
OFF_GB = OFF_GA + D
LATENT = Q_RANK + KV_RANK + ROPE
PH = 8
NK = 128
TOP = 16
SLOTS = PH * TOP
CH = 512
RING = 4
PI = 4


class Link:

    def __init__(self, eng, sem):
        self.eng, self.sem, self.n, self.base = eng, sem, 0, 0

    def __call__(self, ins, turn=None):
        ins.then_inc(self.sem, 1)
        self.n += 1
        self.eng.wait_ge(self.sem, self.base + self.n)
        if turn is not None:
            self.eng.sem_inc(turn, 1)

    @contextmanager
    def loop(self, trips, per):
        start = self.base + self.n
        with self.eng.Fori(0, trips) as i:
            self.base, self.n = i * per + start, 0
            yield i
            assert self.n == per, (self.n, per)
        self.base, self.n = start + trips * per, 0


def col(i, n=1):
    return bass.ds(i, n)


def layer(nc, x, c, ctx_in, c_ctx, w_mod, b_mod, g_pre1, g_post1, g_pre2, g_post2, w_in, g_q, g_kv, w_uq, w_ukv,
          g_sgu, w_s, b_s, w_pa, w_pb, w_o, w_pq, k1, k2, u_exp, v_exp, rope_cos, rope_sin, out):
    w_mod_k = w_mod[0].rearrange("(k p) n -> p k n", p=P)
    w_in_k = w_in[0].rearrange("(k p) n -> p k n", p=P)
    w_pa_k, w_pb_k, w_o_k, w_pq_k = (w[0].rearrange("(k p) n -> p k n", p=P) for w in (w_pa, w_pb, w_o, w_pq))
    chunks = [(w_mod_k, s * CH, CH) for s in range(4)]
    chunks += [(w_in_k, OFF_Q, LATENT)]
    chunks += [(w_in_k, OFF_V + s * CH, CH) for s in range(2)]
    chunks += [(w_in_k, OFF_U + s * CH, CH) for s in range(2)]
    FRONT = len(chunks)
    chunks += [(w_mod_k, s * CH, CH) for s in (6, 7, 8, 9, 4, 5, 10, 11)]
    MODS = len(chunks)
    for s in range(2):
        chunks += [(w_in_k, OFF_GA + s * CH, CH), (w_in_k, OFF_GB + s * CH, CH), (w_pa_k, s * CH, CH), (w_pb_k, s * CH, CH)]
    chunks += [(w_o_k, s * CH, CH) for s in range(2)]
    MERGE = len(chunks)
    chunks += [(w_pq_k, s * CH, CH) for s in range(4)]

    with ExitStack() as top:
        sems = {}

        def sem(name):
            if name not in sems:
                sems[name] = top.enter_context(nc.semaphore(name))
            return sems[name]

        def sb(name, shape, dtype=F32, scope=top):
            return scope.enter_context(nc.sbuf_tensor(name, shape, dtype))

        x_sb = sb("x_sb", [P, NT, D])
        hT = sb("hT", [P, KD, SEQ])
        w_ring = sb("w_ring", [P, RING, KD, CH])
        ident = sb("ident", [P, P])
        cols = sb("cols", [P, 96])
        silu_c = sb("silu_c", [P, 2, KD])
        eps = sb("eps", [P, 1])
        gates = sb("gates", [P, 2, D])
        mod2 = sb("mod2", [P, 2, KD])
        PS = top.enter_context(nc.psum_tensor("PS", [P, 8, CH], F32))

        w_load = [sem(f"w_load{r}") for r in range(RING)]
        w_used = sem("w_used")

        def load(sp, n):
            src, at, width = chunks[n]
            sp.dma_start(w_ring[:, n % RING, :, 0:width], src[:, :, at:at + width]).then_inc(w_load[n % RING], 16)

        def load_chunks(sp, first, last):
            for n in range(first, last):
                if n >= RING:
                    sp.wait_ge(w_used, n - RING + 1)
                load(sp, n)

        def chunk(pe, n):
            pe.wait_ge(w_load[n % RING], 16 * (n // RING + 1))
            return w_ring[:, n % RING]

        C_BMOD, C_C, C_PRE1, C_PRE2, C_GQ, C_GKV, C_END = 0, 48, 64, 72, 80, 82, 83

        late = top.enter_context(ExitStack())
        o_aT = sb("o_aT", [P, KD, SEQ], scope=late)
        cqT = sb("cqT", [P, 2, SEQ], scope=late)
        ckvT = sb("ckvT", [P, KEYS], scope=late)
        krT = sb("krT", [P, KEYS], scope=late)

        with ExitStack() as here:
            def tmp(name, shape, dtype=F32):
                return sb(name, shape, dtype, scope=here)

            rows = tmp("rows", [C_END, P])
            ctx_sb = tmp("ctx_sb", [P, NC, D])
            xn = tmp("xn", [P, NT, D])
            junk = gates[:, 0, :]
            gs_rep = gates[:, 1, :]
            hcT = tmp("hcT", [P, KD, CTX])
            ssq = tmp("ssq", [P, NT + NC])
            root = tmp("root", [P, NT + NC])
            rstd = tmp("rstd", [P, NT + NC])
            lsq = tmp("lsq", [P, 2, NT + NC])
            lroot = tmp("lroot", [P, 2, NT + NC])
            lrstd = tmp("lrstd", [P, 2, NT + NC])
            vsq = tmp("vsq", [P, NT])
            vroot = tmp("vroot", [P, NT])
            vrstd = tmp("vrstd", [P, NT])
            mod_raw = tmp("mod_raw", [P, 16, 2])
            mod1 = tmp("mod1", [P, 16, 2])
            a1 = tmp("a1", [P, KD, 2])
            zq = tmp("zq", [P, NT + NC, Q_RANK + KV_RANK])
            krw = tmp("krw", [P, KD, 2, P])
            kr_raw = tmp("kr_raw", [P, 2, SEQ])
            ws_sb = tmp("ws_sb", [P, GROUPS, P])
            wsT = tmp("wsT", [P, GROUPS, P])
            bs_rep = tmp("bs_rep", [P, GROUPS, P])
            cos_sb = tmp("cos_sb1", [P, SEQ])
            sin_sb = tmp("sin_sb1", [P, SEQ])
            cn = ctx_sb

            J_KR = 1 + 1 + KD + KD // 2 + NT + NC
            J_SGU = J_KR + 3 + 2 * NT + 2 + 4 + KD

            vec_in, x_in, ctx_in_s, tab_in = sem("vec_in"), sem("x_in"), sem("ctx_in"), sem("tab_in")
            full, read = sem("bank_full"), sem("bank_read")
            FULL, READ = full, read
            block = here.enter_context(nc.Block())

            @block.sync
            def _(sp):
                sp.dma_start(x_sb[:, :, :], x[0].rearrange("(t p) d -> p t d", p=P)).then_inc(x_in, 16)
                load_chunks(sp, 0, FRONT + RING)

            @block.gpsimd
            def _(pool):
                nc.gpsimd.memset(ident[:, :], 0.0).then_inc(sem("ident_zero"), 1)
                nc.gpsimd.memset(eps[:, :], EPS).then_inc(sem("eps_set"), 1)
                pool.wait_ge(sem("ident_zero"), 1)
                nc.gpsimd.affine_select(out=ident[:, :], in_=ident[:, :], compare_op=ALU.not_equal, fill=1.0, base=0,
                                        pattern=[[-1, P]], channel_multiplier=1).then_inc(sem("ident_set"), 1)
                pool.wait_ge(w_load[4 % RING], 32)
                kr = w_ring[:, 4 % RING, :, Q_RANK + KV_RANK:LATENT]
                for twin in range(2):
                    o = twin * ROPE
                    nc.gpsimd.tensor_copy(krw[:, :, 0, o:o + ROPE], kr).then_inc(sem("krw_set"), 1)
                    for half in range(2):
                        for part in range(2):
                            a, b = o + 32 * half + 16 * part, 32 * half + 16 * (1 - part)
                            nc.gpsimd.tensor_copy(krw[:, :, 1, a:a + 16], kr[:, :, b:b + 16]).then_inc(sem("krw_set"), 1)

            @block.scalar
            def _(act):
                for r0, src in ((C_BMOD, b_mod[0]), (C_C, c[0]), (C_C + 8, c_ctx), (C_PRE1, g_pre1[0]), (C_PRE2, g_pre2[0]),
                                (C_GQ, g_q[0]), (C_GKV, g_kv[0])):
                    v = src.rearrange("(r p) -> r p", p=P)
                    act.dma_start(rows[r0:r0 + v.shape[0], :], v).then_inc(vec_in, 16)
                act.dma_start(ctx_sb[:, :, :], ctx_in[0].rearrange("(t p) d -> p t d", p=P)).then_inc(ctx_in_s, 16)
                act.dma_start(ws_sb[:, :, :], w_s[0].rearrange("g p q -> p g q")).then_inc(tab_in, 16)
                act.dma_start(bs_rep[:, :, :], b_s[0].partition_broadcast(P)).then_inc(tab_in, 16)
                act.dma_start(gs_rep[:, :], g_sgu[0].partition_broadcast(P)).then_inc(tab_in, 16)
                act.dma_start(cos_sb[:, :], rope_cos).then_inc(tab_in, 16)
                act.dma_start(sin_sb[:, :], rope_sin).then_inc(tab_in, 16)
                link = Link(act, sem("act_link1"))
                job = 0

                def take(fn):
                    nonlocal job
                    act.wait_ge(full, job + 1)
                    fn(PS[:, job % 8]).then_inc(read, 1)
                    job += 1

                act.wait_ge(x_in, 16)
                for t in range(NT):
                    link(nc.scalar.activation(junk[:, :], x_sb[:, t, :], ACT.Square, accum_out=ssq[:, t:t + 1]))
                act.wait_ge(ctx_in_s, 16)
                for t in range(NC):
                    link(nc.scalar.activation(junk[:, :], ctx_sb[:, t, :], ACT.Square, accum_out=ssq[:, NT + t:NT + t + 1]))
                act.wait_ge(sem("eps_set"), 1)
                nc.scalar.activation(root[:, :], ssq[:, :], ACT.Sqrt, bias=eps[:, :], scale=1.0 / D).then_inc(sem("root_x"), 1)
                take(lambda b: nc.scalar.copy(cols[:, 0:C_END], b[:, 0:C_END]))
                act.wait_ge(read, 1)
                nc.scalar.activation(silu_c[:, :, :], cols[:, C_C:C_C + 16].rearrange("p (v k) -> p v k", v=2),
                                     ACT.Silu).then_inc(sem("silu_done"), 1)
                take(lambda b: nc.scalar.copy(mod_raw[:, :, :], b[:, 0:32].rearrange("p (m v) -> p m v", v=2)))
                act.wait_ge(sem("mod1_done"), 2)
                for k in range(KD):
                    take(lambda b: nc.scalar.activation(hT[:, k, :], b, ACT.Identity, bias=mod1[:, k, 0:1], scale=a1[:, k, 0:1]))
                for k in range(0, KD, 2):
                    act.wait_ge(full, job + 1)
                    nc.scalar.activation(hcT[:, k, :], PS[:, job % 8, 0:CTX], ACT.Identity, bias=mod1[:, k, 1:2], scale=a1[:, k, 1:2])
                    take(lambda b: nc.scalar.activation(hcT[:, k + 1, :], b[:, CTX:2 * CTX], ACT.Identity,
                                                        bias=mod1[:, k + 1, 1:2], scale=a1[:, k + 1, 1:2]))
                for t in range(NT):
                    take(lambda b: nc.scalar.copy(zq[:, t, :], b[:, 0:Q_RANK + KV_RANK]))
                for t in range(NT, NT + NC):
                    take(lambda b: nc.scalar.copy(zq[:, t, Q_RANK:], b[:, 0:KV_RANK]))
                act.wait_ge(read, job)
                for t in range(NT):
                    link(nc.scalar.activation(junk[:, 0:Q_RANK], zq[:, t, 0:Q_RANK], ACT.Square, accum_out=lsq[:, 0, t:t + 1]))
                for t in range(NT + NC):
                    link(nc.scalar.activation(junk[:, 0:KV_RANK], zq[:, t, Q_RANK:], ACT.Square, accum_out=lsq[:, 1, t:t + 1]))
                nc.scalar.activation(lroot[:, 0, 0:NT], lsq[:, 0, 0:NT], ACT.Sqrt, bias=eps[:, :], scale=1.0 / Q_RANK).then_inc(sem("root_l"), 1)
                nc.scalar.activation(lroot[:, 1, :], lsq[:, 1, :], ACT.Sqrt, bias=eps[:, :], scale=1.0 / KV_RANK).then_inc(sem("root_l"), 1)
                take(lambda b: nc.scalar.copy(kr_raw[:, 0, :], b))
                take(lambda b: nc.scalar.copy(kr_raw[:, 1, :], b))
                take(lambda b: nc.scalar.copy(krT[:, SEQ:KEYS], b[:, 0:CTX]))
                for s in range(2):
                    for t in range(NT):
                        take(lambda b: nc.scalar.activation(xn[:, t, s * CH:(s + 1) * CH], b, ACT.Gelu_apprx_tanh))
                act.wait_ge(read, job)
                for t in range(NT):
                    link(nc.scalar.activation(junk[:, :], xn[:, t, :], ACT.Square, accum_out=vsq[:, t:t + 1]))
                nc.scalar.activation(vroot[:, :], vsq[:, :], ACT.Sqrt, bias=eps[:, :], scale=1.0 / D).then_inc(sem("root_v"), 1)
                for h in range(2):
                    take(lambda b: nc.scalar.copy(wsT[:, 4 * h:4 * h + 4, :], b.rearrange("p (g q) -> p g q", g=4)))
                for k in range(2):
                    take(lambda b: nc.scalar.mul(cqT[:, k, :], b, cols[:, C_GQ + k:C_GQ + k + 1]))
                take(lambda b: nc.scalar.mul(ckvT[:, 0:SEQ], b, cols[:, C_GKV:C_GKV + 1]))
                take(lambda b: nc.scalar.mul(ckvT[:, SEQ:KEYS], b[:, 0:CTX], cols[:, C_GKV:C_GKV + 1]))
                for k in range(KD):
                    take(lambda b: nc.scalar.activation(o_aT[:, k, :], b, ACT.Gelu_apprx_tanh))

            @block.vector
            def _(dve):
                link = Link(dve, sem("dve_link1"))
                dve.wait_ge(sem("root_x"), 1)
                link(nc.vector.reciprocal(rstd[:, :], root[:, :]))
                for t in range(NT):
                    nc.vector.tensor_scalar(xn[:, t, :], x_sb[:, t, :], rstd[:, t:t + 1], None, ALU.mult).then_inc(sem("xn_done"), 1)
                for t in range(NC):
                    nc.vector.tensor_scalar(cn[:, t, :], ctx_sb[:, t, :], rstd[:, NT + t:NT + t + 1], None, ALU.mult).then_inc(sem("xn_done"), 1)
                dve.wait_ge(read, 2)
                bias = cols[:, 0:16].unsqueeze(2).to_broadcast([P, 16, 2])
                gain = cols[:, C_PRE1:C_PRE1 + KD].unsqueeze(2).to_broadcast([P, KD, 2])
                nc.vector.tensor_tensor(mod1[:, :, :], mod_raw[:, :, :], bias, ALU.add).then_inc(sem("mod1_done"), 1)
                dve.wait_ge(sem("mod1_done"), 1)
                nc.vector.scalar_tensor_tensor(out=a1[:, :, :], in0=mod1[:, KD:2 * KD, :], scalar=1.0, in1=gain,
                                               op0=ALU.add, op1=ALU.mult).then_inc(sem("mod1_done"), 1)
                dve.wait_ge(sem("root_l"), 2)
                link(nc.vector.reciprocal(lrstd[:, 0, 0:NT], lroot[:, 0, 0:NT]))
                link(nc.vector.reciprocal(lrstd[:, 1, :], lroot[:, 1, :]))
                for t in range(NT + NC):
                    if t < NT:
                        nc.vector.tensor_scalar(zq[:, t, 0:Q_RANK], zq[:, t, 0:Q_RANK], lrstd[:, 0, t:t + 1], None, ALU.mult).then_inc(sem("zn_done"), 1)
                    nc.vector.tensor_scalar(zq[:, t, Q_RANK:], zq[:, t, Q_RANK:], lrstd[:, 1, t:t + 1], None, ALU.mult).then_inc(sem("zn_done"), 1)
                dve.wait_ge(tab_in, 80)
                dve.wait_ge(read, J_KR + 2)
                link(nc.vector.tensor_tensor(kr_raw[:, 0, :], kr_raw[:, 0, :], cos_sb[:, :], ALU.mult))
                link(nc.vector.tensor_tensor(kr_raw[:, 1, :], kr_raw[:, 1, :], sin_sb[:, :], ALU.mult))
                link(nc.vector.tensor_tensor(krT[:, 0:SEQ], kr_raw[:, 0, :], kr_raw[:, 1, :], ALU.add))
                dve.wait_ge(sem("root_v"), 1)
                link(nc.vector.reciprocal(vrstd[:, :], vroot[:, :]))
                for t in range(NT):
                    nc.vector.scalar_tensor_tensor(out=xn[:, t, :], in0=xn[:, t, :], scalar=vrstd[:, t:t + 1], in1=gs_rep,
                                                   op0=ALU.mult, op1=ALU.mult).then_inc(sem("v_done"), 1)
                for g in range(GROUPS):
                    dve.wait_ge(full, J_SGU + g + 1)
                    dve.wait_ge(read, J_SGU)
                    sv = PS[:, (J_SGU + g) % 8].rearrange("p (n q) -> p n q", n=NT)
                    sv_b = junk[:, (g % 2) * CH:(g % 2 + 1) * CH].rearrange("p (n q) -> p n q", n=NT)
                    link(nc.vector.tensor_tensor(sv_b, sv, bs_rep[:, g, :].unsqueeze(1).to_broadcast([P, NT, P]), ALU.add))
                    nc.vector.tensor_tensor(o_aT[:, g, :], o_aT[:, g, :], junk[:, (g % 2) * CH:(g % 2 + 1) * CH], ALU.mult).then_inc(sem("sgu_done"), 1)

            @block.tensor
            def _(pe):
                job = 0

                def bank(n_free=1):
                    if job >= 8:
                        pe.wait_ge(read, job - 7)
                    return PS[:, job % 8]

                pe.wait_ge(sem("ident_set"), 1)
                pe.wait_ge(vec_in, 7 * 16)
                nc.tensor.transpose(bank()[:, 0:C_END], rows[:, :], ident[0:C_END, 0:C_END]).then_inc(full, 1)
                job += 1
                pe.wait_ge(sem("silu_done"), 1)
                for s in range(4):
                    w = chunk(pe, s)
                    for m in range(4):
                        for k in range(KD):
                            last = nc.tensor.matmul(PS[:, job % 8, 2 * (4 * s + m):2 * (4 * s + m) + 2], w[:, k, m * P:(m + 1) * P], silu_c[:, :, k],
                                                    start=k == 0, stop=k == KD - 1)
                    if s < 3:
                        last.then_inc(w_used, 1)
                    else:
                        last.then_inc(full, 1)
                job += 1
                pe.wait_ge(sem("xn_done"), NT)
                for k in range(KD):
                    b = bank()
                    for t in range(NT):
                        last = nc.tensor.transpose(b[:, t * P:(t + 1) * P], xn[:, t, k * P:(k + 1) * P], ident[:, :])
                        if k == 0 and t == 0:
                            last.then_inc(w_used, 1)
                    last.then_inc(full, 1)
                    job += 1
                pe.wait_ge(sem("xn_done"), NT + NC)
                for k in range(0, KD, 2):
                    b = bank()
                    for i in range(2):
                        for t in range(NC):
                            last = nc.tensor.transpose(b[:, i * CTX + t * P:i * CTX + (t + 1) * P], cn[:, t, (k + i) * P:(k + i + 1) * P], ident[:, :])
                    last.then_inc(full, 1)
                    job += 1
                w = chunk(pe, 4)
                pe.wait_ge(read, 2 + KD)
                for t in range(NT):
                    b = bank()
                    for k in range(KD):
                        last = nc.tensor.matmul(b[:, 0:Q_RANK + KV_RANK], hT[:, k, t * P:(t + 1) * P], w[:, k, 0:Q_RANK + KV_RANK], start=k == 0, stop=k == KD - 1)
                    last.then_inc(full, 1)
                    job += 1
                pe.wait_ge(read, 2 + KD + KD // 2)
                for t in range(NC):
                    b = bank()
                    for k in range(KD):
                        last = nc.tensor.matmul(b[:, 0:KV_RANK], hcT[:, k, t * P:(t + 1) * P], w[:, k, Q_RANK:Q_RANK + KV_RANK], start=k == 0, stop=k == KD - 1)
                    last.then_inc(full, 1)
                    job += 1
                pe.wait_ge(sem("krw_set"), 10)
                assert job == J_KR
                for kind, src, width in ((0, hT, SEQ), (1, hT, SEQ), (0, hcT, CTX)):
                    b = bank()
                    for k in range(KD):
                        last = nc.tensor.matmul(b[:, 0:width], krw[:, k, kind, :], src[:, k, :], start=k == 0, stop=k == KD - 1)
                    last.then_inc(full, 1)
                    job += 1
                for s in range(2):
                    w = chunk(pe, 5 + s)
                    for t in range(NT):
                        b = bank()
                        for k in range(KD):
                            last = nc.tensor.matmul(b, hT[:, k, t * P:(t + 1) * P], w[:, k, :], start=k == 0, stop=k == KD - 1)
                            if t == 0 and s == 0 and k == 0:
                                last.then_inc(w_used, 1)
                            if t == 0 and s == 1 and k == 0:
                                last.then_inc(w_used, 1)
                        last.then_inc(full, 1)
                        job += 1
                pe.wait_ge(tab_in, 80)
                for h in range(2):
                    b = bank()
                    for g in range(4):
                        last = nc.tensor.transpose(b[:, g * P:(g + 1) * P], ws_sb[:, 4 * h + g, :], ident[:, :])
                        if h == 0 and g == 0:
                            last.then_inc(w_used, 1)
                    last.then_inc(full, 1)
                    job += 1
                pe.wait_ge(sem("zn_done"), 2 * NT + NC)
                for k in range(2):
                    b = bank()
                    for t in range(NT):
                        last = nc.tensor.transpose(b[:, t * P:(t + 1) * P], zq[:, t, k * P:(k + 1) * P], ident[:, :])
                    last.then_inc(full, 1)
                    job += 1
                for t0, n in ((0, NT), (NT, NC)):
                    b = bank()
                    for t in range(n):
                        last = nc.tensor.transpose(b[:, t * P:(t + 1) * P], zq[:, t0 + t, Q_RANK:], ident[:, :])
                    last.then_inc(full, 1)
                    job += 1
                for s in range(2):
                    w = chunk(pe, 7 + s)
                    for m in range(4):
                        b = bank()
                        for k in range(KD):
                            last = nc.tensor.matmul(b, w[:, k, m * P:(m + 1) * P], hT[:, k, :], start=k == 0, stop=k == KD - 1)
                            if s == 1 and m == 0 and k == 0:
                                last.then_inc(w_used, 1)
                        last.then_inc(full, 1)
                        job += 1
                assert job == J_SGU
                pe.wait_ge(sem("v_done"), NT)
                for g in range(GROUPS):
                    b = bank()
                    for t in range(NT):
                        last = nc.tensor.matmul(b[:, t * P:(t + 1) * P], xn[:, t, g * P:(g + 1) * P], wsT[:, g, :], start=True, stop=True)
                        if g == 0 and t == 0:
                            last.then_inc(w_used, 1)
                    last.then_inc(full, 1)
                    job += 1

        oT = sb("oT", [P, HEADS, SEQ], scope=late)
        with ExitStack() as here:
            def tmp(name, shape, dtype=F32):
                return sb(name, shape, dtype, scope=here)

            wq = tmp("wq", [P, 2, 2 * (NOPE + ROPE)])
            wkv = tmp("wkv", [P, 2, NOPE + VD])
            wqr = tmp("wqr", [P, 2, 2, P])
            cos_sb = tmp("cos_sb", [P, SEQ])
            sin_sb = tmp("sin_sb", [P, SEQ])
            rot = tmp("rot", [P, 2, SEQ])
            qnT = tmp("qnT", [P, 2, SEQ])
            qrT = tmp("qrT", [P, SEQ])
            knT = tmp("knT", [P, 2, KEYS])
            v_sb = tmp("v_sb", [P, NKT, 2, VD])
            probs = tmp("probs", [P, 2, KEYS])
            pT = tmp("pT", [P, NKT, SEQ])
            top_s = tmp("top_s", [P, 2, 1])
            neg_s = tmp("neg_s", [P, 2, 1])
            den = tmp("den", [P, 2, 1])
            rden = tmp("rden", [P, 2, 1])
            silu_rep = v_sb[:, 0:4, :, :].rearrange("p a b c -> p (a b c)").rearrange("p (k n) -> p k n", k=KD)
            bmod_rep = pT[:, 0:4, :].rearrange("p a n -> p (a n)").rearrange("p (g n) -> p g n", g=2)
            rep_in, pair_in, wqr_set = sem("rep_in"), sem("pair_in"), sem("wqr_set")
            proj_full, proj_read, rope_full, rope_done = sem("proj_full"), sem("proj_read"), sem("rope_full"), sem("rope_done")
            scores_full, max_done, exp_done, probs_done = sem("scores_full"), sem("max_done"), sem("exp_done"), sem("probs_done")
            pt_full, pt_copied, o_full, o_copied = sem("pt_full"), sem("pt_copied"), sem("o_full"), sem("o_copied")
            mod_full, mod_read = sem("mod_full"), sem("mod_read")
            PAIRS, PER = HEADS // 2, 2 * NT
            PROJ = 7
            block = here.enter_context(nc.Block())

            @block.sync
            def _(sp):
                sp.dma_start(cos_sb[:, :], rope_cos).then_inc(rep_in, 16)
                sp.dma_start(sin_sb[:, :], rope_sin).then_inc(rep_in, 16)
                for g, (seg, gain) in enumerate(((2, g_post1), (5, g_post2))):
                    sp.dma_start(gates[:, g, :], gain[0].partition_broadcast(P)).then_inc(rep_in, 16)
                    sp.dma_start(bmod_rep[:, g, :], b_mod[0][seg * D:(seg + 1) * D].partition_broadcast(P)).then_inc(rep_in, 16)

                def load_pair(h):
                    width = 2 * (NOPE + ROPE)
                    sp.dma_start(wq[:, :, :], w_uq[0].rearrange("(k p) n -> p k n", p=P)[:, :, bass.ds(h * width, width)]).then_inc(pair_in, 16)
                    width = 2 * (NOPE + VD)
                    sp.dma_start(wkv[:, :, :].rearrange("p h n -> p (h n)"), w_ukv[0][:, bass.ds(h * width, width)]).then_inc(pair_in, 16)

                load_pair(0)
                load_chunks(sp, FRONT + RING, MODS + RING - 1)
                sp.wait_ge(mod_full, 5)
                load(sp, MODS + RING - 1)
                with sp.Fori(1, PAIRS) as h:
                    sp.wait_ge(proj_full, h * PROJ)
                    load_pair(h)

            @block.tensor
            def _(pe):
                pe.sem_inc(pt_full, 1)
                pe.sem_inc(o_full, 1)
                pe.sem_inc(rope_full, 1)
                for s in range(4):
                    w = chunk(pe, FRONT + s)
                    for m in range(4):
                        for k in range(KD):
                            last = nc.tensor.matmul(PS[:, 0, 4 * s + m:4 * s + m + 1], w[:, k, m * P:(m + 1) * P], silu_c[:, 0, k:k + 1],
                                                    start=k == 0, stop=k == KD - 1)
                            if s and m == 0 and k == 0:
                                last.then_inc(w_used, 1)
                last.then_inc(mod_full, 1)
                pe.wait_ge(sem("rep_set"), 1)
                for s in range(4):
                    w = chunk(pe, FRONT + 4 + s)
                    for k in range(KD):
                        last = nc.tensor.matmul(PS[:, 1 + s, :], silu_rep[:, k, :], w[:, k, :], start=k == 0, stop=k == KD - 1)
                        if k == 0:
                            last.then_inc(w_used, 1)
                    last.then_inc(mod_full, 1)
                pe.wait_ge(mod_read, 5)
                with pe.Fori(0, PAIRS) as h:
                    pe.wait_ge(pair_in, h * 32 + 32)
                    pe.wait_ge(exp_done, h * PER + 1)
                    pe.wait_ge(pt_copied, h * PER + 1)
                    pe.wait_ge(o_copied, h * 2 + 1)
                    for i in range(2):
                        for k in range(2):
                            last = nc.tensor.matmul(PS[:, i, :], wq[:, k, i * (NOPE + ROPE):i * (NOPE + ROPE) + NOPE], cqT[:, k, :], start=k == 0, stop=k == 1)
                        last.then_inc(proj_full, 1)
                    pe.wait_ge(wqr_set, h * 6 + 6)
                    for kind in range(2):
                        for k in range(2):
                            last = nc.tensor.matmul(PS[:, 2 + kind, :], wqr[:, k, kind, :], cqT[:, k, :], start=k == 0, stop=k == 1)
                        last.then_inc(rope_full, 1)
                    for i in range(2):
                        nc.tensor.matmul(PS[:, 4 + 2 * i, :], wkv[:, i, 0:NOPE], ckvT[:, 0:SEQ], start=True, stop=True)
                        nc.tensor.matmul(PS[:, 5 + 2 * i, 0:CTX], wkv[:, i, 0:NOPE], ckvT[:, SEQ:KEYS], start=True, stop=True).then_inc(proj_full, 1)
                    for b in range(3):
                        if b < 2:
                            pe.wait_ge(proj_read, h * PROJ + (b + 1))
                        else:
                            pe.wait_ge(rope_done, h + 1)
                        for t in range(2):
                            last = nc.tensor.matmul(PS[:, b, t * 2 * VD:(t + 1) * 2 * VD], ckvT[:, (2 * b + t) * P:(2 * b + t + 1) * P],
                                                    wkv[:, :, NOPE:NOPE + VD], start=True, stop=True)
                        last.then_inc(proj_full, 1)

                    def scores(n):
                        i, t, b = n // NT, n % NT, 2 * (n % 2)
                        r = slice(i * ROPE, (i + 1) * ROPE)
                        for bb, k0, k1 in ((b, 0, SEQ), (b + 1, SEQ, KEYS)):
                            nc.tensor.matmul(PS[:, bb, 0:k1 - k0], qnT[:, i, t * P:(t + 1) * P], knT[:, i, k0:k1], start=True, stop=False)
                            last = nc.tensor.matmul(PS[:, bb, 0:k1 - k0], qrT[r, t * P:(t + 1) * P], krT[r, k0:k1], start=False, stop=True)
                        last.then_inc(scores_full, 1)

                    pe.wait_ge(proj_read, h * PROJ + PROJ)
                    scores(0)
                    for n in range(PER):
                        if n + 1 < PER:
                            pe.wait_ge(exp_done, h * PER + (n + 1))
                            scores(n + 1)
                        pe.wait_ge(probs_done, h * PER + (n + 1))
                        pe.wait_ge(pt_copied, h * PER + (n + 1))
                        for kt in range(NKT):
                            last = nc.tensor.transpose(PS[:, 4 + kt // 4, kt % 4 * P:(kt % 4 + 1) * P], probs[:, n % 2, kt * P:(kt + 1) * P], ident[:, :])
                        last.then_inc(pt_full, 1)
                        if n % NT == NT - 1:
                            i = n // NT
                            pe.wait_ge(pt_copied, h * PER + (n + 2))
                            pe.wait_ge(o_copied, h * 2 + (i + 1))
                            for kt in range(NKT):
                                last = nc.tensor.matmul(PS[:, 6, :], v_sb[:, kt, i, :], pT[:, kt, :], start=kt == 0, stop=kt == NKT - 1)
                            last.then_inc(o_full, 1)

            @block.scalar
            def _(act):
                act.sem_inc(exp_done, 1)
                act.sem_inc(pt_copied, 1)
                with act.Fori(0, PAIRS) as h:
                    act.wait_ge(pair_in, h * 32 + 32)
                    act.wait_ge(rope_full, h * 2 + 1)
                    for i in range(2):
                        src = wq[:, :, i * (NOPE + ROPE) + NOPE:(i + 1) * (NOPE + ROPE)]
                        nc.scalar.copy(wqr[:, :, 0, i * ROPE:(i + 1) * ROPE], src).then_inc(wqr_set, 1)
                        for part in range(2):
                            dst_v = wqr[:, :, 1, i * ROPE:(i + 1) * ROPE].rearrange("p k (h x q) -> p k h x q", h=2, x=2)[:, :, :, part, :]
                            src_v = src.rearrange("p k (h x q) -> p k h x q", h=2, x=2)[:, :, :, 1 - part, :]
                            nc.scalar.copy(dst_v, src_v).then_inc(wqr_set, 1)
                    job = 0
                    for dst, src in ((qnT[:, 0, :], PS[:, 0, :]), (qnT[:, 1, :], PS[:, 1, :]),
                                     (knT[:, 0, :], PS[:, 4:6, :].rearrange("p b n -> p (b n)")[:, 0:KEYS]),
                                     (knT[:, 1, :], PS[:, 6:8, :].rearrange("p b n -> p (b n)")[:, 0:KEYS]),
                                     *((v_sb[:, 2 * b:2 * b + 2, :, :].rearrange("p t i v -> p (t i v)"), PS[:, b, :]) for b in range(3))):
                        act.wait_ge(proj_full, h * PROJ + (job + 1))
                        nc.scalar.copy(dst, src).then_inc(proj_read, 1)
                        job += 1

                    def exps(n):
                        act.wait_ge(max_done, h * PER + (n + 1))
                        if n:
                            act.wait_ge(pt_full, h * PER + n)
                        s = PS[:, 2 * (n % 2):2 * (n % 2) + 2, :].rearrange("p b n -> p (b n)")[:, 0:KEYS]
                        nc.scalar.activation(probs[:, n % 2, :], s, ACT.Exp, bias=neg_s[:, n % 2, :], scale=SCALE,
                                             accum_out=den[:, n % 2, :]).then_inc(exp_done, 1)

                    exps(0)
                    for n in range(PER):
                        if n + 1 < PER:
                            exps(n + 1)
                        act.wait_ge(pt_full, h * PER + (n + 2))
                        if n % NT == 0:
                            act.wait_ge(o_full, h * 2 + (n // NT + 1))
                        src = PS[:, 4:6, :].rearrange("p b n -> p (b n)")[:, 0:KEYS].rearrange("p (k n) -> p k n", k=NKT)
                        nc.scalar.copy(pT[:, :, n % NT * P:(n % NT + 1) * P], src).then_inc(pt_copied, 1)

            @block.vector
            def _(dve):
                link = Link(dve, sem("dve_link2"))
                dve.sem_inc(o_copied, 1)
                nc.vector.tensor_copy(silu_rep, silu_c[:, 0, :].unsqueeze(2).to_broadcast([P, KD, P])).then_inc(sem("rep_set"), 1)
                dve.wait_ge(mod_full, 1)
                link(nc.vector.tensor_tensor(mod2[:, :, :].rearrange("p a k -> p (a k)"), PS[:, 0, 0:16], cols[:, 3 * KD:5 * KD], ALU.add))
                nc.vector.scalar_tensor_tensor(out=mod2[:, 1, :], in0=mod2[:, 1, :], scalar=1.0, in1=cols[:, C_PRE2:C_PRE2 + KD],
                                               op0=ALU.add, op1=ALU.mult).then_inc(mod_read, 1)
                dve.wait_ge(rep_in, 6 * 16)
                for s in range(4):
                    dve.wait_ge(mod_full, 2 + s)
                    g, part = s // 2, slice(s % 2 * CH, (s % 2 + 1) * CH)
                    link(nc.vector.tensor_tensor(bmod_rep[:, g, part], PS[:, 1 + s, :], bmod_rep[:, g, part], ALU.add))
                    nc.vector.tensor_tensor(gates[:, g, part], bmod_rep[:, g, part], gates[:, g, part], ALU.mult).then_inc(mod_read, 1)
                LINKS = 2 + 2 * PER
                with link.loop(PAIRS, LINKS) as h:
                    for kind, table in ((0, cos_sb), (1, sin_sb)):
                        dve.wait_ge(rope_full, h * 2 + (kind + 2))
                        link(nc.vector.tensor_tensor(rot[:, kind, :], PS[:, 2 + kind, :], table[:, :], ALU.mult))
                    nc.vector.tensor_tensor(qrT[:, :], rot[:, 0, :], rot[:, 1, :], ALU.add).then_inc(rope_done, 1)
                    for n in range(PER):
                        b = n % 2
                        dve.wait_ge(scores_full, h * PER + (n + 1))
                        s = PS[:, 2 * b:2 * b + 2, :].rearrange("p b n -> p (b n)")[:, 0:KEYS]
                        link(nc.vector.reduce_max(top_s[:, b, :], s, AX.X))
                        nc.vector.tensor_scalar(neg_s[:, b, :], top_s[:, b, :], -SCALE, None, ALU.mult).then_inc(max_done, 1)
                        dve.wait_ge(exp_done, h * PER + (n + 2))
                        link(nc.vector.reciprocal(rden[:, b, :], den[:, b, :]))
                        link_free = nc.vector.tensor_scalar(probs[:, b, :], probs[:, b, :], rden[:, b, :], None, ALU.mult)
                        link_free.then_inc(probs_done, 1)
                        if n == NT or n == PER - 1:
                            i = 0 if n == NT else 1
                            dve.wait_ge(o_full, h * 2 + (i + 2))
                            link_o = nc.vector.tensor_copy(oT[:, col(h * 2 + i), :].rearrange("p a n -> p (a n)"), PS[:, 6, :])
                            link_o.then_inc(o_copied, 1)

        full3, read3 = sem("merge_full"), sem("merge_read")
        with ExitStack() as here:
            def tmp(name, shape, dtype=F32):
                return sb(name, shape, dtype, scope=here)

            mT = tmp("mT", [P, KD, SEQ])
            sig = tmp("sig", [P, 2, 2, SEQ])
            prod = tmp("prod", [P, 2, SEQ])
            ysq = tmp("ysq", [P, 2, NT])
            yroot = tmp("yroot", [P, 2, NT])
            yrstd = tmp("yrstd", [P, 2, NT])
            xn2 = mT[:, :, :].rearrange("p k n -> p (k n)").rearrange("p (t d) -> p t d", t=NT)
            sig_done, prod_done, m_done, y_full, y_read = sem("sig_done"), sem("prod_done"), sem("m_done"), sem("y_full"), sem("y_read")
            ysq_done, root3, x1_done, xn2_done = sem("ysq_done"), sem("root3"), sem("x1_done"), sem("xn2_done")
            block = here.enter_context(nc.Block())

            @block.sync
            def _(sp):
                for j in range(4):
                    sp.wait_ge(full3, 4 * 3 + j + 1)
                    load(sp, MODS + RING + j)
                for j in range(4):
                    sp.wait_ge(full3, 16 + 4 * 3 + j + 1)
                    load(sp, MODS + 2 * RING + j)
                for j in range(2):
                    sp.wait_ge(y_full, NT)
                    load(sp, MERGE + 2 + j)

            @block.tensor
            def _(pe):
                for s in range(2):
                    w = [chunk(pe, MODS + 4 * s + j) for j in range(4)]
                    for m in range(4):
                        n, b = 4 * s + m, m % 2 * 4
                        if n >= 2:
                            pe.wait_ge(sig_done, 2 * (n - 1))
                            pe.wait_ge(prod_done, 2 * (n - 1))
                        for j, src in enumerate((hT, hT, o_aT, oT)):
                            for k in range(KD):
                                last = nc.tensor.matmul(PS[:, b + j, :], w[j][:, k, m * P:(m + 1) * P], src[:, k, :], start=k == 0, stop=k == KD - 1)
                            last.then_inc(full3, 1)
                w = [chunk(pe, MODS + 8 + j) for j in range(2)]
                pe.wait_ge(m_done, 8)
                for t in range(NT):
                    for j in range(2):
                        for k in range(KD):
                            last = nc.tensor.matmul(PS[:, 2 * t + j, :], mT[:, k, t * P:(t + 1) * P], w[j][:, k, :], start=k == 0, stop=k == KD - 1)
                    last.then_inc(y_full, 1)
                pe.wait_ge(xn2_done, NT)
                pe.wait_ge(y_read, NT)
                for k in range(KD):
                    for t in range(NT):
                        last = nc.tensor.transpose(PS[:, k, t * P:(t + 1) * P], xn2[:, t, k * P:(k + 1) * P], ident[:, :])
                    last.then_inc(sem("h2_full"), 1)

            @block.scalar
            def _(act):
                for n in range(8):
                    for j in range(2):
                        act.wait_ge(full3, 4 * n + j + 1)
                        if n >= 2:
                            act.wait_ge(prod_done, 2 * (n - 2) + j + 1)
                        nc.scalar.activation(sig[:, n % 2, j, :], PS[:, n % 2 * 4 + j, :], ACT.Sigmoid).then_inc(sig_done, 1)
                act.wait_ge(m_done, 8)
                for t in range(NT):
                    act.wait_ge(y_full, t + 1)
                    y = PS[:, 2 * t:2 * t + 2, :].rearrange("p b n -> p (b n)")
                    scratch = sig[:, t % 2, :, :].rearrange("p a n -> p (a n)")
                    if t >= 2:
                        act.wait_ge(ysq_done, t - 1)
                    nc.scalar.activation(scratch, y, ACT.Square, accum_out=ysq[:, 0, t:t + 1]).then_inc(ysq_done, 1)
                act.wait_ge(ysq_done, NT)
                nc.scalar.activation(yroot[:, 0, :], ysq[:, 0, :], ACT.Sqrt, bias=eps[:, :], scale=1.0 / D).then_inc(root3, 1)
                for t in range(NT):
                    act.wait_ge(x1_done, t + 1)
                    scratch = sig[:, t % 2, :, :].rearrange("p a n -> p (a n)")
                    act.wait_ge(ysq_done, NT + t)
                    nc.scalar.activation(scratch, x_sb[:, t, :], ACT.Square, accum_out=ysq[:, 1, t:t + 1]).then_inc(ysq_done, 1)
                act.wait_ge(ysq_done, 2 * NT)
                nc.scalar.activation(yroot[:, 1, :], ysq[:, 1, :], ACT.Sqrt, bias=eps[:, :], scale=1.0 / D).then_inc(root3, 1)
                for k in range(KD):
                    act.wait_ge(sem("h2_full"), k + 1)
                    nc.scalar.activation(hT[:, k, :], PS[:, k, :], ACT.Identity, bias=mod2[:, 0, k:k + 1], scale=mod2[:, 1, k:k + 1]).then_inc(sem("h2_done"), 1)

            @block.vector
            def _(dve):
                link = Link(dve, sem("dve_link3"))
                for n in range(8):
                    for j in range(2):
                        dve.wait_ge(full3, 4 * n + 2 + j + 1)
                        dve.wait_ge(sig_done, 2 * n + j + 1)
                        if n:
                            dve.wait_ge(m_done, n)
                        nc.vector.tensor_tensor(prod[:, j, :], sig[:, n % 2, j, :], PS[:, n % 2 * 4 + 2 + j, :], ALU.mult).then_inc(prod_done, 1)
                    dve.wait_ge(prod_done, 2 * n + 2)
                    nc.vector.tensor_tensor(mT[:, n, :], prod[:, 0, :], prod[:, 1, :], ALU.add).then_inc(m_done, 1)
                dve.wait_ge(root3, 1)
                link(nc.vector.reciprocal(yrstd[:, 0, :], yroot[:, 0, :]))
                for t in range(NT):
                    y = PS[:, 2 * t:2 * t + 2, :].rearrange("p b n -> p (b n)")
                    scaled = mT[:, 2 * t:2 * t + 2, :].rearrange("p b n -> p (b n)")
                    dve.wait_ge(y_full, NT)
                    nc.vector.scalar_tensor_tensor(out=scaled, in0=y, scalar=yrstd[:, 0, t:t + 1], in1=gates[:, 0, :], op0=ALU.mult, op1=ALU.mult).then_inc(y_read, 1)
                    dve.wait_ge(y_read, t + 1)
                    nc.vector.tensor_tensor(x_sb[:, t, :], x_sb[:, t, :], scaled, ALU.add).then_inc(x1_done, 1)
                dve.wait_ge(root3, 2)
                dve.wait_ge(x1_done, NT)
                link(nc.vector.reciprocal(yrstd[:, 1, :], yroot[:, 1, :]))
                for t in range(NT):
                    nc.vector.tensor_scalar(xn2[:, t, :], x_sb[:, t, :], yrstd[:, 1, t:t + 1], None, ALU.mult).then_inc(xn2_done, 1)
        late.close()

        idx_all = sb("idx_all", [P, NT, SLOTS], I32)
        gw_all = sb("gw_all", [P, NT, SLOTS])
        y2 = sb("y2", [P, NT, D])
        h2 = sb("h2", [P, NT, D])
        with ExitStack() as here:
            def tmp(name, shape, dtype=F32):
                return sb(name, shape, dtype, scope=here)

            qT = tmp("qT", [P, 2 * PH, SEQ])
            k_sb = tmp("k_sb", [P, 2, P])
            kT = tmp("kT", [P, 2, NK])
            q_cur = qT[:, :, 0:P]
            s_cur = tmp("s_cur", [P, 2 * PH, NK])
            s_rest = tmp("s_rest", [P, 2 * PH, NK])
            best = tmp("best", [P, 2 * PH, TOP])
            best_i = tmp("best_i", [P, 2 * PH, TOP], U32)
            best_f = tmp("best_f", [P, 2 * PH, TOP])
            cand = s_cur[:, :, :].rearrange("p h k -> p (h k)").rearrange("p (h c) -> p h c", h=PH)
            cand_rest = s_rest[:, :, :].rearrange("p h k -> p (h k)").rearrange("p (h c) -> p h c", h=PH)
            picks = s_rest[:, :, :].rearrange("p h k -> p (h k)").rearrange("p (s a) -> p s a", a=TOP)
            top_v = tmp("top_v", [P, PH, TOP])
            top_p = tmp("top_p", [P, SLOTS], U32)
            part = tmp("part", [P, 2, SLOTS], U32)
            part_f = tmp("part_f", [P, 2, SLOTS])
            chosen = tmp("chosen", [P, 2, SLOTS])
            expo = tmp("expo", [P, PH, TOP])
            total = tmp("total", [P, PH])
            iota_i = tmp("iota_i", [P, TOP], I32)
            iota_f = tmp("iota_f", [P, TOP])
            k_in, q_full, q_read = sem("k_in"), sem("q_full"), sem("q_read")
            key_full, key_read, s_used, soft_in, soft_out = sem("key_full"), sem("key_read"), sem("s_used"), sem("soft_in"), sem("soft_out")
            LOW = -3.0e38
            block = here.enter_context(nc.Block())

            @block.sync
            def _(sp):
                sp.dma_start(k_sb[:, 0, :], k1[0]).then_inc(k_in, 16)
                sp.dma_start(k_sb[:, 1, :], k2[0]).then_inc(k_in, 16)

            @block.gpsimd
            def _(pool):
                nc.gpsimd.iota(iota_i[:, :], pattern=[[1, TOP]], base=0, channel_multiplier=0).then_inc(sem("iota_set"), 1)
                nc.gpsimd.memset(y2[:, :, :], 0.0).then_inc(sem("y2_zero"), 1)

            @block.tensor
            def _(pe):
                pe.wait_ge(k_in, 32)
                for i in range(2):
                    nc.tensor.transpose(PS[:, 0, i * P:(i + 1) * P], k_sb[:, i, :], ident[:, :]).then_inc(q_full, 1)
                for k in range(0, KD, 2):
                    b = 1 + k // 2 % 2 * 2
                    if k >= 4:
                        pe.wait_ge(q_read, k // 2)
                    for i in range(2):
                        for t in range(NT):
                            last = nc.tensor.transpose(PS[:, b + i, t * P:(t + 1) * P], hT[:, k + i, t * P:(t + 1) * P], ident[:, :])
                    last.then_inc(q_full, 1)
                for n in range(2 * PH):
                    w = chunk(pe, MERGE + n // 4)
                    b = n % 8
                    pe.wait_ge(q_read, 5 if n < 8 else 5 + n - 7)
                    for k in range(KD):
                        last = nc.tensor.matmul(PS[:, b, :], w[:, k, n % 4 * P:(n % 4 + 1) * P], hT[:, k, :], start=k == 0, stop=k == KD - 1)
                    last.then_inc(q_full, 1)
                pe.wait_ge(q_read, 5 + 2 * PH)
                for t in range(NT):
                    if t:
                        pe.wait_ge(key_read, t)
                    for n in range(2 * PH):
                        last = nc.tensor.matmul(PS[:, n // 4, n % 4 * NK:(n % 4 + 1) * NK], qT[:, n, t * P:(t + 1) * P], kT[:, n % 2, :], start=True, stop=True)
                    last.then_inc(key_full, 1)

            @block.scalar
            def _(act):
                act.wait_ge(q_full, 2)
                nc.scalar.copy(kT[:, :, :], PS[:, 0, 0:2 * P].rearrange("p (i n) -> p i n", i=2)).then_inc(q_read, 1)
                for k in range(0, KD, 2):
                    b = 1 + k // 2 % 2 * 2
                    act.wait_ge(q_full, 3 + k // 2)
                    src = PS[:, b:b + 2, :].rearrange("p i (t n) -> p t i n", t=NT)
                    dst = h2[:, :, k * P:(k + 2) * P].rearrange("p t (i n) -> p t i n", i=2)
                    nc.scalar.copy(dst, src).then_inc(q_read, 1)
                for n in range(2 * PH):
                    act.wait_ge(q_full, 6 + n + 1)
                    nc.scalar.copy(qT[:, n, :], PS[:, n % 8, :]).then_inc(q_read, 1)
                with act.Fori(0, NT) as t:
                    act.wait_ge(key_full, t + 1)
                    act.wait_ge(s_used, t + 1)
                    nc.scalar.copy(s_cur[:, :, :].rearrange("p h k -> p (h k)"), PS[:, 0:4, :].rearrange("p b n -> p (b n)")).then_inc(key_read, 1)
                    act.wait_ge(soft_in, t + 1)
                    nc.scalar.activation(expo[:, :, :], expo[:, :, :], ACT.Exp).then_inc(soft_out, 1)

            @block.vector
            def _(dve):
                link = Link(dve, sem("dve_link4"))
                dve.sem_inc(s_used, 1)
                turn = sem("turn")
                dve.wait_ge(sem("iota_set"), 1)
                link(nc.vector.tensor_copy(iota_f[:, :], iota_i[:, :]))

                def top16(values, indices, source, rest, count):
                    for n in range(count):
                        last = nc.vector.max(values(n)[:, 0:8], source[:, n, :])
                    link(last, turn)
                    for n in range(count):
                        nc.vector.max_index(indices(n)[:, 0:8], values(n)[:, 0:8], source[:, n, :])
                        last = nc.vector.match_replace(rest[:, n, :], values(n)[:, 0:8], source[:, n, :], LOW)
                    link(last, turn)
                    for n in range(count):
                        last = nc.vector.max(values(n)[:, 8:16], rest[:, n, :])
                    link(last, turn)
                    for n in range(count):
                        last = nc.vector.max_index(indices(n)[:, 8:16], values(n)[:, 8:16], rest[:, n, :])
                    link(last, turn)

                with link.loop(NT, 23) as t:
                    dve.wait_ge(key_read, t + 1)
                    dve.sem_inc(turn, 1)
                    top16(lambda n: best[:, n, :], lambda n: best_i[:, n, :], s_cur, s_rest, 2 * PH)
                    link(nc.vector.tensor_copy(best_f[:, :, :], best_i[:, :, :]))
                    pair = best[:, :, :].rearrange("p (h i) a -> p h i a", i=2)
                    link(nc.vector.tensor_tensor(cand.rearrange("p h (a b) -> p h a b", a=TOP),
                                                 pair[:, :, 0, :].unsqueeze(3).to_broadcast([P, PH, TOP, TOP]),
                                                 pair[:, :, 1, :].unsqueeze(2).to_broadcast([P, PH, TOP, TOP]), ALU.add), turn)
                    top16(lambda n: top_v[:, n, :], lambda n: top_p[:, n * TOP:(n + 1) * TOP], cand, cand_rest, PH)
                    nc.vector.tensor_tensor(expo[:, :, :], top_v[:, :, :], top_v[:, :, 0:1].to_broadcast([P, PH, TOP]), ALU.subtract).then_inc(soft_in, 1)
                    link(nc.vector.tensor_scalar(part[:, 0, :], top_p[:, :], 4, None, ALU.logical_shift_right))
                    link(nc.vector.tensor_scalar(part[:, 1, :], top_p[:, :], 15, None, ALU.bitwise_and))
                    link(nc.vector.tensor_copy(part_f[:, :, :], part[:, :, :]))
                    index = best_f[:, :, :].rearrange("p (h i) a -> p h i a", i=2)
                    for i in range(2):
                        link(nc.vector.tensor_tensor(picks, part_f[:, i, :].unsqueeze(2).to_broadcast([P, SLOTS, TOP]),
                                                     iota_f[:, :].unsqueeze(1).to_broadcast([P, SLOTS, TOP]), ALU.is_equal))
                        p4 = picks.rearrange("p (h k) a -> p h k a", h=PH)
                        link(nc.vector.tensor_tensor(p4, p4, index[:, :, i, :].unsqueeze(2).to_broadcast([P, PH, TOP, TOP]), ALU.mult))
                        link(nc.vector.tensor_reduce(chosen[:, i, :], picks, AX.X, ALU.add))
                    slot = idx_all[:, col(t), :].rearrange("p a s -> p (a s)")
                    link(nc.vector.scalar_tensor_tensor(out=slot, in0=chosen[:, 0, :], scalar=float(NK), in1=chosen[:, 1, :], op0=ALU.mult, op1=ALU.add))
                    dve.wait_ge(soft_out, t + 1)
                    link(nc.vector.tensor_reduce(total[:, :], expo[:, :, :], AX.X, ALU.add))
                    link(nc.vector.reciprocal(total[:, :], total[:, :]))
                    link(nc.vector.tensor_tensor(gw_all[:, col(t), :].rearrange("p a (h k) -> p (a h) k", h=PH), expo[:, :, :],
                                                 total[:, :].unsqueeze(2).to_broadcast([P, PH, TOP]), ALU.mult))
                    nc.vector.memset(total[:, 0:1], 0.0).then_inc(s_used, 1)

        with ExitStack() as here:
            def tmp(name, shape, dtype=F32):
                return sb(name, shape, dtype, scope=here)

            bufs = w_ring[:, :, :, :].rearrange("p r k n -> p (r k n)").rearrange("p (w s j d) -> p w s j d", w=2, s=2, j=PI)
            u_buf, v_buf = bufs[:, 0], bufs[:, 1]
            idx_cur = tmp("idx_cur", [P, 2, PI], I32)
            dots = tmp("dots", [P, PI])
            acts = tmp("acts", [P, PI])
            coef = tmp("coef", [P, PI])
            product = tmp("product", [P, D])
            zsq = tmp("zsq", [P, NT])
            zroot = tmp("zroot", [P, NT])
            zrstd = tmp("zrstd", [P, NT])
            u_in = [[sem(f"u_in{s}{j}") for j in range(PI)] for s in range(2)]
            v_in = [[sem(f"v_in{s}{j}") for j in range(PI)] for s in range(2)]
            dots_done, acts_done, coef_done, v_used, idx_set = sem("dots_done"), sem("acts_done"), sem("coef_done"), sem("v_used"), sem("idx_set")
            out_done, z_sq, z_out = sem("out_done"), sem("z_sq"), sem("z_out")
            GROUPS_T = SLOTS // PI
            TRIPS = NT * GROUPS_T
            idx_flat = idx_all[:, :, :].rearrange("p t s -> p (t s)")
            gw_flat = gw_all[:, :, :].rearrange("p t s -> p (t s)")
            block = here.enter_context(nc.Block())

            @block.gpsimd
            def _(pool):
                def group(i, s, first):
                    if not first:
                        pool.wait_ge(v_used, i * (2 * PI) + ((s - 1) * PI + 1))
                        pool.sem_inc(sem("pool_turn"), 1)
                    nc.gpsimd.tensor_copy(idx_cur[:, s, :], idx_flat[:, bass.ds(i * (2 * PI) + s * PI, PI)]).then_inc(idx_set, 1)
                    pool.wait_ge(idx_set, i * 2 + (s + 1))
                    pool.sem_inc(sem("pool_turn"), 1)
                    for j in range(PI):
                        at = bass.IndirectOffsetOnAxis(ap=idx_cur[:, s, j:j + 1], axis=0)
                        nc.gpsimd.indirect_dma_start(u_buf[:, s, j, :], None, u_exp[0], at).then_inc(u_in[s][j], 16)
                        nc.gpsimd.indirect_dma_start(v_buf[:, s, j, :], None, v_exp[0], at).then_inc(v_in[s][j], 16)

                pool.wait_ge(sem("y2_zero"), 1)
                group(0, 0, True)
                group(0, 1, True)
                with pool.Fori(1, TRIPS // 2) as i:
                    group(i, 0, False)
                    group(i, 1, False)

            @block.scalar
            def _(act):
                with act.Fori(0, TRIPS) as g:
                    act.wait_ge(dots_done, g * PI + (PI + 1))
                    act.wait_ge(coef_done, g + 1)
                    nc.scalar.activation(acts[:, :], dots[:, :], ACT.Gelu_apprx_tanh).then_inc(acts_done, 1)
                act.wait_ge(v_used, 1 + TRIPS * PI)
                for t in range(NT):
                    scratch = u_buf[:, 0, t, :]
                    nc.scalar.activation(scratch, y2[:, t, :], ACT.Square, accum_out=zsq[:, t:t + 1]).then_inc(z_sq, 1)
                act.wait_ge(z_sq, NT)
                nc.scalar.activation(zroot[:, :], zsq[:, :], ACT.Sqrt, bias=eps[:, :], scale=1.0 / D).then_inc(z_sq, 1)

            @block.vector
            def _(dve):
                link = Link(dve, sem("dve_link5"))
                for started in (coef_done, dots_done, v_used):
                    dve.sem_inc(started, 1)
                for t in range(NT):
                    with dve.Fori(t * GROUPS_T // 2, (t + 1) * GROUPS_T // 2) as i:
                        for s in range(2):
                            for j in range(PI):
                                dve.wait_ge(u_in[s][j], i * 16 + 16)
                                dve.wait_ge(dots_done, i * (2 * PI) + (s * PI + j + 1))
                                nc.vector.scalar_tensor_tensor(out=product[:, :], in0=u_buf[:, s, j, :], scalar=1.0, in1=h2[:, t, :],
                                                               op0=ALU.mult, op1=ALU.mult, accum_out=dots[:, j:j + 1]).then_inc(dots_done, 1)
                            dve.wait_ge(acts_done, i * 2 + (s + 1))
                            nc.vector.tensor_tensor(coef[:, :], acts[:, :], gw_flat[:, bass.ds(i * (2 * PI) + s * PI, PI)], ALU.mult).then_inc(coef_done, 1)
                            dve.wait_ge(coef_done, i * 2 + (s + 2))
                            for j in range(PI):
                                dve.wait_ge(v_in[s][j], i * 16 + 16)
                                dve.wait_ge(v_used, i * (2 * PI) + (s * PI + j + 1))
                                nc.vector.scalar_tensor_tensor(out=y2[:, t, :], in0=v_buf[:, s, j, :], scalar=coef[:, j:j + 1], in1=y2[:, t, :],
                                                               op0=ALU.mult, op1=ALU.add).then_inc(v_used, 1)
                dve.wait_ge(z_sq, NT + 1)
                link(nc.vector.reciprocal(zrstd[:, :], zroot[:, :]))
                for t in range(NT):
                    link(nc.vector.scalar_tensor_tensor(out=y2[:, t, :], in0=y2[:, t, :], scalar=zrstd[:, t:t + 1], in1=gates[:, 1, :], op0=ALU.mult, op1=ALU.mult))
                    nc.vector.tensor_tensor(x_sb[:, t, :], x_sb[:, t, :], y2[:, t, :], ALU.add).then_inc(z_out, 1)

            @block.sync
            def _(sp):
                for t in range(NT):
                    sp.wait_ge(z_out, t + 1)
                    sp.dma_start(out[0, t * P:(t + 1) * P, :], x_sb[:, t, :]).then_inc(out_done, 16)
                sp.wait_ge(out_done, NT * 16)


_INS = ['x', 'c', 'ctx', 'c_ctx', 'w_mod', 'b_mod', 'g_pre1', 'g_post1', 'g_pre2', 'g_post2', 'w_in', 'g_q', 'g_kv', 'w_uq', 'w_ukv',
        'g_sgu', 'w_s', 'b_s', 'w_pa', 'w_pb', 'w_o', 'w_pq', 'k1', 'k2', 'u_exp', 'v_exp']


def rope_tables():
    quarter = ROPE // 4
    freqs = np.float32(10000.0) ** (-np.arange(quarter, dtype=np.float32) / np.float32(quarter))
    t = np.arange(SEQ)
    ang = [pos.astype(np.float32)[None, :] * freqs[:, None] for pos in (t // GRID_W, t % GRID_W)]
    cos = np.concatenate([np.cos(a) for a in ang for _ in range(2)])
    sin = np.concatenate([s * np.sin(a) for a in ang for s in (-1, 1)])
    return (np.ascontiguousarray(np.tile(z, (2, 1)).astype(np.float32)) for z in (cos, sin))


def kernel(**inputs):
    import concourse.bacc as bacc
    from concourse.bass_utils import run_bass_kernel_spmd

    nc = bacc.Bacc("TRN2", target_bir_lowering=False, num_devices=1)
    cos, sin = rope_tables()
    arrays, args = {}, []
    for name, a in [(n, inputs[n]) for n in _INS] + [("rope_cos", cos), ("rope_sin", sin)]:
        a = np.ascontiguousarray(a)
        arrays[f"in_{name}"] = a
        args.append(nc.dram_tensor(f"in_{name}", a.shape, mybir.dt.from_np(a.dtype), kind="ExternalInput").ap())
    args.append(nc.dram_tensor("out_0", (1, SEQ, D), F32, kind="ExternalOutput").ap())
    layer(nc, *args)
    r = run_bass_kernel_spmd(nc, [arrays], core_ids=[0])
    return r.results[0]["out_0"]
```

```python
from contextlib import ExitStack, contextmanager

import numpy as np

import concourse.bass as bass
from concourse import mybir

F32 = mybir.dt.float32
F32R = mybir.dt.float32r
BF16 = mybir.dt.bfloat16
U32 = mybir.dt.uint32
I32 = mybir.dt.int32
ACT = mybir.ActivationFunctionType
ALU = mybir.AluOpType
AX = mybir.AxisListType

P = 128
D = 1024
KD = D // P
SEQ = 512
CTX = 256
NT = SEQ // P
NC = CTX // P
KEYS = SEQ + CTX
NKT = KEYS // P
GRID_W = 64
EPS = 1e-6
GROUPS = 8
HEADS = 8
NOPE, ROPE, VD = 128, 64, 128
Q_RANK, KV_RANK = 256, 128
SCALE = (NOPE + ROPE) ** -0.5
OFF_U, OFF_V = 0, 1024
OFF_Q = 2048
OFF_GA = OFF_Q + Q_RANK + KV_RANK + ROPE
OFF_GB = OFF_GA + D
LATENT = Q_RANK + KV_RANK + ROPE
PH = 8
NK = 128
TOP = 16
SLOTS = PH * TOP
CH = 512
RING = 4
TOK = 4
STAGE = 32
PAIRS = 4
EXP_AT = 13
HOTS = 4
HALF = NK // 2
CHOICE = 47000
PARTS = ((0, 0), (0, 1), (1, 0))


class Link:

    def __init__(self, eng, sem):
        self.eng, self.sem, self.n, self.base = eng, sem, 0, 0

    def __call__(self, ins, turn=None):
        ins.then_inc(self.sem, 1)
        self.n += 1
        self.eng.wait_ge(self.sem, self.base + self.n)
        if turn is not None:
            self.eng.sem_inc(turn, 1)

    @contextmanager
    def loop(self, trips, per):
        start = self.base + self.n
        with self.eng.Fori(0, trips) as i:
            self.base, self.n = i * per + start, 0
            yield i
            assert self.n == per, (self.n, per)
        self.base, self.n = start + trips * per, 0


def col(i, n=1):
    return bass.ds(i, n)


def layer(nc, x, c, ctx_in, c_ctx, w_mod, b_mod, g_pre1, g_post1, g_pre2, g_post2, w_in, g_q, g_kv, w_uq, w_ukv,
          g_sgu, w_s, b_s, w_pa, w_pb, w_o, w_pq, k1, k2, u_exp, v_exp, rope_cos, rope_sin, out):
    w_mod_k = w_mod[0].rearrange("(k p) n -> p k n", p=P)
    w_in_k = w_in[0].rearrange("(k p) n -> p k n", p=P)
    w_pa_k, w_pb_k, w_o_k, w_pq_k = (w[0].rearrange("(k p) n -> p k n", p=P) for w in (w_pa, w_pb, w_o, w_pq))
    chunks = [(w_mod_k, s * CH, CH) for s in range(4)]
    chunks += [(w_in_k, OFF_Q, LATENT)]
    chunks += [(w_in_k, OFF_V + s * CH, CH) for s in range(2)]
    chunks += [(w_in_k, OFF_U + s * CH, CH) for s in range(2)]
    FRONT = len(chunks)
    chunks += [(w_mod_k, s * CH, CH) for s in (6, 7, 8, 9, 4, 5, 10, 11)]
    MODS = len(chunks)

    with ExitStack() as top:
        sems = {}

        def sem(name):
            if name not in sems:
                sems[name] = top.enter_context(nc.semaphore(name))
            return sems[name]

        placed = {}

        def sb(name, shape, dtype=F32, scope=top):
            placed[name] = -(-nc.sbuf_base // 32) * 32
            return scope.enter_context(nc.sbuf_tensor(name, shape, dtype))

        def over(name, base, shape, at=0):
            return nc.alloc_sbuf_tensor_at(name, shape, F32R, offset=placed[base] + at)

        x_sb = sb("x_sb", [P, NT, D])
        w_ring = sb("w_ring", [P, RING, KD, CH])
        ident = sb("ident", [P, P])
        cols = sb("cols", [P, 96])
        silu_c = sb("silu_c", [P, 2, KD])
        eps = sb("eps", [P, 1])
        gates = sb("gates", [P, 2, D])
        rstd2 = sb("rstd2", [P, NT])
        mod2 = sb("mod2", [P, 2, KD])
        PS = top.enter_context(nc.psum_tensor("PS", [P, 8, CH], F32))

        w_load = [sem(f"w_load{r}") for r in range(RING)]
        w_used = sem("w_used")

        def load(sp, n):
            src, at, width = chunks[n]
            sp.dma_start(w_ring[:, n % RING, :, 0:width], src[:, :, at:at + width]).then_inc(w_load[n % RING], 16)

        def load_chunks(sp, first, last):
            for n in range(first, last):
                if n >= RING:
                    sp.wait_ge(w_used, n - RING + 1)
                load(sp, n)

        def chunk(pe, n):
            pe.wait_ge(w_load[n % RING], 16 * (n // RING + 1))
            return w_ring[:, n % RING]

        m_raw = w_ring[:, 0:2].rearrange("p r k n -> p (r k n)").rearrange("p (r j k n) -> p r j k n", r=2, j=4, k=KD)
        m_in = [sem(f"m_in{r}") for r in range(2)]
        pq_in = [sem(f"pq_in{s}") for s in range(4)]
        PQ_SLOT = (0, 2, 1, 3)

        def load_merge(sp, n):
            for j, (src, at) in enumerate(((w_in_k, OFF_GA), (w_in_k, OFF_GB), (w_pa_k, 0), (w_pb_k, 0))):
                sp.dma_start(m_raw[:, n % 2, j, :, :], src[:, :, at + n * P:at + (n + 1) * P]).then_inc(m_in[n % 2], 16)

        C_BMOD, C_C, C_PRE1, C_PRE2, C_GQ, C_GKV, C_END = 0, 48, 64, 72, 80, 82, 83

        late = top.enter_context(ExitStack())
        hT = sb("hT", [P, KD, SEQ], scope=late)
        o_aT = sb("o_aT", [P, KD, SEQ], scope=late)
        cqT = sb("cqT", [P, 2, SEQ], scope=late)
        ckvT = sb("ckvT", [P, KEYS], scope=late)
        krT = sb("krT", [P, KEYS], scope=late)

        with ExitStack() as here:
            def tmp(name, shape, dtype=F32):
                return sb(name, shape, dtype, scope=here)

            rows = tmp("rows", [C_END, P])
            ctx_sb = tmp("ctx_sb", [P, NC, D])
            xn = tmp("xn", [P, NT, D])
            junk = gates[:, 0, :]
            gs_rep = gates[:, 1, :]
            hcT = tmp("hcT", [P, KD, CTX])
            ssq = tmp("ssq", [P, NT + NC])
            root = tmp("root", [P, NT + NC])
            rstd = tmp("rstd", [P, NT + NC])
            lsq = tmp("lsq", [P, 2, NT + NC])
            lroot = tmp("lroot", [P, 2, NT + NC])
            lrstd = tmp("lrstd", [P, 2, NT + NC])
            vsq = tmp("vsq", [P, NT])
            vroot = tmp("vroot", [P, NT])
            vrstd = tmp("vrstd", [P, NT])
            mod_raw = tmp("mod_raw", [P, 16, 2])
            mod1 = tmp("mod1", [P, 16, 2])
            a1 = tmp("a1", [P, KD, 2])
            zq = tmp("zq", [P, NT + NC, Q_RANK + KV_RANK])
            krw = tmp("krw", [P, KD, 2, P])
            kr_raw = tmp("kr_raw", [P, 2, SEQ])
            ws_sb = tmp("ws_sb", [P, GROUPS, P])
            wsT = tmp("wsT", [P, GROUPS, P])
            bs_rep = tmp("bs_rep", [P, GROUPS, P])
            cos_sb = tmp("cos_sb1", [P, SEQ])
            sin_sb = tmp("sin_sb1", [P, SEQ])
            cn = ctx_sb
            mod_row = hcT[0:2, :, :].rearrange("p k n -> p (k n)")

            J_MOD = 1 + 4 + 1
            J_KR = J_MOD + KD + KD // 2 + NT + NC
            J_SGU = J_KR + 3 + 2 * NT + 2 + 4 + KD

            vec_in, x_in, ctx_in_s, tab_in = sem("vec_in"), sem("x_in"), sem("ctx_in"), sem("tab_in")
            full, read = sem("bank_full"), sem("bank_read")
            FULL, READ = full, read
            block = here.enter_context(nc.Block())

            @block.sync
            def _(sp):
                sp.wait_ge(vec_in, 7 * 16)
                load_chunks(sp, 0, 1)
                sp.dma_start(x_sb[:, :, :], x[0].rearrange("(t p) d -> p t d", p=P)).then_inc(x_in, 16)
                load_chunks(sp, 1, 2)
                sp.dma_start(ctx_sb[:, :, :], ctx_in[0].rearrange("(t p) d -> p t d", p=P)).then_inc(ctx_in_s, 16)
                load_chunks(sp, 2, 5)
                sp.dma_start(ws_sb[:, :, :], w_s[0].rearrange("g p q -> p g q")).then_inc(tab_in, 16)
                sp.dma_start(bs_rep[:, :, :], b_s[0].partition_broadcast(P)).then_inc(tab_in, 16)
                sp.dma_start(gs_rep[:, :], g_sgu[0].partition_broadcast(P)).then_inc(tab_in, 16)
                sp.dma_start(cos_sb[:, :], rope_cos).then_inc(tab_in, 16)
                sp.dma_start(sin_sb[:, :], rope_sin).then_inc(tab_in, 16)
                load_chunks(sp, 5, FRONT + RING)

            @block.gpsimd
            def _(pool):
                nc.gpsimd.memset(ident[:, :], 0.0).then_inc(sem("ident_zero"), 1)
                nc.gpsimd.memset(eps[:, :], EPS).then_inc(sem("eps_set"), 1)
                pool.wait_ge(sem("ident_zero"), 1)
                nc.gpsimd.affine_select(out=ident[:, :], in_=ident[:, :], compare_op=ALU.not_equal, fill=1.0, base=0,
                                        pattern=[[-1, P]], channel_multiplier=1).then_inc(sem("ident_set"), 1)
                pool.wait_ge(w_load[4 % RING], 32)
                kr = w_ring[:, 4 % RING, :, Q_RANK + KV_RANK:LATENT]
                for twin in range(2):
                    o = twin * ROPE
                    nc.gpsimd.tensor_copy(krw[:, :, 0, o:o + ROPE], kr).then_inc(sem("krw_set"), 1)
                    for half in range(2):
                        for part in range(2):
                            a, b = o + 32 * half + 16 * part, 32 * half + 16 * (1 - part)
                            nc.gpsimd.tensor_copy(krw[:, :, 1, a:a + 16], kr[:, :, b:b + 16]).then_inc(sem("krw_set"), 1)

            @block.scalar
            def _(act):
                for r0, src in ((C_BMOD, b_mod[0]), (C_C, c[0]), (C_C + 8, c_ctx), (C_PRE1, g_pre1[0]), (C_PRE2, g_pre2[0]),
                                (C_GQ, g_q[0]), (C_GKV, g_kv[0])):
                    v = src.rearrange("(r p) -> r p", p=P)
                    act.dma_start(rows[r0:r0 + v.shape[0], :], v).then_inc(vec_in, 16)
                link = Link(act, sem("act_link1"))
                job = 0

                def take(fn):
                    nonlocal job
                    act.wait_ge(full, job + 1)
                    fn(PS[:, job % 8]).then_inc(read, 1)
                    job += 1

                take(lambda b: nc.scalar.copy(cols[:, 0:C_END], b[:, 0:C_END]))
                act.wait_ge(read, 1)
                nc.scalar.activation(silu_c[:, :, :], cols[:, C_C:C_C + 16].rearrange("p (v k) -> p v k", v=2),
                                     ACT.Silu).then_inc(sem("silu_done"), 1)
                act.wait_ge(x_in, 16)
                for t in range(NT):
                    link(nc.scalar.activation(junk[:, :], x_sb[:, t, :], ACT.Square, accum_out=ssq[:, t:t + 1]))
                act.wait_ge(ctx_in_s, 16)
                for t in range(NC):
                    link(nc.scalar.activation(junk[:, :], ctx_sb[:, t, :], ACT.Square, accum_out=ssq[:, NT + t:NT + t + 1]))
                act.wait_ge(sem("eps_set"), 1)
                nc.scalar.activation(root[:, :], ssq[:, :], ACT.Sqrt, bias=eps[:, :], scale=1.0 / D).then_inc(sem("root_x"), 1)
                for n in range(4):
                    take(lambda b: nc.scalar.copy(mod_row[:, n * CH:(n + 1) * CH], b[0:2, :]))
                take(lambda b: nc.scalar.copy(mod_raw[:, :, :], b[:, 0:32].rearrange("p (m v) -> p m v", v=2)))
                act.wait_ge(sem("mod1_done"), 2)
                for k in range(KD):
                    take(lambda b: nc.scalar.activation(hT[:, k, :], b, ACT.Identity, bias=mod1[:, k, 0:1], scale=a1[:, k, 0:1]))
                for k in range(0, KD, 2):
                    act.wait_ge(full, job + 1)
                    nc.scalar.activation(hcT[:, k, :], PS[:, job % 8, 0:CTX], ACT.Identity, bias=mod1[:, k, 1:2], scale=a1[:, k, 1:2])
                    take(lambda b: nc.scalar.activation(hcT[:, k + 1, :], b[:, CTX:2 * CTX], ACT.Identity,
                                                        bias=mod1[:, k + 1, 1:2], scale=a1[:, k + 1, 1:2]))
                for t in range(NT):
                    take(lambda b: nc.scalar.copy(zq[:, t, :], b[:, 0:Q_RANK + KV_RANK]))
                for t in range(NT, NT + NC):
                    take(lambda b: nc.scalar.copy(zq[:, t, Q_RANK:], b[:, 0:KV_RANK]))
                act.wait_ge(read, job)
                for t in range(NT):
                    link(nc.scalar.activation(junk[:, 0:Q_RANK], zq[:, t, 0:Q_RANK], ACT.Square, accum_out=lsq[:, 0, t:t + 1]))
                for t in range(NT + NC):
                    link(nc.scalar.activation(junk[:, 0:KV_RANK], zq[:, t, Q_RANK:], ACT.Square, accum_out=lsq[:, 1, t:t + 1]))
                nc.scalar.activation(lroot[:, 0, 0:NT], lsq[:, 0, 0:NT], ACT.Sqrt, bias=eps[:, :], scale=1.0 / Q_RANK).then_inc(sem("root_l"), 1)
                nc.scalar.activation(lroot[:, 1, :], lsq[:, 1, :], ACT.Sqrt, bias=eps[:, :], scale=1.0 / KV_RANK).then_inc(sem("root_l"), 1)
                take(lambda b: nc.scalar.copy(kr_raw[:, 0, :], b))
                take(lambda b: nc.scalar.copy(kr_raw[:, 1, :], b))
                take(lambda b: nc.scalar.copy(krT[:, SEQ:KEYS], b[:, 0:CTX]))
                for s in range(2):
                    for t in range(NT):
                        take(lambda b: nc.scalar.activation(xn[:, t, s * CH:(s + 1) * CH], b, ACT.Gelu_apprx_tanh))
                act.wait_ge(read, job)
                for t in range(NT):
                    link(nc.scalar.activation(junk[:, :], xn[:, t, :], ACT.Square, accum_out=vsq[:, t:t + 1]))
                nc.scalar.activation(vroot[:, :], vsq[:, :], ACT.Sqrt, bias=eps[:, :], scale=1.0 / D).then_inc(sem("root_v"), 1)
                for h in range(2):
                    take(lambda b: nc.scalar.copy(wsT[:, 4 * h:4 * h + 4, :], b.rearrange("p (g q) -> p g q", g=4)))
                for k in range(2):
                    take(lambda b: nc.scalar.mul(cqT[:, k, :], b, cols[:, C_GQ + k:C_GQ + k + 1]))
                take(lambda b: nc.scalar.mul(ckvT[:, 0:SEQ], b, cols[:, C_GKV:C_GKV + 1]))
                take(lambda b: nc.scalar.mul(ckvT[:, SEQ:KEYS], b[:, 0:CTX], cols[:, C_GKV:C_GKV + 1]))
                for k in range(KD):
                    take(lambda b: nc.scalar.activation(o_aT[:, k, :], b, ACT.Gelu_apprx_tanh))

            @block.vector
            def _(dve):
                link = Link(dve, sem("dve_link1"))
                dve.wait_ge(sem("root_x"), 1)
                link(nc.vector.reciprocal(rstd[:, :], root[:, :]))
                for t in range(NT):
                    nc.vector.tensor_scalar(xn[:, t, :], x_sb[:, t, :], rstd[:, t:t + 1], None, ALU.mult).then_inc(sem("xn_done"), 1)
                for t in range(NC):
                    nc.vector.tensor_scalar(cn[:, t, :], ctx_sb[:, t, :], rstd[:, NT + t:NT + t + 1], None, ALU.mult).then_inc(sem("xn_done"), 1)
                dve.wait_ge(read, J_MOD)
                bias = cols[:, 0:16].unsqueeze(2).to_broadcast([P, 16, 2])
                gain = cols[:, C_PRE1:C_PRE1 + KD].unsqueeze(2).to_broadcast([P, KD, 2])
                nc.vector.tensor_tensor(mod1[:, :, :], mod_raw[:, :, :], bias, ALU.add).then_inc(sem("mod1_done"), 1)
                dve.wait_ge(sem("mod1_done"), 1)
                nc.vector.scalar_tensor_tensor(out=a1[:, :, :], in0=mod1[:, KD:2 * KD, :], scalar=1.0, in1=gain,
                                               op0=ALU.add, op1=ALU.mult).then_inc(sem("mod1_done"), 1)
                dve.wait_ge(sem("root_l"), 2)
                link(nc.vector.reciprocal(lrstd[:, 0, 0:NT], lroot[:, 0, 0:NT]))
                link(nc.vector.reciprocal(lrstd[:, 1, :], lroot[:, 1, :]))
                for t in range(NT + NC):
                    if t < NT:
                        nc.vector.tensor_scalar(zq[:, t, 0:Q_RANK], zq[:, t, 0:Q_RANK], lrstd[:, 0, t:t + 1], None, ALU.mult).then_inc(sem("zn_done"), 1)
                    nc.vector.tensor_scalar(zq[:, t, Q_RANK:], zq[:, t, Q_RANK:], lrstd[:, 1, t:t + 1], None, ALU.mult).then_inc(sem("zn_done"), 1)
                dve.wait_ge(tab_in, 80)
                dve.wait_ge(read, J_KR + 2)
                link(nc.vector.tensor_tensor(kr_raw[:, 0, :], kr_raw[:, 0, :], cos_sb[:, :], ALU.mult))
                link(nc.vector.tensor_tensor(kr_raw[:, 1, :], kr_raw[:, 1, :], sin_sb[:, :], ALU.mult))
                link(nc.vector.tensor_tensor(krT[:, 0:SEQ], kr_raw[:, 0, :], kr_raw[:, 1, :], ALU.add))
                dve.wait_ge(sem("root_v"), 1)
                link(nc.vector.reciprocal(vrstd[:, :], vroot[:, :]))
                for t in range(NT):
                    nc.vector.scalar_tensor_tensor(out=xn[:, t, :], in0=xn[:, t, :], scalar=vrstd[:, t:t + 1], in1=gs_rep,
                                                   op0=ALU.mult, op1=ALU.mult).then_inc(sem("v_done"), 1)
                for g in range(GROUPS):
                    dve.wait_ge(full, J_SGU + g + 1)
                    dve.wait_ge(read, J_SGU)
                    sv = PS[:, (J_SGU + g) % 8].rearrange("p (n q) -> p n q", n=NT)
                    sv_b = junk[:, (g % 2) * CH:(g % 2 + 1) * CH].rearrange("p (n q) -> p n q", n=NT)
                    link(nc.vector.tensor_tensor(sv_b, sv, bs_rep[:, g, :].unsqueeze(1).to_broadcast([P, NT, P]), ALU.add))
                    nc.vector.tensor_tensor(o_aT[:, g, :], o_aT[:, g, :], junk[:, (g % 2) * CH:(g % 2 + 1) * CH], ALU.mult).then_inc(sem("sgu_done"), 1)

            @block.tensor
            def _(pe):
                job = 0

                def bank(n_free=1):
                    if job >= 8:
                        pe.wait_ge(read, job - 7)
                    return PS[:, job % 8]

                pe.wait_ge(sem("ident_set"), 1)
                pe.wait_ge(vec_in, 7 * 16)
                nc.tensor.transpose(bank()[:, 0:C_END], rows[:, :], ident[0:C_END, 0:C_END]).then_inc(full, 1)
                job += 1
                pe.wait_ge(sem("silu_done"), 1)
                for n in range(4):
                    w = chunk(pe, n)
                    for k in range(KD):
                        last = nc.tensor.matmul(PS[0:2, job % 8, :], silu_c[:, :, k], w[:, k, :], start=k == 0, stop=k == KD - 1)
                        if n and k == 0:
                            last.then_inc(w_used, 1)
                    last.then_inc(full, 1)
                    job += 1
                pe.wait_ge(read, 1 + 4)
                for m in range(16):
                    last = nc.tensor.transpose(PS[:, job % 8, 2 * m:2 * m + 2], mod_row[:, m * P:(m + 1) * P], ident[0:2, 0:2])
                last.then_inc(full, 1)
                job += 1
                pe.wait_ge(sem("xn_done"), NT)
                for k in range(KD):
                    b = bank()
                    for t in range(NT):
                        last = nc.tensor.transpose(b[:, t * P:(t + 1) * P], xn[:, t, k * P:(k + 1) * P], ident[:, :])
                        if k == 0 and t == 0:
                            last.then_inc(w_used, 1)
                    last.then_inc(full, 1)
                    job += 1
                pe.wait_ge(sem("xn_done"), NT + NC)
                for k in range(0, KD, 2):
                    b = bank()
                    for i in range(2):
                        for t in range(NC):
                            last = nc.tensor.transpose(b[:, i * CTX + t * P:i * CTX + (t + 1) * P], cn[:, t, (k + i) * P:(k + i + 1) * P], ident[:, :])
                    last.then_inc(full, 1)
                    job += 1
                w = chunk(pe, 4)
                pe.wait_ge(read, J_MOD + KD)
                for t in range(NT):
                    b = bank()
                    for k in range(KD):
                        last = nc.tensor.matmul(b[:, 0:Q_RANK + KV_RANK], hT[:, k, t * P:(t + 1) * P], w[:, k, 0:Q_RANK + KV_RANK], start=k == 0, stop=k == KD - 1)
                    last.then_inc(full, 1)
                    job += 1
                pe.wait_ge(read, J_MOD + KD + KD // 2)
                for t in range(NC):
                    b = bank()
                    for k in range(KD):
                        last = nc.tensor.matmul(b[:, 0:KV_RANK], hcT[:, k, t * P:(t + 1) * P], w[:, k, Q_RANK:Q_RANK + KV_RANK], start=k == 0, stop=k == KD - 1)
                    last.then_inc(full, 1)
                    job += 1
                pe.wait_ge(sem("krw_set"), 10)
                assert job == J_KR
                for kind, src, width in ((0, hT, SEQ), (1, hT, SEQ), (0, hcT, CTX)):
                    b = bank()
                    for k in range(KD):
                        last = nc.tensor.matmul(b[:, 0:width], krw[:, k, kind, :], src[:, k, :], start=k == 0, stop=k == KD - 1)
                    last.then_inc(full, 1)
                    job += 1
                for s in range(2):
                    w = chunk(pe, 5 + s)
                    for t in range(NT):
                        b = bank()
                        for k in range(KD):
                            last = nc.tensor.matmul(b, hT[:, k, t * P:(t + 1) * P], w[:, k, :], start=k == 0, stop=k == KD - 1)
                            if t == 0 and s == 0 and k == 0:
                                last.then_inc(w_used, 1)
                            if t == 0 and s == 1 and k == 0:
                                last.then_inc(w_used, 1)
                        last.then_inc(full, 1)
                        job += 1
                pe.wait_ge(tab_in, 80)
                for h in range(2):
                    b = bank()
                    for g in range(4):
                        last = nc.tensor.transpose(b[:, g * P:(g + 1) * P], ws_sb[:, 4 * h + g, :], ident[:, :])
                        if h == 0 and g == 0:
                            last.then_inc(w_used, 1)
                    last.then_inc(full, 1)
                    job += 1
                pe.wait_ge(sem("zn_done"), 2 * NT + NC)
                for k in range(2):
                    b = bank()
                    for t in range(NT):
                        last = nc.tensor.transpose(b[:, t * P:(t + 1) * P], zq[:, t, k * P:(k + 1) * P], ident[:, :])
                    last.then_inc(full, 1)
                    job += 1
                for t0, n in ((0, NT), (NT, NC)):
                    b = bank()
                    for t in range(n):
                        last = nc.tensor.transpose(b[:, t * P:(t + 1) * P], zq[:, t0 + t, Q_RANK:], ident[:, :])
                    last.then_inc(full, 1)
                    job += 1
                for s in range(2):
                    w = chunk(pe, 7 + s)
                    for m in range(4):
                        b = bank()
                        for k in range(KD):
                            last = nc.tensor.matmul(b, w[:, k, m * P:(m + 1) * P], hT[:, k, :], start=k == 0, stop=k == KD - 1)
                            if s == 1 and m == 0 and k == 0:
                                last.then_inc(w_used, 1)
                        last.then_inc(full, 1)
                        job += 1
                assert job == J_SGU
                pe.wait_ge(sem("v_done"), NT)
                for g in range(GROUPS):
                    b = bank()
                    for t in range(NT):
                        last = nc.tensor.matmul(b[:, t * P:(t + 1) * P], xn[:, t, g * P:(g + 1) * P], wsT[:, g, :], start=True, stop=True)
                        if g == 0 and t == 0:
                            last.then_inc(w_used, 1)
                    last.then_inc(full, 1)
                    job += 1

        oT = sb("oT", [P, HEADS, SEQ], scope=late)
        with ExitStack() as here:
            def tmp(name, shape, dtype=F32):
                return sb(name, shape, dtype, scope=here)

            wq = tmp("wq", [P, 2, 2 * (NOPE + ROPE)])
            wkv = tmp("wkv", [P, 2, NOPE + VD])
            wqr = tmp("wqr", [P, 2, 2, P])
            cos_sb = tmp("cos_sb", [P, SEQ])
            sin_sb = tmp("sin_sb", [P, SEQ])
            rot = tmp("rot", [P, 2, SEQ])
            qnT = tmp("qnT", [P, 2, SEQ])
            qrT = tmp("qrT", [P, SEQ])
            knT = tmp("knT", [P, 2, KEYS])
            v_sb = tmp("v_sb", [P, NKT, 2, VD])
            probs = tmp("probs", [P, 2, KEYS])
            pT = tmp("pT", [P, NKT, SEQ])
            top_s = tmp("top_s", [P, 2, 1])
            neg_s = tmp("neg_s", [P, 2, 1])
            den = tmp("den", [P, 2, 1])
            rden = tmp("rden", [P, 2, 1])
            silu_rep = v_sb[:, 0:4, :, :].rearrange("p a b c -> p (a b c)").rearrange("p (k n) -> p k n", k=KD)
            bmod_rep = pT[:, 0:4, :].rearrange("p a n -> p (a n)").rearrange("p (g n) -> p g n", g=2)
            rep_in, pair_in, wqr_set = sem("rep_in"), sem("pair_in"), sem("wqr_set")
            proj_full, proj_read, rope_full, rope_done = sem("proj_full"), sem("proj_read"), sem("rope_full"), sem("rope_done")
            scores_full, max_done, exp_done, probs_done = sem("scores_full"), sem("max_done"), sem("exp_done"), sem("probs_done")
            pt_full, pt_copied, o_full, o_copied = sem("pt_full"), sem("pt_copied"), sem("o_full"), sem("o_copied")
            row_full, row_read, mod_full, mod_read = sem("row_full"), sem("row_read"), sem("mod_full"), sem("mod_read")
            mod_row = [r.rearrange("p a n -> p (a n)")[0:1, 0:D] for r in (probs, pT[:, 4:6, :])]
            HPAIRS, PER = HEADS // 2, 2 * NT
            PROJ = 7
            block = here.enter_context(nc.Block())

            @block.sync
            def _(sp):
                sp.dma_start(cos_sb[:, :], rope_cos).then_inc(rep_in, 16)
                sp.dma_start(sin_sb[:, :], rope_sin).then_inc(rep_in, 16)
                for g, (seg, gain) in enumerate(((2, g_post1), (5, g_post2))):
                    sp.dma_start(gates[:, g, :], gain[0].partition_broadcast(P)).then_inc(rep_in, 16)
                    sp.dma_start(bmod_rep[:, g, :], b_mod[0][seg * D:(seg + 1) * D].partition_broadcast(P)).then_inc(rep_in, 16)

                def load_pair(h):
                    width = 2 * (NOPE + ROPE)
                    sp.dma_start(wq[:, :, :], w_uq[0].rearrange("(k p) n -> p k n", p=P)[:, :, bass.ds(h * width, width)]).then_inc(pair_in, 16)
                    width = 2 * (NOPE + VD)
                    sp.dma_start(wkv[:, :, :].rearrange("p h n -> p (h n)"), w_ukv[0][:, bass.ds(h * width, width)]).then_inc(pair_in, 16)

                load_pair(0)
                load_chunks(sp, FRONT + RING, MODS)
                sp.wait_ge(mod_full, 5)
                load_merge(sp, 0)
                load_merge(sp, 1)
                with sp.Fori(1, HPAIRS) as h:
                    sp.wait_ge(proj_full, h * PROJ)
                    load_pair(h)

            @block.tensor
            def _(pe):
                pe.sem_inc(pt_full, 1)
                pe.sem_inc(o_full, 1)
                pe.sem_inc(rope_full, 1)
                for n in range(4):
                    w = chunk(pe, FRONT + n)
                    for k in range(KD):
                        last = nc.tensor.matmul(PS[0:1, n, :], silu_c[:, 0, k:k + 1], w[:, k, :], start=k == 0, stop=k == KD - 1)
                        if n and k == 0:
                            last.then_inc(w_used, 1)
                    last.then_inc(row_full, 1)
                pe.wait_ge(row_read, 4)
                for m in range(16):
                    last = nc.tensor.transpose(PS[:, 4, m:m + 1], mod_row[m // 8][:, m % 8 * P:(m % 8 + 1) * P], ident[0:1, 0:1])
                last.then_inc(mod_full, 1)
                pe.wait_ge(sem("rep_set"), 1)
                for s in range(4):
                    w = chunk(pe, FRONT + 4 + s)
                    for k in range(KD):
                        last = nc.tensor.matmul(PS[:, (5 + s) % 8, :], silu_rep[:, k, :], w[:, k, :], start=k == 0, stop=k == KD - 1)
                        if k == 0:
                            last.then_inc(w_used, 1)
                    last.then_inc(mod_full, 1)
                pe.wait_ge(mod_read, 5)
                with pe.Fori(0, HPAIRS) as h:
                    pe.wait_ge(pair_in, h * 32 + 32)
                    pe.wait_ge(exp_done, h * PER + 1)
                    pe.wait_ge(pt_copied, h * PER + 1)
                    pe.wait_ge(o_copied, h * 2 + 1)
                    for i in range(2):
                        for k in range(2):
                            last = nc.tensor.matmul(PS[:, i, :], wq[:, k, i * (NOPE + ROPE):i * (NOPE + ROPE) + NOPE], cqT[:, k, :], start=k == 0, stop=k == 1)
                        last.then_inc(proj_full, 1)
                    pe.wait_ge(wqr_set, h * 6 + 6)
                    for kind in range(2):
                        for k in range(2):
                            last = nc.tensor.matmul(PS[:, 2 + kind, :], wqr[:, k, kind, :], cqT[:, k, :], start=k == 0, stop=k == 1)
                        last.then_inc(rope_full, 1)
                    for i in range(2):
                        nc.tensor.matmul(PS[:, 4 + 2 * i, :], wkv[:, i, 0:NOPE], ckvT[:, 0:SEQ], start=True, stop=True)
                        nc.tensor.matmul(PS[:, 5 + 2 * i, 0:CTX], wkv[:, i, 0:NOPE], ckvT[:, SEQ:KEYS], start=True, stop=True).then_inc(proj_full, 1)
                    for b in range(3):
                        if b < 2:
                            pe.wait_ge(proj_read, h * PROJ + (b + 1))
                        else:
                            pe.wait_ge(rope_done, h + 1)
                        for t in range(2):
                            last = nc.tensor.matmul(PS[:, b, t * 2 * VD:(t + 1) * 2 * VD], ckvT[:, (2 * b + t) * P:(2 * b + t + 1) * P],
                                                    wkv[:, :, NOPE:NOPE + VD], start=True, stop=True)
                        last.then_inc(proj_full, 1)

                    def scores(n):
                        i, t, b = n // NT, n % NT, 2 * (n % 2)
                        r = slice(i * ROPE, (i + 1) * ROPE)
                        for bb, k0, k1 in ((b, 0, SEQ), (b + 1, SEQ, KEYS)):
                            nc.tensor.matmul(PS[:, bb, 0:k1 - k0], qnT[:, i, t * P:(t + 1) * P], knT[:, i, k0:k1], start=True, stop=False)
                            last = nc.tensor.matmul(PS[:, bb, 0:k1 - k0], qrT[r, t * P:(t + 1) * P], krT[r, k0:k1], start=False, stop=True)
                        last.then_inc(scores_full, 1)

                    pe.wait_ge(proj_read, h * PROJ + PROJ)
                    scores(0)
                    for n in range(PER):
                        if n + 1 < PER:
                            pe.wait_ge(exp_done, h * PER + (n + 1))
                            scores(n + 1)
                        pe.wait_ge(probs_done, h * PER + (n + 1))
                        pe.wait_ge(pt_copied, h * PER + (n + 1))
                        for kt in range(NKT):
                            last = nc.tensor.transpose(PS[:, 4 + kt // 4, kt % 4 * P:(kt % 4 + 1) * P], probs[:, n % 2, kt * P:(kt + 1) * P], ident[:, :])
                        last.then_inc(pt_full, 1)
                        if n % NT == NT - 1:
                            i = n // NT
                            pe.wait_ge(pt_copied, h * PER + (n + 2))
                            pe.wait_ge(o_copied, h * 2 + (i + 1))
                            for kt in range(NKT):
                                last = nc.tensor.matmul(PS[:, 6, :], v_sb[:, kt, i, :], pT[:, kt, :], start=kt == 0, stop=kt == NKT - 1)
                            last.then_inc(o_full, 1)

            @block.scalar
            def _(act):
                act.sem_inc(exp_done, 1)
                act.sem_inc(pt_copied, 1)
                for n in range(4):
                    act.wait_ge(row_full, n + 1)
                    nc.scalar.copy(mod_row[n // 2][:, n % 2 * CH:(n % 2 + 1) * CH], PS[0:1, n, :]).then_inc(row_read, 1)
                with act.Fori(0, HPAIRS) as h:
                    act.wait_ge(pair_in, h * 32 + 32)
                    act.wait_ge(rope_full, h * 2 + 1)
                    for i in range(2):
                        src = wq[:, :, i * (NOPE + ROPE) + NOPE:(i + 1) * (NOPE + ROPE)]
                        nc.scalar.copy(wqr[:, :, 0, i * ROPE:(i + 1) * ROPE], src).then_inc(wqr_set, 1)
                        for part in range(2):
                            dst_v = wqr[:, :, 1, i * ROPE:(i + 1) * ROPE].rearrange("p k (h x q) -> p k h x q", h=2, x=2)[:, :, :, part, :]
                            src_v = src.rearrange("p k (h x q) -> p k h x q", h=2, x=2)[:, :, :, 1 - part, :]
                            nc.scalar.copy(dst_v, src_v).then_inc(wqr_set, 1)
                    job = 0
                    for dst, src in ((qnT[:, 0, :], PS[:, 0, :]), (qnT[:, 1, :], PS[:, 1, :]),
                                     (knT[:, 0, :], PS[:, 4:6, :].rearrange("p b n -> p (b n)")[:, 0:KEYS]),
                                     (knT[:, 1, :], PS[:, 6:8, :].rearrange("p b n -> p (b n)")[:, 0:KEYS]),
                                     *((v_sb[:, 2 * b:2 * b + 2, :, :].rearrange("p t i v -> p (t i v)"), PS[:, b, :]) for b in range(3))):
                        act.wait_ge(proj_full, h * PROJ + (job + 1))
                        nc.scalar.copy(dst, src).then_inc(proj_read, 1)
                        job += 1

                    def exps(n):
                        act.wait_ge(max_done, h * PER + (n + 1))
                        if n:
                            act.wait_ge(pt_full, h * PER + n)
                        s = PS[:, 2 * (n % 2):2 * (n % 2) + 2, :].rearrange("p b n -> p (b n)")[:, 0:KEYS]
                        nc.scalar.activation(probs[:, n % 2, :], s, ACT.Exp, bias=neg_s[:, n % 2, :], scale=SCALE,
                                             accum_out=den[:, n % 2, :]).then_inc(exp_done, 1)

                    exps(0)
                    for n in range(PER):
                        if n + 1 < PER:
                            exps(n + 1)
                        act.wait_ge(pt_full, h * PER + (n + 2))
                        if n % NT == 0:
                            act.wait_ge(o_full, h * 2 + (n // NT + 1))
                        src = PS[:, 4:6, :].rearrange("p b n -> p (b n)")[:, 0:KEYS].rearrange("p (k n) -> p k n", k=NKT)
                        nc.scalar.copy(pT[:, :, n % NT * P:(n % NT + 1) * P], src).then_inc(pt_copied, 1)

            @block.vector
            def _(dve):
                link = Link(dve, sem("dve_link2"))
                dve.sem_inc(o_copied, 1)
                nc.vector.tensor_copy(silu_rep, silu_c[:, 0, :].unsqueeze(2).to_broadcast([P, KD, P])).then_inc(sem("rep_set"), 1)
                dve.wait_ge(mod_full, 1)
                link(nc.vector.tensor_tensor(mod2[:, :, :].rearrange("p a k -> p (a k)"), PS[:, 4, 0:16], cols[:, 3 * KD:5 * KD], ALU.add))
                nc.vector.scalar_tensor_tensor(out=mod2[:, 1, :], in0=mod2[:, 1, :], scalar=1.0, in1=cols[:, C_PRE2:C_PRE2 + KD],
                                               op0=ALU.add, op1=ALU.mult).then_inc(mod_read, 1)
                dve.wait_ge(rep_in, 6 * 16)
                for s in range(4):
                    dve.wait_ge(mod_full, 2 + s)
                    g, part = s // 2, slice(s % 2 * CH, (s % 2 + 1) * CH)
                    link(nc.vector.tensor_tensor(bmod_rep[:, g, part], PS[:, (5 + s) % 8, :], bmod_rep[:, g, part], ALU.add))
                    nc.vector.tensor_tensor(gates[:, g, part], bmod_rep[:, g, part], gates[:, g, part], ALU.mult).then_inc(mod_read, 1)
                LINKS = 2 + 2 * PER
                with link.loop(HPAIRS, LINKS) as h:
                    for kind, table in ((0, cos_sb), (1, sin_sb)):
                        dve.wait_ge(rope_full, h * 2 + (kind + 2))
                        link(nc.vector.tensor_tensor(rot[:, kind, :], PS[:, 2 + kind, :], table[:, :], ALU.mult))
                    nc.vector.tensor_tensor(qrT[:, :], rot[:, 0, :], rot[:, 1, :], ALU.add).then_inc(rope_done, 1)
                    for n in range(PER):
                        b = n % 2
                        dve.wait_ge(scores_full, h * PER + (n + 1))
                        s = PS[:, 2 * b:2 * b + 2, :].rearrange("p b n -> p (b n)")[:, 0:KEYS]
                        link(nc.vector.reduce_max(top_s[:, b, :], s, AX.X))
                        nc.vector.tensor_scalar(neg_s[:, b, :], top_s[:, b, :], -SCALE, None, ALU.mult).then_inc(max_done, 1)
                        dve.wait_ge(exp_done, h * PER + (n + 2))
                        link(nc.vector.reciprocal(rden[:, b, :], den[:, b, :]))
                        link_free = nc.vector.tensor_scalar(probs[:, b, :], probs[:, b, :], rden[:, b, :], None, ALU.mult)
                        link_free.then_inc(probs_done, 1)
                        if n == NT or n == PER - 1:
                            i = 0 if n == NT else 1
                            dve.wait_ge(o_full, h * 2 + (i + 2))
                            link_o = nc.vector.tensor_copy(oT[:, col(h * 2 + i), :].rearrange("p a n -> p (a n)"), PS[:, 6, :])
                            link_o.then_inc(o_copied, 1)

        full3 = sem("merge_full")
        with ExitStack() as here:
            def tmp(name, shape, dtype=F32):
                return sb(name, shape, dtype, scope=here)

            src_hi = [tmp(f"{n}_hi", [P, KD, SEQ], F32R) for n in ("hT", "o_aT", "oT")]
            src = [[hi, over(f"{n}_lo", n, [P, KD, SEQ])] for hi, n in zip(src_hi, ("hT", "o_aT", "oT"))]
            SLOT = KD * CH * 4
            piece = over("piece", "w_ring", [P, 4, 2, KD, P], 2 * SLOT)
            wo = [over("wo_hi", "w_ring", [P, 2, KD, CH], 2 * SLOT), over("wo_lo", "w_ring", [P, 2, KD, CH])]
            mT = x_sb[:, :, :].rearrange("p t d -> p (t d)").rearrange("p (k n) -> p k n", k=KD)
            m = src[0]
            sig = tmp("sig", [P, 2, 2, SEQ])
            prod = tmp("prod", [P, 2, SEQ])
            ysq = tmp("ysq", [P, 2, NT])
            yroot = tmp("yroot", [P, 2, NT])
            yrstd = tmp("yrstd", [P, 1, NT])
            src_high, src_low, piece_high, piece_low = sem("src_high"), sem("src_low"), sem("piece_high"), sem("piece_low")
            wo_in, wo_high, wo_low, m_high, m_low = [sem(f"wo_in{r}") for r in range(2)], sem("wo_high"), sem("wo_low"), sem("m_high"), sem("m_low")
            sig_done, prod_done, m_done, y_half, y_full, y_read = sem("sig_done"), sem("prod_done"), sem("m_done"), sem("y_half"), sem("y_full"), sem("y_read")
            ysq_done, root3, x1_done, x_again = sem("ysq_done"), sem("root3"), sem("x1_done"), sem("x_again")
            block = here.enter_context(nc.Block())

            @block.sync
            def _(sp):
                for n in range(2, 8):
                    sp.wait_ge(piece_low, 4 * (n - 1))
                    load_merge(sp, n)
                for h in range(2):
                    sp.wait_ge(piece_low, 4 * (7 + h))
                    sp.dma_start(w_ring[:, h], w_o_k[:, :, h * CH:(h + 1) * CH]).then_inc(wo_in[h], 16)
                sp.wait_ge(m_low, KD)
                sp.dma_start(x_sb[:, :, :], x[0].rearrange("(t p) d -> p t d", p=P)).then_inc(x_again, 16)
                for s in range(4):
                    if s % 2 == 0:
                        sp.wait_ge(y_full if s else y_half, NT)
                    sp.dma_start(w_ring[:, PQ_SLOT[s]], w_pq_k[:, :, s * CH:(s + 1) * CH]).then_inc(pq_in[s], 16)

            @block.tensor
            def _(pe):
                for n in range(8):
                    b = n % 2 * 4
                    if n >= 2:
                        pe.wait_ge(sig_done, 2 * (n - 1))
                        pe.wait_ge(prod_done, 2 * (n - 1))
                    for j, i in enumerate((0, 0, 1, 2)):
                        pe.wait_ge(piece_high, 4 * n + j + 1)
                        pe.wait_ge(piece_low, 4 * n + j + 1)
                        for k in range(KD):
                            if n == 0:
                                pe.wait_ge(src_low, i * KD + k + 1)
                            for a, c_ in PARTS:
                                last = nc.tensor.matmul(PS[:, b + j, :], piece[:, j, a, k, :], src[i][c_][:, k, :],
                                                        start=k == 0 and (a, c_) == PARTS[0], stop=k == KD - 1 and (a, c_) == PARTS[-1])
                        last.then_inc(full3, 1)
                for h in range(2):
                    pe.wait_ge(wo_high, h + 1)
                    pe.wait_ge(wo_low, h + 1)
                    for t in range(NT):
                        for k in range(KD):
                            if h == 0 and t == 0:
                                pe.wait_ge(m_low, k + 1)
                            for a, c_ in PARTS:
                                last = nc.tensor.matmul(PS[:, 2 * t + h, :], m[a][:, k, t * P:(t + 1) * P], wo[c_][:, h, k, :],
                                                        start=k == 0 and (a, c_) == PARTS[0], stop=k == KD - 1 and (a, c_) == PARTS[-1])
                        last.then_inc(y_full if h else y_half, 1)

            @block.scalar
            def _(act):
                def high(g):
                    n, j = g // 4, g % 4
                    act.wait_ge(m_in[n % 2], 64 * (n // 2 + 1))
                    if n:
                        act.wait_ge(full3, g - 3)
                    nc.scalar.copy(piece[:, j, 0, :, :], m_raw[:, n % 2, j, :, :]).then_inc(piece_high, 1)

                for j in range(4):
                    high(j)
                    if j != 1:
                        i = max(j - 1, 0)
                        for k in range(KD):
                            nc.scalar.copy(src_hi[i][:, k, :], (hT, o_aT, oT)[i][:, k, :]).then_inc(src_high, 1)
                for n in range(8):
                    for j in range(4):
                        if n < 7:
                            high(4 * (n + 1) + j)
                        if j < 2:
                            act.wait_ge(full3, 4 * n + j + 1)
                            if n >= 2:
                                act.wait_ge(prod_done, 2 * (n - 2) + j + 1)
                            nc.scalar.activation(sig[:, n % 2, j, :], PS[:, n % 2 * 4 + j, :], ACT.Sigmoid).then_inc(sig_done, 1)

                def wo_hi(h):
                    act.wait_ge(wo_in[h], 16)
                    act.wait_ge(full3, 30 + 2 * h)
                    nc.scalar.copy(wo[0][:, h, :, :], w_ring[:, h]).then_inc(wo_high, 1)

                wo_hi(0)
                for n in range(8):
                    act.wait_ge(m_done, n + 1)
                    nc.scalar.copy(m[0][:, n, :], mT[:, n, :]).then_inc(m_high, 1)
                wo_hi(1)
                for t in range(NT):
                    for kind in range(2):
                        act.wait_ge(x1_done if kind else y_full, t + 1)
                        vec = x_sb[:, t, :] if kind else PS[:, 2 * t:2 * t + 2, :].rearrange("p b n -> p (b n)")
                        scratch = sig[:, kind, :, :].rearrange("p a n -> p (a n)")
                        nc.scalar.activation(scratch, vec, ACT.Square, accum_out=ysq[:, kind, t:t + 1]).then_inc(ysq_done, 1)
                        act.wait_ge(ysq_done, 2 * t + kind + 1)
                        nc.scalar.activation(yroot[:, kind, t:t + 1], ysq[:, kind, t:t + 1], ACT.Sqrt, bias=eps[:, :], scale=1.0 / D).then_inc(root3, 1)

            @block.vector
            def _(dve):
                link = Link(dve, sem("dve_link3"))

                def low(g):
                    n, j = g // 4, g % 4
                    dve.wait_ge(piece_high, g + 1)
                    nc.vector.tensor_tensor(piece[:, j, 1, :, :], m_raw[:, n % 2, j, :, :], piece[:, j, 0, :, :].bitcast(F32), ALU.subtract).then_inc(piece_low, 1)

                def m_lo(n):
                    dve.wait_ge(m_high, n + 1)
                    nc.vector.tensor_tensor(m[1][:, n, :], mT[:, n, :], m[0][:, n, :].bitcast(F32), ALU.subtract).then_inc(m_low, 1)

                def wo_lo(h):
                    dve.wait_ge(wo_high, h + 1)
                    nc.vector.tensor_tensor(wo[1][:, h, :, :], w_ring[:, h], wo[0][:, h, :, :].bitcast(F32), ALU.subtract).then_inc(wo_low, 1)

                for j in range(4):
                    low(j)
                    if j != 1:
                        i = max(j - 1, 0)
                        for k in range(KD):
                            dve.wait_ge(src_high, i * KD + k + 1)
                            nc.vector.tensor_tensor(src[i][1][:, k, :], (hT, o_aT, oT)[i][:, k, :], src_hi[i][:, k, :].bitcast(F32), ALU.subtract).then_inc(src_low, 1)
                for n in range(8):
                    if n == 7:
                        wo_lo(0)
                        for k in range(7):
                            m_lo(k)
                    for j in range(4):
                        if n < 7:
                            low(4 * (n + 1) + j)
                        if j >= 2:
                            dve.wait_ge(full3, 4 * n + j + 1)
                            dve.wait_ge(sig_done, 2 * n + j - 1)
                            if n:
                                dve.wait_ge(m_done, n)
                            nc.vector.tensor_tensor(prod[:, j - 2, :], sig[:, n % 2, j - 2, :], PS[:, n % 2 * 4 + j, :], ALU.mult).then_inc(prod_done, 1)
                    dve.wait_ge(prod_done, 2 * n + 2)
                    nc.vector.tensor_tensor(mT[:, n, :], prod[:, 0, :], prod[:, 1, :], ALU.add).then_inc(m_done, 1)
                m_lo(7)
                wo_lo(1)
                dve.wait_ge(m_done, 8)
                dve.wait_ge(x_again, 16)
                for t in range(NT):
                    y = PS[:, 2 * t:2 * t + 2, :].rearrange("p b n -> p (b n)")
                    scaled = prod[:, :, :].rearrange("p b n -> p (b n)")
                    dve.wait_ge(root3, 2 * t + 1)
                    link(nc.vector.reciprocal(yrstd[:, 0, t:t + 1], yroot[:, 0, t:t + 1]))
                    if t:
                        dve.wait_ge(x1_done, t)
                    nc.vector.scalar_tensor_tensor(out=scaled, in0=y, scalar=yrstd[:, 0, t:t + 1], in1=gates[:, 0, :], op0=ALU.mult, op1=ALU.mult).then_inc(y_read, 1)
                    dve.wait_ge(y_read, t + 1)
                    nc.vector.tensor_tensor(x_sb[:, t, :], x_sb[:, t, :], scaled, ALU.add).then_inc(x1_done, 1)
                    dve.wait_ge(root3, 2 * t + 2)
                    link(nc.vector.reciprocal(rstd2[:, t:t + 1], yroot[:, 1, t:t + 1]))
        late.close()

        act_dram = nc.dram_tensor("act_dram", (P, NK, SEQ), F32).ap()
        wgt_dram = nc.dram_tensor("wgt_dram", (P, SEQ // STAGE, NK, STAGE), F32).ap()
        hidden = top.enter_context(ExitStack())
        h2 = [sb(f"h2_{n}", [P, KD, SEQ], F32R, scope=hidden) for n in ("hi", "lo")]
        s_all = w_ring[:, 0:2].rearrange("p r k n -> p (r k n)").rearrange("p (t h k) -> p t h k", t=NT, h=2 * PH)
        u_raw = w_ring[:, 2:4].rearrange("p r k n -> p (r k n)").rearrange("p (r a d) -> p r a d", r=PAIRS, a=2)
        u_in = [sem(f"u_in{r}") for r in range(PAIRS)]
        u_v = u_exp[0].rearrange("(p b) d -> p b d", p=P)

        v_v = v_exp[0].rearrange("(p b) d -> p b d", p=P)
        v_raw = w_ring[:, 2:4].rearrange("p r k n -> p (r k n)").rearrange("p (r a d) -> p r a d", r=2, a=4)
        v_in = [sem(f"v_in{r}") for r in range(2)]

        def load_v(sp, n, r):
            sp.dma_start(v_raw[:, r, :, :], v_v[:, bass.ds(n * 4, 4), :]).then_inc(v_in[r], 16)

        def load_u(sp, pair, q):
            sp.dma_start(u_raw[:, q, :, :], u_v[:, bass.ds(pair * 2, 2), :]).then_inc(u_in[q], 16)

        with ExitStack() as here:
            def tmp(name, shape, dtype=F32):
                return sb(name, shape, dtype, scope=here)

            qT = tmp("qT", [P, 2 * PH, SEQ])
            w_hl = [tmp(f"w_{n}", [P, 4, KD, P], F32R) for n in ("hi", "lo")]
            k_sb = tmp("k_sb", [P, 2, P])
            kT = tmp("kT", [P, 2, NK])
            h2_f = tmp("h2_f", [P, 2, SEQ])
            xn2 = qT[:, 0:8, :].rearrange("p k n -> p (k n)").rearrange("p (t d) -> p t d", t=NT)
            k_in, kt_full, kt_read, xn2_done = sem("k_in"), sem("kt_full"), sem("kt_read"), sem("xn2_done")
            h2_full, h2_hi, h2_lo = sem("h2_full"), sem("h2_hi"), sem("h2_lo")
            whi_done, wlo_done, wsplit_used = sem("whi_done"), sem("wlo_done"), sem("wsplit_used")
            q_full, q_read, key_full, key_read = sem("q_full"), sem("q_read"), sem("key_full"), sem("key_read")
            block = here.enter_context(nc.Block())

            @block.sync
            def _(sp):
                sp.dma_start(k_sb[:, 0, :], k1[0]).then_inc(k_in, 16)
                sp.dma_start(k_sb[:, 1, :], k2[0]).then_inc(k_in, 16)
                sp.wait_ge(wlo_done, 2 * PH)
                for q in range(PAIRS):
                    load_u(sp, q, q)

            @block.tensor
            def _(pe):
                pe.wait_ge(xn2_done, NT)
                for k in range(KD):
                    for t in range(NT):
                        last = nc.tensor.transpose(PS[:, k, t * P:(t + 1) * P], xn2[:, t, k * P:(k + 1) * P], ident[:, :])
                    last.then_inc(h2_full, 1)
                for n in range(2 * PH):
                    pe.wait_ge(whi_done, n + 1)
                    pe.wait_ge(wlo_done, n + 1)
                    if n >= 8:
                        pe.wait_ge(q_read, n - 7)
                    if n == 8:
                        pe.wait_ge(k_in, 32)
                        for i in range(2):
                            last = nc.tensor.transpose(PS[:, 0, i * P:(i + 1) * P], k_sb[:, i, :], ident[:, :])
                        last.then_inc(kt_full, 1)
                        pe.wait_ge(kt_read, 1)
                    for k in range(KD):
                        if n == 0:
                            pe.wait_ge(h2_lo, k + 1)
                        if n < 8 and k == 0:
                            pe.wait_ge(h2_lo, n + 1)
                        for a, c_ in PARTS:
                            last = nc.tensor.matmul(PS[:, n % 8, :], w_hl[a][:, n % 4, k, :], h2[c_][:, k, :],
                                                    start=k == 0 and (a, c_) == PARTS[0], stop=k == KD - 1 and (a, c_) == PARTS[-1])
                    last.then_inc(q_full, 1)
                pe.wait_ge(q_read, 2 * PH)
                for t in range(NT):
                    if t >= 2:
                        pe.wait_ge(key_read, t - 1)
                    for n in range(2 * PH):
                        last = nc.tensor.matmul(PS[:, t % 2 * 4 + n // 4, n % 4 * NK:(n % 4 + 1) * NK], qT[:, n, t * P:(t + 1) * P], kT[:, n % 2, :], start=True, stop=True)
                    last.then_inc(key_full, 1)

            @block.scalar
            def _(act):

                def w_high(n):
                    c_, m = n // 4, n % 4
                    act.wait_ge(pq_in[c_], 16)
                    nc.scalar.copy(w_hl[0][:, m, :, :], w_ring[:, PQ_SLOT[c_], :, m * P:(m + 1) * P]).then_inc(whi_done, 1)

                w_high(0)
                for k in range(KD):
                    act.wait_ge(h2_full, k + 1)
                    nc.scalar.activation(h2[0][:, k, :], PS[:, k, :], ACT.Identity, bias=mod2[:, 0, k:k + 1], scale=mod2[:, 1, k:k + 1]).then_inc(h2_hi, 1)
                for n in range(1, 4):
                    w_high(n)
                for n in range(2 * PH):
                    if n == 8:
                        act.wait_ge(kt_full, 1)
                        nc.scalar.copy(kT[:, :, :], PS[:, 0, 0:2 * P].rearrange("p (i n) -> p i n", i=2)).then_inc(kt_read, 1)
                    act.wait_ge(q_full, n + 1)
                    nc.scalar.copy(qT[:, n, :], PS[:, n % 8, :]).then_inc(q_read, 1)
                    if n + 4 < 2 * PH:
                        w_high(n + 4)
                act.wait_ge(wlo_done, 16)
                for t in range(NT):
                    act.wait_ge(key_full, t + 1)
                    nc.scalar.copy(s_all[:, t, :, :].rearrange("p h k -> p (h k)"), PS[:, t % 2 * 4:t % 2 * 4 + 4, :].rearrange("p b n -> p (b n)")).then_inc(key_read, 1)

            @block.vector
            def _(dve):
                for t in range(NT):
                    nc.vector.tensor_scalar(xn2[:, t, :], x_sb[:, t, :], rstd2[:, t:t + 1], None, ALU.mult).then_inc(xn2_done, 1)

                def w_low(n):
                    c_, m = n // 4, n % 4
                    dve.wait_ge(whi_done, n + 1)
                    nc.vector.tensor_tensor(w_hl[1][:, m, :, :], w_ring[:, PQ_SLOT[c_], :, m * P:(m + 1) * P], w_hl[0][:, m, :, :].bitcast(F32), ALU.subtract).then_inc(wlo_done, 1)

                w_low(0)
                link = Link(dve, sem("dve_link4"))
                for k in range(KD):
                    dve.wait_ge(h2_hi, k + 1)
                    link(nc.vector.tensor_scalar(h2_f[:, k % 2, :], PS[:, k, :], mod2[:, 1, k:k + 1], mod2[:, 0, k:k + 1], ALU.mult, ALU.add))
                    nc.vector.tensor_tensor(h2[1][:, k, :], h2_f[:, k % 2, :], h2[0][:, k, :].bitcast(F32), ALU.subtract).then_inc(h2_lo, 1)
                for n in range(1, 2 * PH):
                    w_low(n)

        with ExitStack() as here:
            def tmp(name, shape, dtype=F32):
                return sb(name, shape, dtype, scope=here)

            uT = [tmp(f"uT_{n}", [P, 2, KD, P], F32R) for n in ("hi", "lo")]
            a_out = tmp("a_out", [P, 2, 2, SEQ])
            s_cur = tmp("s_cur", [P, 2 * PH, NK])
            s_rest = tmp("s_rest", [P, 2 * PH, NK])
            best = tmp("best", [P, 2 * PH, TOP])
            best_i = tmp("best_i", [P, 2 * PH, TOP], U32)
            best_f = tmp("best_f", [P, 2 * PH, TOP])
            cand = s_cur[:, :, :].rearrange("p h k -> p (h k)").rearrange("p (h c) -> p h c", h=PH)
            cand_rest = s_rest[:, :, :].rearrange("p h k -> p (h k)").rearrange("p (h c) -> p h c", h=PH)
            picks = s_rest[:, :, :].rearrange("p h k -> p (h k)").rearrange("p (s a) -> p s a", a=TOP)
            top_v = tmp("top_v", [P, PH, TOP])
            top_p = tmp("top_p", [P, SLOTS], U32)
            part = tmp("part", [P, 2, SLOTS], U32)
            part_f = tmp("part_f", [P, 2, SLOTS])
            chosen = tmp("chosen", [P, NT, 3, SLOTS])
            expo = tmp("expo", [P, PH, TOP])
            total = tmp("total", [P, PH])
            iota_i = tmp("iota_i", [P, NK], I32)
            iota_f = tmp("iota_f", [P, TOP])
            iota_k = tmp("iota_k", [P, NK])
            slotT = s_cur[:, :, :].rearrange("p h k -> p (h k)").rearrange("p (a t) -> p a t", a=4)
            partT = s_rest[:, :, :].rearrange("p h k -> p (h k)").rearrange("p (a t) -> p a t", a=4).bitcast(F32R)
            hot1 = tmp("hot1", [P, HOTS, TOK, NK], F32R)
            hot2 = tmp("hot2", [P, HOTS, TOK, 2, NK], F32R)
            w_stage = w_ring[:, 0:2].rearrange("p r k n -> p (r k n)").rearrange("p (s b t) -> p s b t", s=2, b=NK)
            ut_full, ut_hi, ut_lo = sem("ut_full"), sem("ut_hi"), sem("ut_lo")
            a_full, a_done, a_stored = sem("a_full"), sem("a_done"), [sem(f"a_stored{r}") for r in range(2)]
            s_cur_set, s_used, soft_in, soft_out, chosen_done = sem("s_cur_set"), sem("s_used"), sem("soft_in"), sem("soft_out"), sem("chosen_done")
            slot_full, slot_read, hot_done = sem("slot_full"), sem("slot_read"), sem("hot_done")
            w_full, w_read, w_stored = sem("wgt_full"), sem("wgt_read"), [sem(f"wgt_stored{r}") for r in range(2)]
            iota_set, turn = sem("iota_set"), sem("turn")
            LOW = -3.0e38
            block = here.enter_context(nc.Block())

            @block.sync
            def _(sp):
                with sp.Fori(0, NK // 2 // PAIRS - 1) as i:
                    for q in range(PAIRS):
                        sp.wait_ge(ut_full, i * (4 * PAIRS) + (4 * q + 4))
                        load_u(sp, i * PAIRS + (PAIRS + q), q)
                for r in range(2):
                    sp.wait_ge(ut_full, 2 * NK - 4 * PAIRS + 8 * (r + 1))
                    load_v(sp, r, r)

            @block.gpsimd
            def _(pool):
                nc.gpsimd.iota(iota_i[:, :], pattern=[[1, NK]], base=0, channel_multiplier=0).then_inc(iota_set, 1)

            CREDIT = HOTS

            @block.tensor
            def _(pe):
                pe.sem_inc(a_full, CREDIT)
                pe.sem_inc(w_full, CREDIT)

                def turn_u(i, q, r, first=False):
                    pe.wait_ge(u_in[q], i * 16 + 16)
                    for half in range(2):
                        if not first:
                            pe.wait_ge(ut_hi, i * (4 * PAIRS) + (4 * q + 2 * r + half - 1))
                            pe.wait_ge(ut_lo, i * (4 * PAIRS) + (4 * q + 2 * r + half - 1))
                        for k in range(4):
                            last = nc.tensor.transpose(PS[:, half, k * P:(k + 1) * P], u_raw[:, q, r, (4 * half + k) * P:(4 * half + k + 1) * P], ident[:, :])
                        last.then_inc(ut_full, 1)

                def activations(i, q, r):
                    pe.wait_ge(ut_hi, i * (4 * PAIRS) + (4 * q + 2 * r + 2))
                    pe.wait_ge(ut_lo, i * (4 * PAIRS) + (4 * q + 2 * r + 2))
                    pe.wait_ge(a_done, i * (2 * PAIRS) + (2 * q + r - 1 + CREDIT))
                    for k in range(KD):
                        for a, c_ in PARTS:
                            last = nc.tensor.matmul(PS[:, 2 + r, :], uT[a][:, r, k, :], h2[c_][:, k, :],
                                                    start=k == 0 and (a, c_) == PARTS[0], stop=k == KD - 1 and (a, c_) == PARTS[-1])
                    last.then_inc(a_full, 1)

                def weights(i, n):
                    pe.wait_ge(hot_done, i * (4 * PAIRS) + (n + 1))
                    pe.wait_ge(w_read, i * (4 * PAIRS) + (n - 1 + CREDIT))
                    for j in range(TOK):
                        for g in range(2):
                            last = nc.tensor.matmul(PS[:, 4 + n % 2, j * NK:(j + 1) * NK], hot1[:, n % HOTS, j, :], hot2[:, n % HOTS, j, g, :], start=g == 0, stop=g == 1)
                    last.then_inc(w_full, 1)

                def pairs(i, dense=None, more=True):
                    for q in range(PAIRS):
                        turn_u(i, q, 1)
                        activations(i, q, 0)
                        if dense is not None:
                            weights(dense, 4 * q)
                            weights(dense, 4 * q + 1)
                        if q < PAIRS - 1:
                            turn_u(i, q + 1, 0)
                        elif more:
                            turn_u(i + 1, 0, 0)
                        activations(i, q, 1)
                        if dense is not None:
                            weights(dense, 4 * q + 2)
                            weights(dense, 4 * q + 3)

                turn_u(0, 0, 0, first=True)
                with pe.Fori(0, HALF // 2 // PAIRS) as i:
                    pairs(i)
                pe.wait_ge(chosen_done, NT)
                for a in range(3):
                    for t in range(NT):
                        last = nc.tensor.transpose(PS[:, 4 + a, t * P:(t + 1) * P], chosen[:, t, a, :], ident[:, :])
                last.then_inc(slot_full, 1)
                pe.wait_ge(slot_read, 1)
                with pe.Fori(HALF // 2 // PAIRS, NK // 2 // PAIRS - 1) as i:
                    pairs(i, dense=i - HALF // 2 // PAIRS)
                pairs(NK // 2 // PAIRS - 1, dense=(NK - HALF) // 2 // PAIRS - 1, more=False)

            @block.scalar
            def _(act):
                act.sem_inc(a_done, CREDIT)
                act.sem_inc(w_read, CREDIT)
                for r in range(2):
                    act.sem_inc(a_stored[r], 16)
                    act.sem_inc(w_stored[r], 16)

                def high(i, j):
                    r = j % 2
                    act.wait_ge(a_full, i * 16 + (j - 1 + CREDIT))
                    for half in range(2):
                        act.wait_ge(ut_full, i * 32 + (2 * j + half + 1))
                        nc.scalar.copy(uT[0][:, r, 4 * half:4 * half + 4, :].rearrange("p k n -> p (k n)"), PS[:, half, :]).then_inc(ut_hi, 1)

                def gelu(i, j):
                    s = j // 2 % 2
                    if j % 2 == 0:
                        act.wait_ge(a_stored[s], i * 64 + 16 * (j // 4) + 16)
                    act.wait_ge(a_full, i * 16 + (j + 1 + CREDIT))
                    nc.scalar.activation(a_out[:, s, j % 2, :], PS[:, 2 + j % 2, :], ACT.Gelu_apprx_tanh).then_inc(a_done, 1)
                    if j % 2:
                        act.wait_ge(a_done, i * 16 + (j + 1 + CREDIT))
                        act.dma_start(act_dram[:, bass.ds(i * 16 + (j - 1), 2), :], a_out[:, s, :, :]).then_inc(a_stored[s], 16)

                def scores_of(t):
                    nc.scalar.copy(s_cur[:, :, :], s_all[:, col(t), :, :].rearrange("p a h k -> p (a h) k")).then_inc(s_cur_set, 1)

                def choice(t, more):
                    for j in range(16):
                        high(t, j + 1)
                        gelu(t, j)
                        if j == EXP_AT:
                            act.wait_ge(soft_in, t + 1)
                            nc.scalar.activation(expo[:, :, :], expo[:, :, :], ACT.Exp).then_inc(soft_out, 1)
                            if more:
                                act.wait_ge(s_used, t + 1)
                                scores_of(t + 1)

                scores_of(0)
                high(0, 0)
                with act.Fori(0, NT - 1) as t:
                    choice(t, True)
                choice(NT - 1, False)

                def dense(i, more):
                    for j in range(16):
                        if j < 15 or more:
                            high(i, j + 1)
                        gelu(i, j)
                        s = j // 4 % 2
                        if j % 4 == 0:
                            act.wait_ge(w_stored[s], (i - NT) * 32 + 16 * (j // 8) + 16)
                        for n in range(2):
                            c0 = (2 * (j % 4) + n) * TOK
                            act.wait_ge(w_full, (i - NT) * 32 + (2 * j + n + 1 + CREDIT))
                            nc.scalar.copy(w_stage[:, s, :, c0:c0 + TOK], PS[:, 4 + n, :].rearrange("p (t b) -> p b t", t=TOK)).then_inc(w_read, 1)
                        if j % 4 == 3:
                            act.wait_ge(w_read, (i - NT) * 32 + (2 * j + 2 + CREDIT))
                            act.dma_start(wgt_dram[:, bass.ds((i - NT) * 4 + j // 4, 1), :, :].rearrange("p a b t -> p (a b t)"),
                                          w_stage[:, s, :, :].rearrange("p b t -> p (b t)")).then_inc(w_stored[s], 16)

                with act.Fori(NT, 2 * NT - 1) as i:
                    dense(i, True)
                dense(2 * NT - 1, False)

            @block.vector
            def _(dve):
                link = Link(dve, sem("dve_link5"))
                dve.wait_ge(iota_set, 1)
                nc.vector.tensor_copy(iota_k[:, :], iota_i[:, :])
                link(nc.vector.tensor_copy(iota_f[:, :], iota_i[:, 0:TOP]))

                def low(i, per, j):
                    r, half = j // 2 % 2, j % 2
                    dve.wait_ge(ut_hi, i * per + (j + 1))
                    part_of = slice(4 * half, 4 * half + 4)
                    nc.vector.tensor_tensor(uT[1][:, r, part_of, :].rearrange("p k n -> p (k n)"), PS[:, half, :],
                                            uT[0][:, r, part_of, :].rearrange("p k n -> p (k n)").bitcast(F32), ALU.subtract).then_inc(ut_lo, 1)

                with link.loop(NT, 20) as t:
                    done = [0, 0]

                    def beside(elements):
                        done[1] += elements + 60
                        while done[0] < 32 and done[1] * 32 >= CHOICE * (done[0] + 1):
                            low(t, 32, done[0])
                            done[0] += 1

                    def top16(values, indices, source, rest, count):
                        width = source.shape[2]
                        for n in range(count):
                            last = nc.vector.max(values(n)[:, 0:8], source[:, n, :])
                            if n < count - 1:
                                beside(width)
                        link(last, turn)
                        for n in range(count):
                            nc.vector.max_index(indices(n)[:, 0:8], values(n)[:, 0:8], source[:, n, :])
                            last = nc.vector.match_replace(rest[:, n, :], values(n)[:, 0:8], source[:, n, :], LOW)
                            if n < count - 1:
                                beside(2 * width + 60)
                        link(last, turn)
                        for n in range(count):
                            last = nc.vector.max(values(n)[:, 8:16], rest[:, n, :])
                            if n < count - 1:
                                beside(width)
                        link(last, turn)
                        for n in range(count):
                            last = nc.vector.max_index(indices(n)[:, 8:16], values(n)[:, 8:16], rest[:, n, :])
                            if n < count - 1:
                                beside(width)
                        link(last, turn)

                    dve.wait_ge(s_cur_set, t + 1)
                    dve.sem_inc(turn, 1)
                    top16(lambda n: best[:, n, :], lambda n: best_i[:, n, :], s_cur, s_rest, 2 * PH)
                    link(nc.vector.tensor_copy(best_f[:, :, :], best_i[:, :, :]))
                    pair = best[:, :, :].rearrange("p (h i) a -> p h i a", i=2)
                    link(nc.vector.tensor_tensor(cand.rearrange("p h (a b) -> p h a b", a=TOP),
                                                 pair[:, :, 0, :].unsqueeze(3).to_broadcast([P, PH, TOP, TOP]),
                                                 pair[:, :, 1, :].unsqueeze(2).to_broadcast([P, PH, TOP, TOP]), ALU.add), turn)
                    beside(2048)
                    dve.sem_inc(turn, 1)
                    top16(lambda n: top_v[:, n, :], lambda n: top_p[:, n * TOP:(n + 1) * TOP], cand, cand_rest, PH)
                    assert done[0] <= 2 * EXP_AT + 3, done
                    nc.vector.tensor_tensor(expo[:, :, :], top_v[:, :, :], top_v[:, :, 0:1].to_broadcast([P, PH, TOP]), ALU.subtract).then_inc(soft_in, 1)
                    nc.vector.tensor_scalar(part[:, 0, :], top_p[:, :], 4, None, ALU.logical_shift_right).then_inc(s_used, 1)
                    link(nc.vector.tensor_scalar(part[:, 1, :], top_p[:, :], 15, None, ALU.bitwise_and))
                    link(nc.vector.tensor_copy(part_f[:, :, :], part[:, :, :]))
                    index = best_f[:, :, :].rearrange("p (h i) a -> p h i a", i=2)
                    for i in range(2):
                        link(nc.vector.tensor_tensor(picks, part_f[:, i, :].unsqueeze(2).to_broadcast([P, SLOTS, TOP]),
                                                     iota_f[:, :].unsqueeze(1).to_broadcast([P, SLOTS, TOP]), ALU.is_equal))
                        beside(2048)
                        p4 = picks.rearrange("p (h k) a -> p h k a", h=PH)
                        link(nc.vector.tensor_tensor(p4, p4, index[:, :, i, :].unsqueeze(2).to_broadcast([P, PH, TOP, TOP]), ALU.mult))
                        beside(2048)
                        link(nc.vector.tensor_reduce(chosen[:, col(t), i, :].rearrange("p a s -> p (a s)"), picks, AX.X, ALU.add))
                        beside(2048)
                    for j in range(done[0], 32):
                        low(t, 32, j)
                    dve.wait_ge(soft_out, t + 1)
                    link(nc.vector.tensor_reduce(total[:, :], expo[:, :, :], AX.X, ALU.add))
                    link(nc.vector.reciprocal(total[:, :], total[:, :]))
                    nc.vector.tensor_tensor(chosen[:, col(t), 2, :].rearrange("p a (h k) -> p (a h) k", h=PH), expo[:, :, :],
                                            total[:, :].unsqueeze(2).to_broadcast([P, PH, TOP]), ALU.mult).then_inc(chosen_done, 1)

                dve.wait_ge(slot_full, 1)
                for a in range(3):
                    last = nc.vector.tensor_copy(slotT[:, a, :], PS[:, 4 + a, :])
                link(last)
                link(nc.vector.tensor_copy(partT[:, 0, :], slotT[:, 2, :]))
                nc.vector.tensor_tensor(partT[:, 1, :], slotT[:, 2, :], partT[:, 0, :].bitcast(F32), ALU.subtract).then_inc(slot_read, 1)
                dve.wait_ge(slot_read, 1)

                with dve.Fori(0, (NK - HALF) // 4) as i:
                    for j in range(8):
                        low(i + 2 * HALF // 8, 8, j)
                        r = j % HOTS
                        dve.wait_ge(w_full, i * 8 + (j + 1 - HOTS + CREDIT))
                        first = slotT[:, 0, bass.ds(i * (8 * TOK) + j * TOK, TOK)]
                        nc.vector.tensor_tensor(hot1[:, r, :, :], iota_k[:, :].unsqueeze(1).to_broadcast([P, TOK, NK]),
                                                first.unsqueeze(2).to_broadcast([P, TOK, NK]), ALU.is_equal)
                        for n in range(TOK):
                            at = bass.ds(i * (8 * TOK) + (j * TOK + n), 1)
                            for g in range(2):
                                last = nc.vector.tensor_scalar(hot2[:, r, n, g, :], iota_k[:, :], slotT[:, 1, at], partT[:, g, at].bitcast(F32), ALU.is_equal, ALU.mult)
                        last.then_inc(hot_done, 1)
        hidden.close()

        with ExitStack() as here:
            def tmp(name, shape, dtype=F32):
                return sb(name, shape, dtype, scope=here)

            a_raw = tmp("a_raw", [P, 2, 4, SEQ])
            w_raw = tmp("w_raw", [P, 2, SEQ // STAGE, 4, STAGE])
            v_hl = [tmp(f"v_{n}", [P, 2, D], F32R) for n in ("hi", "lo")]
            g_hl = [tmp(f"g_{n}", [P, 2, SEQ], F32R) for n in ("hi", "lo")]
            g_f = tmp("g_f", [P, 2, SEQ])
            zsq = tmp("zsq", [P, NT])
            zroot = tmp("zroot", [P, NT])
            zrstd = tmp("zrstd", [P, NT])
            zout = tmp("zout", [P, NT, D])
            aw_in = [sem(f"aw_in{r}") for r in range(2)]
            v_hi, v_lo, g_done, g_hi, g_lo, pv_done = sem("v_hi"), sem("v_lo"), sem("g_done"), sem("g_hi"), sem("g_lo"), sem("pv_done")
            z_sq, z_out, out_done = sem("z_sq"), sem("z_out"), sem("out_done")
            block = here.enter_context(nc.Block())

            @block.sync
            def _(sp):
                def load_aw(n, r):
                    sp.dma_start(a_raw[:, r, :, :], act_dram[:, bass.ds(n * 4, 4), :]).then_inc(aw_in[r], 16)
                    sp.dma_start(w_raw[:, r, :, :, :], wgt_dram[:, :, bass.ds(n * 4, 4), :]).then_inc(aw_in[r], 16)

                for r in range(2):
                    sp.wait_ge(a_stored[r], 16 + 16 * NK // 4)
                    sp.wait_ge(w_stored[r], 16 + 16 * SEQ // STAGE // 2)
                load_aw(0, 0)
                load_aw(1, 1)
                with sp.Fori(1, NK // 8) as i:
                    for r in range(2):
                        sp.wait_ge(v_lo, i * 8 + (4 * r - 4))
                        sp.wait_ge(g_done, i * 8 + (4 * r - 4))
                        load_v(sp, i * 2 + r, r)
                        load_aw(i * 2 + r, r)
                for t in range(NT):
                    sp.wait_ge(z_out, t + 1)
                    sp.dma_start(out[0, t * P:(t + 1) * P, :], x_sb[:, t, :]).then_inc(out_done, 16)
                sp.wait_ge(out_done, NT * 16)

            @block.tensor
            def _(pe):
                pe.sem_inc(pv_done, CREDIT)

                def blocks(i, first=False, last_one=False):
                    for j in range(4):
                        for s in (v_hi, v_lo, g_hi, g_lo):
                            pe.wait_ge(s, i * 4 + (j + 1))
                        for t in range(NT):
                            for half in range(2):
                                for a, c_ in PARTS:
                                    last = nc.tensor.matmul(PS[:, 2 * t + half, :], g_hl[a][:, j % 2, t * P:(t + 1) * P], v_hl[c_][:, j % 2, half * CH:(half + 1) * CH],
                                                            start=first and j == 0 and (a, c_) == PARTS[0],
                                                            stop=last_one and j == 3 and (a, c_) == PARTS[-1], skip_group_check=True)
                        last.then_inc(pv_done, 1)

                blocks(0, first=True)
                with pe.Fori(1, NK // 4 - 1) as i:
                    blocks(i)
                blocks(NK // 4 - 1, last_one=True)

            @block.scalar
            def _(act):
                with act.Fori(0, NK // 8) as i:
                    for j in range(8):
                        if j % 4 == 0:
                            act.wait_ge(v_in[j // 4], i * 16 + 16)
                        act.wait_ge(pv_done, i * 8 + (j - 1 + CREDIT))
                        nc.scalar.copy(v_hl[0][:, j % 2, :], v_raw[:, j // 4, j % 4, :]).then_inc(v_hi, 1)
                        act.wait_ge(g_done, i * 8 + (j + 1))
                        nc.scalar.copy(g_hl[0][:, j % 2, :], g_f[:, j % 2, :]).then_inc(g_hi, 1)
                act.wait_ge(pv_done, NK + CREDIT)
                for t in range(NT):
                    y = PS[:, 2 * t:2 * t + 2, :].rearrange("p b n -> p (b n)")
                    nc.scalar.activation(zout[:, t, :], y, ACT.Square, accum_out=zsq[:, t:t + 1]).then_inc(z_sq, 1)
                act.wait_ge(z_sq, NT)
                nc.scalar.activation(zroot[:, :], zsq[:, :], ACT.Sqrt, bias=eps[:, :], scale=1.0 / D).then_inc(z_sq, 1)

            @block.vector
            def _(dve):
                with dve.Fori(0, NK // 8) as i:
                    for j in range(8):
                        if j % 4 == 0:
                            dve.wait_ge(aw_in[j // 4], i * 32 + 32)
                        nc.vector.tensor_tensor(g_f[:, j % 2, :].rearrange("p (g t) -> p g t", t=STAGE), a_raw[:, j // 4, j % 4, :].rearrange("p (g t) -> p g t", t=STAGE),
                                                w_raw[:, j // 4, :, j % 4, :], ALU.mult).then_inc(g_done, 1)
                        dve.wait_ge(v_hi, i * 8 + (j + 1))
                        nc.vector.tensor_tensor(v_hl[1][:, j % 2, :], v_raw[:, j // 4, j % 4, :], v_hl[0][:, j % 2, :].bitcast(F32), ALU.subtract).then_inc(v_lo, 1)
                        dve.wait_ge(g_hi, i * 8 + (j + 1))
                        nc.vector.tensor_tensor(g_hl[1][:, j % 2, :], g_f[:, j % 2, :], g_hl[0][:, j % 2, :].bitcast(F32), ALU.subtract).then_inc(g_lo, 1)
                link = Link(dve, sem("dve_link6"))
                dve.wait_ge(z_sq, NT + 1)
                link(nc.vector.reciprocal(zrstd[:, :], zroot[:, :]))
                for t in range(NT):
                    y = PS[:, 2 * t:2 * t + 2, :].rearrange("p b n -> p (b n)")
                    link(nc.vector.scalar_tensor_tensor(out=zout[:, t, :], in0=y, scalar=zrstd[:, t:t + 1], in1=gates[:, 1, :], op0=ALU.mult, op1=ALU.mult))
                    nc.vector.tensor_tensor(x_sb[:, t, :], x_sb[:, t, :], zout[:, t, :], ALU.add).then_inc(z_out, 1)


_INS = ['x', 'c', 'ctx', 'c_ctx', 'w_mod', 'b_mod', 'g_pre1', 'g_post1', 'g_pre2', 'g_post2', 'w_in', 'g_q', 'g_kv', 'w_uq', 'w_ukv',
        'g_sgu', 'w_s', 'b_s', 'w_pa', 'w_pb', 'w_o', 'w_pq', 'k1', 'k2', 'u_exp', 'v_exp']


def rope_tables():
    quarter = ROPE // 4
    freqs = np.float32(10000.0) ** (-np.arange(quarter, dtype=np.float32) / np.float32(quarter))
    t = np.arange(SEQ)
    ang = [pos.astype(np.float32)[None, :] * freqs[:, None] for pos in (t // GRID_W, t % GRID_W)]
    cos = np.concatenate([np.cos(a) for a in ang for _ in range(2)])
    sin = np.concatenate([s * np.sin(a) for a in ang for s in (-1, 1)])
    return (np.ascontiguousarray(np.tile(z, (2, 1)).astype(np.float32)) for z in (cos, sin))


def kernel(**inputs):
    import concourse.bacc as bacc
    from concourse.bass_utils import run_bass_kernel_spmd

    nc = bacc.Bacc("TRN2", target_bir_lowering=False, num_devices=1)
    cos, sin = rope_tables()
    arrays, args = {}, []
    for name, a in [(n, inputs[n]) for n in _INS] + [("rope_cos", cos), ("rope_sin", sin)]:
        a = np.ascontiguousarray(a)
        arrays[f"in_{name}"] = a
        args.append(nc.dram_tensor(f"in_{name}", a.shape, mybir.dt.from_np(a.dtype), kind="ExternalInput").ap())
    args.append(nc.dram_tensor("out_0", (1, SEQ, D), F32, kind="ExternalOutput").ap())
    layer(nc, *args)
    r = run_bass_kernel_spmd(nc, [arrays], core_ids=[0])
    return r.results[0]["out_0"]
```

```python
from contextlib import ExitStack, contextmanager

import numpy as np

import concourse.bass as bass
from concourse import mybir

F32 = mybir.dt.float32
F32R = mybir.dt.float32r
U32 = mybir.dt.uint32
I32 = mybir.dt.int32
ACT = mybir.ActivationFunctionType
ALU = mybir.AluOpType
AX = mybir.AxisListType

P = 128
D = 1024
KD = D // P
SEQ = 512
CTX = 256
NT = SEQ // P
NC = CTX // P
KEYS = SEQ + CTX
NKT = KEYS // P
GRID_W = 64
EPS = 1e-6
GROUPS = 8
HEADS = 8
NOPE, ROPE, VD = 128, 64, 128
Q_RANK, KV_RANK = 256, 128
SCALE = (NOPE + ROPE) ** -0.5
OFF_U, OFF_V = 0, 1024
OFF_Q = 2048
OFF_GA = OFF_Q + Q_RANK + KV_RANK + ROPE
OFF_GB = OFF_GA + D
LATENT = Q_RANK + KV_RANK + ROPE
PH = 8
NK = 128
TOP = 16
SLOTS = PH * TOP
CH = 512
RING = 4
TOK = 4
STAGE = 32
PAIRS = 4
EXP_AT = 13
HOTS = 4
HALF = NK // 2
CHOICE = 47000
PARTS = ((0, 0), (0, 1), (1, 0))


class Link:

    def __init__(self, eng, sem):
        self.eng, self.sem, self.n, self.base = eng, sem, 0, 0

    def __call__(self, ins, turn=None):
        ins.then_inc(self.sem, 1)
        self.n += 1
        self.eng.wait_ge(self.sem, self.base + self.n)
        if turn is not None:
            self.eng.sem_inc(turn, 1)

    @contextmanager
    def loop(self, trips, per, first=0):
        start = self.base + self.n
        with self.eng.Fori(first, first + trips) as i:
            self.base, self.n = i * per + (start - first * per), 0
            yield i
            assert self.n == per, (self.n, per)
        self.base, self.n = start + trips * per, 0


def col(i, n=1):
    return bass.ds(i, n)


def layer(nc, x, c, ctx_in, c_ctx, w_mod, b_mod, g_pre1, g_post1, g_pre2, g_post2, w_in, g_q, g_kv, w_uq, w_ukv,
          g_sgu, w_s, b_s, w_pa, w_pb, w_o, w_pq, k1, k2, u_exp, v_exp, rope_cos, rope_sin, out):
    w_mod_k = w_mod[0].rearrange("(k p) n -> p k n", p=P)
    w_in_k = w_in[0].rearrange("(k p) n -> p k n", p=P)
    w_pa_k, w_pb_k, w_o_k, w_pq_k = (w[0].rearrange("(k p) n -> p k n", p=P) for w in (w_pa, w_pb, w_o, w_pq))
    chunks = [(w_mod_k, s * CH, CH) for s in range(4)]
    chunks += [(w_in_k, OFF_Q, LATENT)]
    chunks += [(w_in_k, OFF_V + s * CH, CH) for s in range(2)]
    chunks += [(w_in_k, OFF_U + s * CH, CH) for s in range(2)]
    MOD_PART = (3, 4, 2, 5)

    with ExitStack() as top:
        sems = {}

        def sem(name):
            if name not in sems:
                sems[name] = top.enter_context(nc.semaphore(name))
            return sems[name]

        placed = {}
        SLOT = KD * CH * 4

        def sb(name, shape, dtype=F32, scope=top):
            placed[name] = -(-nc.sbuf_base // 32) * 32
            return scope.enter_context(nc.sbuf_tensor(name, shape, dtype))

        def over(name, base, shape, at=0, dtype=F32R):
            return nc.alloc_sbuf_tensor_at(name, shape, dtype, offset=placed[base] + at)

        x_sb = sb("x_sb", [P, NT, D])
        w_ring = sb("w_ring", [P, RING, KD, CH])
        ident = sb("ident", [P, P])
        cols = sb("cols", [P, 96])
        silu_c = sb("silu_c", [P, 2, KD])
        eps = sb("eps", [P, 1])
        gates = sb("gates", [P, 2, D])
        rstd2 = sb("rstd2", [P, NT])
        mod2 = sb("mod2", [P, 2, KD])
        PS = top.enter_context(nc.psum_tensor("PS", [P, 8, CH], F32))

        w_load = [sem(f"w_load{r}") for r in range(RING)]
        w_used = sem("w_used")
        slot_of = [0, 1, 2, 3, 0, 1, 0, 1, 0]

        def load(sp, n):
            src, at, width = chunks[n]
            sp.dma_start(w_ring[:, slot_of[n], :, 0:width], src[:, :, at:at + width]).then_inc(w_load[slot_of[n]], 16)

        def chunk(eng, n):
            eng.wait_ge(w_load[slot_of[n]], 16 * slot_of[:n + 1].count(slot_of[n]))
            return w_ring[:, slot_of[n]]

        mod_in = [sem(f"mod_in{r}") for r in range(2)]

        def load_mod(sp, h, r):
            at = MOD_PART[h] * D + r * CH
            sp.dma_start(w_ring[:, r], w_mod_k[:, :, at:at + CH]).then_inc(mod_in[r], 16)

        m_raw = w_ring[:, 0:2].rearrange("p r k n -> p (r k n)").rearrange("p (r j k n) -> p r j k n", r=2, j=4, k=KD)
        m_in = [sem(f"m_in{r}") for r in range(2)]
        pq_in = [sem(f"pq_in{s}") for s in range(4)]
        PQ_SLOT = (0, 2, 1, 3)

        def load_merge(sp, n):
            for j, (src, at) in enumerate(((w_in_k, OFF_GA), (w_in_k, OFF_GB), (w_pa_k, 0), (w_pb_k, 0))):
                sp.dma_start(m_raw[:, n % 2, j, :, :], src[:, :, at + n * P:at + (n + 1) * P]).then_inc(m_in[n % 2], 16)

        C_BMOD, C_C, C_PRE1, C_PRE2, C_GQ, C_GKV, C_END = 0, 48, 64, 72, 80, 82, 83

        heads_w = top.enter_context(ExitStack())
        cos_sb, sin_sb, wq, wkv = (heads_w.enter_context(nc.sbuf_tensor(name, shape, F32, side="right")) for name, shape in
                                   (("cos_sb", [P, SEQ]), ("sin_sb", [P, SEQ]), ("wq", [P, 2, 2 * (NOPE + ROPE)]), ("wkv", [P, 2, NOPE + VD])))
        pair_in = sem("pair_in")

        def load_pair(sp, h):
            width = 2 * (NOPE + ROPE)
            sp.dma_start(wq[:, :, :], w_uq[0].rearrange("(k p) n -> p k n", p=P)[:, :, h * width:(h + 1) * width]).then_inc(pair_in, 16)
            width = 2 * (NOPE + VD)
            sp.dma_start(wkv[:, :, :].rearrange("p h n -> p (h n)"), w_ukv[0][:, h * width:(h + 1) * width]).then_inc(pair_in, 16)

        late = top.enter_context(ExitStack())
        hT = sb("hT", [P, KD, SEQ], scope=late)
        o_aT = sb("o_aT", [P, KD, SEQ], scope=late)
        cqT = sb("cqT", [P, 2, SEQ], scope=late)
        ckvT = sb("ckvT", [P, KEYS], scope=late)
        krT = sb("krT", [P, KEYS], scope=late)

        with ExitStack() as here:
            def tmp(name, shape, dtype=F32):
                return sb(name, shape, dtype, scope=here)

            rows = tmp("rows", [C_END, P])
            ctx_sb = tmp("ctx_sb", [P, NC, D])
            hcT = tmp("hcT", [P, KD, CTX])
            xn = tmp("xn", [P, NT, D])
            h_hl = [over("h_hi", "ctx_sb", [P, KD, SEQ]), over("h_lo", "hT", [P, KD, SEQ])]
            v_piece = over("v_piece", "w_ring", [P, 2, 2, KD, 2 * P], 2 * SLOT)
            u_piece = over("u_piece", "w_ring", [P, 4, 2, KD, P], 2 * SLOT)
            junk = gates[:, 0, :]
            gs_rep = gates[:, 1, :]
            ssq = tmp("ssq", [P, NT + NC])
            root = tmp("root", [P, NT + NC])
            rstd = tmp("rstd", [P, NT + NC])
            lsq = tmp("lsq", [P, 2, NT + NC])
            lroot = tmp("lroot", [P, 2, NT + NC])
            lrstd = tmp("lrstd", [P, 2, NT + NC])
            vsq = tmp("vsq", [P, NT])
            vroot = tmp("vroot", [P, NT])
            vrstd = tmp("vrstd", [P, NT])
            mod_raw = tmp("mod_raw", [P, 16, 2])
            mod1 = tmp("mod1", [P, 16, 2])
            a1 = tmp("a1", [P, KD, 2])
            zq = tmp("zq", [P, NT + NC, Q_RANK + KV_RANK])
            krw = tmp("krw", [P, KD, 2, P])
            kr_raw = tmp("kr_raw", [P, 2, SEQ])
            ws_sb = tmp("ws_sb", [P, GROUPS, P])
            wsT = tmp("wsT", [P, GROUPS, P])
            bs_rep = tmp("bs_rep", [P, GROUPS, P])
            cn = ctx_sb
            mod_row = hcT[0:2, :, :].rearrange("p k n -> p (k n)")

            J_MOD = 1 + 4 + 1
            J_KR = J_MOD + KD + KD // 2 + NT + NC
            J_V = J_KR + 3
            J_U = J_V + 2 * NT + 2 + 4
            J_SGU = J_U + KD

            vec_in, x_in, ctx_in_s, tab_in = sem("vec_in"), sem("x_in"), sem("ctx_in"), sem("tab_in")
            full, read = sem("bank_full"), sem("bank_read")
            h_high, h_low, v_high, v_low, v_used, u_high, u_low = (sem(n) for n in ("h_high", "h_low", "v_high", "v_low", "v_used", "u_high", "u_low"))
            block = here.enter_context(nc.Block())

            @block.sync
            def _(sp):
                sp.wait_ge(vec_in, 7 * 16)
                load(sp, 0)
                sp.dma_start(x_sb[:, :, :], x[0].rearrange("(t p) d -> p t d", p=P)).then_inc(x_in, 16)
                load(sp, 1)
                sp.dma_start(ctx_sb[:, :, :], ctx_in[0].rearrange("(t p) d -> p t d", p=P)).then_inc(ctx_in_s, 16)
                load(sp, 2)
                load(sp, 3)
                sp.wait_ge(w_used, 1)
                load(sp, 4)
                sp.dma_start(ws_sb[:, :, :], w_s[0].rearrange("g p q -> p g q")).then_inc(tab_in, 16)
                sp.dma_start(bs_rep[:, :, :], b_s[0].partition_broadcast(P)).then_inc(tab_in, 16)
                sp.dma_start(gs_rep[:, :], g_sgu[0].partition_broadcast(P)).then_inc(tab_in, 16)
                sp.dma_start(cos_sb[:, :], rope_cos).then_inc(tab_in, 16)
                sp.dma_start(sin_sb[:, :], rope_sin).then_inc(tab_in, 16)
                sp.wait_ge(w_used, 2)
                load(sp, 5)
                sp.wait_ge(full, J_KR)
                sp.wait_ge(sem("krw_set"), 10)
                load(sp, 6)
                sp.wait_ge(v_low, 2)
                load(sp, 7)
                sp.wait_ge(v_low, 4)
                load(sp, 8)
                load_pair(sp, 0)
                sp.wait_ge(u_low, 4)
                load_mod(sp, 0, 1)
                sp.wait_ge(u_low, 8)
                load_mod(sp, 0, 0)

            @block.gpsimd
            def _(pool):
                nc.gpsimd.memset(ident[:, :], 0.0).then_inc(sem("ident_zero"), 1)
                nc.gpsimd.memset(eps[:, :], EPS).then_inc(sem("eps_set"), 1)
                pool.wait_ge(sem("ident_zero"), 1)
                nc.gpsimd.affine_select(out=ident[:, :], in_=ident[:, :], compare_op=ALU.not_equal, fill=1.0, base=0,
                                        pattern=[[-1, P]], channel_multiplier=1).then_inc(sem("ident_set"), 1)
                kr = chunk(pool, 4)[:, :, Q_RANK + KV_RANK:LATENT]
                for twin in range(2):
                    o = twin * ROPE
                    nc.gpsimd.tensor_copy(krw[:, :, 0, o:o + ROPE], kr).then_inc(sem("krw_set"), 1)
                    for half in range(2):
                        for part in range(2):
                            a, b = o + 32 * half + 16 * part, 32 * half + 16 * (1 - part)
                            nc.gpsimd.tensor_copy(krw[:, :, 1, a:a + 16], kr[:, :, b:b + 16]).then_inc(sem("krw_set"), 1)
                pool.wait_ge(full, J_SGU)
                for k in range(KD):
                    nc.gpsimd.tensor_tensor(hT[:, k, :], h_hl[0][:, k, :].bitcast(F32), h_hl[1][:, k, :].bitcast(F32), ALU.add).then_inc(sem("h_whole"), 1)

            @block.scalar
            def _(act):
                for r0, src in ((C_BMOD, b_mod[0]), (C_C, c[0]), (C_C + 8, c_ctx), (C_PRE1, g_pre1[0]), (C_PRE2, g_pre2[0]),
                                (C_GQ, g_q[0]), (C_GKV, g_kv[0])):
                    v = src.rearrange("(r p) -> r p", p=P)
                    act.dma_start(rows[r0:r0 + v.shape[0], :], v).then_inc(vec_in, 16)
                link = Link(act, sem("act_link1"))
                job = 0

                def take(fn):
                    nonlocal job
                    act.wait_ge(full, job + 1)
                    fn(PS[:, job % 8]).then_inc(read, 1)
                    job += 1

                take(lambda b: nc.scalar.copy(cols[:, 0:C_END], b[:, 0:C_END]))
                act.wait_ge(read, 1)
                nc.scalar.activation(silu_c[:, :, :], cols[:, C_C:C_C + 16].rearrange("p (v k) -> p v k", v=2),
                                     ACT.Silu).then_inc(sem("silu_done"), 1)
                act.wait_ge(x_in, 16)
                for t in range(NT):
                    link(nc.scalar.activation(junk[:, :], x_sb[:, t, :], ACT.Square, accum_out=ssq[:, t:t + 1]))
                act.wait_ge(ctx_in_s, 16)
                for t in range(NC):
                    link(nc.scalar.activation(junk[:, :], ctx_sb[:, t, :], ACT.Square, accum_out=ssq[:, NT + t:NT + t + 1]))
                act.wait_ge(sem("eps_set"), 1)
                nc.scalar.activation(root[:, :], ssq[:, :], ACT.Sqrt, bias=eps[:, :], scale=1.0 / D).then_inc(sem("root_x"), 1)
                for n in range(4):
                    take(lambda b: nc.scalar.copy(mod_row[:, n * CH:(n + 1) * CH], b[0:2, :]))
                take(lambda b: nc.scalar.copy(mod_raw[:, :, :], b[:, 0:32].rearrange("p (m v) -> p m v", v=2)))
                act.wait_ge(sem("mod1_done"), 2)
                for k in range(KD):
                    take(lambda b: nc.scalar.activation(hT[:, k, :], b, ACT.Identity, bias=mod1[:, k, 0:1], scale=a1[:, k, 0:1]))
                for k in range(0, KD, 2):
                    act.wait_ge(full, job + 1)
                    nc.scalar.activation(hcT[:, k, :], PS[:, job % 8, 0:CTX], ACT.Identity, bias=mod1[:, k, 1:2], scale=a1[:, k, 1:2])
                    take(lambda b: nc.scalar.activation(hcT[:, k + 1, :], b[:, CTX:2 * CTX], ACT.Identity,
                                                        bias=mod1[:, k + 1, 1:2], scale=a1[:, k + 1, 1:2]))
                def v_hi(p):
                    w = chunk(act, 5 + p // 2)
                    if p < 2:
                        act.wait_ge(w_used, 4)
                    elif p == 2:
                        act.wait_ge(v_used, 1)
                    else:
                        act.wait_ge(full, J_V + NT)
                    nc.scalar.copy(v_piece[:, p % 2, 0, :, :], w[:, :, p % 2 * 2 * P:(p % 2 + 1) * 2 * P]).then_inc(v_high, 1)

                def u_hi(m):
                    w = chunk(act, 7 + m // 4)
                    if m < 2:
                        act.wait_ge(v_used, 2)
                    elif m < 4:
                        act.wait_ge(full, J_V + 2 * NT)
                    else:
                        act.wait_ge(full, J_U + m - 3)
                    nc.scalar.copy(u_piece[:, m % 4, 0, :, :], w[:, :, m % 4 * P:(m % 4 + 1) * P]).then_inc(u_high, 1)

                v_hi(0)
                v_hi(1)
                for t in range(NT):
                    take(lambda b: nc.scalar.copy(zq[:, t, :], b[:, 0:Q_RANK + KV_RANK]))
                for t in range(NT, NT + NC):
                    take(lambda b: nc.scalar.copy(zq[:, t, Q_RANK:], b[:, 0:KV_RANK]))
                act.wait_ge(read, job)
                for t in range(NT):
                    link(nc.scalar.activation(junk[:, 0:Q_RANK], zq[:, t, 0:Q_RANK], ACT.Square, accum_out=lsq[:, 0, t:t + 1]))
                for t in range(NT + NC):
                    link(nc.scalar.activation(junk[:, 0:KV_RANK], zq[:, t, Q_RANK:], ACT.Square, accum_out=lsq[:, 1, t:t + 1]))
                nc.scalar.activation(lroot[:, 0, 0:NT], lsq[:, 0, 0:NT], ACT.Sqrt, bias=eps[:, :], scale=1.0 / Q_RANK).then_inc(sem("root_l"), 1)
                nc.scalar.activation(lroot[:, 1, :], lsq[:, 1, :], ACT.Sqrt, bias=eps[:, :], scale=1.0 / KV_RANK).then_inc(sem("root_l"), 1)
                take(lambda b: nc.scalar.copy(kr_raw[:, 0, :], b))
                take(lambda b: nc.scalar.copy(kr_raw[:, 1, :], b))
                take(lambda b: nc.scalar.copy(krT[:, SEQ:KEYS], b[:, 0:CTX]))
                act.wait_ge(full, J_V)
                for k in range(KD):
                    nc.scalar.copy(h_hl[0][:, k, :], hT[:, k, :]).then_inc(h_high, 1)
                for s in range(2):
                    if s == 0:
                        v_hi(2)
                    else:
                        v_hi(3)
                        u_hi(0)
                        u_hi(1)
                    for t in range(NT):
                        take(lambda b: nc.scalar.activation(xn[:, t, s * CH:(s + 1) * CH], b, ACT.Gelu_apprx_tanh))
                u_hi(2)
                u_hi(3)
                act.wait_ge(read, job)
                for t in range(NT):
                    link(nc.scalar.activation(junk[:, :], xn[:, t, :], ACT.Square, accum_out=vsq[:, t:t + 1]))
                nc.scalar.activation(vroot[:, :], vsq[:, :], ACT.Sqrt, bias=eps[:, :], scale=1.0 / D).then_inc(sem("root_v"), 1)
                for h in range(2):
                    take(lambda b: nc.scalar.copy(wsT[:, 4 * h:4 * h + 4, :], b.rearrange("p (g q) -> p g q", g=4)))
                for k in range(2):
                    take(lambda b: nc.scalar.mul(cqT[:, k, :], b, cols[:, C_GQ + k:C_GQ + k + 1]))
                take(lambda b: nc.scalar.mul(ckvT[:, 0:SEQ], b, cols[:, C_GKV:C_GKV + 1]))
                take(lambda b: nc.scalar.mul(ckvT[:, SEQ:KEYS], b[:, 0:CTX], cols[:, C_GKV:C_GKV + 1]))
                for k in range(KD):
                    take(lambda b: nc.scalar.activation(o_aT[:, k, :], b, ACT.Gelu_apprx_tanh))
                    if k < 4:
                        u_hi(4 + k)

            @block.vector
            def _(dve):
                link = Link(dve, sem("dve_link1"))
                dve.wait_ge(sem("root_x"), 1)
                link(nc.vector.reciprocal(rstd[:, :], root[:, :]))
                for t in range(NT):
                    nc.vector.tensor_scalar(xn[:, t, :], x_sb[:, t, :], rstd[:, t:t + 1], None, ALU.mult).then_inc(sem("xn_done"), 1)
                for t in range(NC):
                    nc.vector.tensor_scalar(cn[:, t, :], ctx_sb[:, t, :], rstd[:, NT + t:NT + t + 1], None, ALU.mult).then_inc(sem("xn_done"), 1)
                dve.wait_ge(read, J_MOD)
                bias = cols[:, 0:16].unsqueeze(2).to_broadcast([P, 16, 2])
                gain = cols[:, C_PRE1:C_PRE1 + KD].unsqueeze(2).to_broadcast([P, KD, 2])
                nc.vector.tensor_tensor(mod1[:, :, :], mod_raw[:, :, :], bias, ALU.add).then_inc(sem("mod1_done"), 1)
                dve.wait_ge(sem("mod1_done"), 1)
                nc.vector.scalar_tensor_tensor(out=a1[:, :, :], in0=mod1[:, KD:2 * KD, :], scalar=1.0, in1=gain,
                                               op0=ALU.add, op1=ALU.mult).then_inc(sem("mod1_done"), 1)

                def v_lo(p):
                    dve.wait_ge(v_high, p + 1)
                    w = w_ring[:, slot_of[5 + p // 2], :, p % 2 * 2 * P:(p % 2 + 1) * 2 * P]
                    nc.vector.tensor_tensor(v_piece[:, p % 2, 1, :, :], w, v_piece[:, p % 2, 0, :, :].bitcast(F32), ALU.subtract).then_inc(v_low, 1)

                def u_lo(m):
                    dve.wait_ge(u_high, m + 1)
                    w = w_ring[:, slot_of[7 + m // 4], :, m % 4 * P:(m % 4 + 1) * P]
                    nc.vector.tensor_tensor(u_piece[:, m % 4, 1, :, :], w, u_piece[:, m % 4, 0, :, :].bitcast(F32), ALU.subtract).then_inc(u_low, 1)

                v_lo(0)
                v_lo(1)
                dve.wait_ge(sem("root_l"), 2)
                link(nc.vector.reciprocal(lrstd[:, 0, 0:NT], lroot[:, 0, 0:NT]))
                link(nc.vector.reciprocal(lrstd[:, 1, :], lroot[:, 1, :]))
                for t in range(NT + NC):
                    if t < NT:
                        nc.vector.tensor_scalar(zq[:, t, 0:Q_RANK], zq[:, t, 0:Q_RANK], lrstd[:, 0, t:t + 1], None, ALU.mult).then_inc(sem("zn_done"), 1)
                    nc.vector.tensor_scalar(zq[:, t, Q_RANK:], zq[:, t, Q_RANK:], lrstd[:, 1, t:t + 1], None, ALU.mult).then_inc(sem("zn_done"), 1)
                for k in range(KD):
                    dve.wait_ge(h_high, k + 1)
                    nc.vector.tensor_tensor(h_hl[1][:, k, :], hT[:, k, :], h_hl[0][:, k, :].bitcast(F32), ALU.subtract).then_inc(h_low, 1)
                dve.wait_ge(tab_in, 80)
                dve.wait_ge(read, J_KR + 2)
                link(nc.vector.tensor_tensor(kr_raw[:, 0, :], kr_raw[:, 0, :], cos_sb[:, :], ALU.mult))
                link(nc.vector.tensor_tensor(kr_raw[:, 1, :], kr_raw[:, 1, :], sin_sb[:, :], ALU.mult))
                link(nc.vector.tensor_tensor(krT[:, 0:SEQ], kr_raw[:, 0, :], kr_raw[:, 1, :], ALU.add))
                for p in (2, 3):
                    v_lo(p)
                for m in range(4):
                    u_lo(m)
                dve.wait_ge(sem("root_v"), 1)
                link(nc.vector.reciprocal(vrstd[:, :], vroot[:, :]))
                for t in range(NT):
                    nc.vector.scalar_tensor_tensor(out=xn[:, t, :], in0=xn[:, t, :], scalar=vrstd[:, t:t + 1], in1=gs_rep,
                                                   op0=ALU.mult, op1=ALU.mult).then_inc(sem("v_done"), 1)
                for m in range(4, 8):
                    u_lo(m)
                for g in range(GROUPS):
                    dve.wait_ge(full, J_SGU + g + 1)
                    dve.wait_ge(read, J_SGU)
                    sv = PS[:, (J_SGU + g) % 8].rearrange("p (n q) -> p n q", n=NT)
                    sv_b = junk[:, (g % 2) * CH:(g % 2 + 1) * CH].rearrange("p (n q) -> p n q", n=NT)
                    link(nc.vector.tensor_tensor(sv_b, sv, bs_rep[:, g, :].unsqueeze(1).to_broadcast([P, NT, P]), ALU.add))
                    nc.vector.tensor_tensor(o_aT[:, g, :], o_aT[:, g, :], junk[:, (g % 2) * CH:(g % 2 + 1) * CH], ALU.mult).then_inc(sem("sgu_done"), 1)

            @block.tensor
            def _(pe):
                job = 0

                def bank():
                    if job >= 8:
                        pe.wait_ge(read, job - 7)
                    return PS[:, job % 8]

                pe.wait_ge(sem("ident_set"), 1)
                pe.wait_ge(vec_in, 7 * 16)
                nc.tensor.transpose(bank()[:, 0:C_END], rows[:, :], ident[0:C_END, 0:C_END]).then_inc(full, 1)
                job += 1
                pe.wait_ge(sem("silu_done"), 1)
                for n in range(4):
                    w = chunk(pe, n)
                    for k in range(KD):
                        last = nc.tensor.matmul(PS[0:2, job % 8, :], silu_c[:, :, k], w[:, k, :], start=k == 0, stop=k == KD - 1)
                        if n and k == 0:
                            last.then_inc(w_used, 1)
                    last.then_inc(full, 1)
                    job += 1
                pe.wait_ge(read, 1 + 4)
                for m in range(16):
                    last = nc.tensor.transpose(PS[:, job % 8, 2 * m:2 * m + 2], mod_row[:, m * P:(m + 1) * P], ident[0:2, 0:2])
                last.then_inc(full, 1)
                job += 1
                pe.wait_ge(sem("xn_done"), NT)
                for k in range(KD):
                    b = bank()
                    for t in range(NT):
                        last = nc.tensor.transpose(b[:, t * P:(t + 1) * P], xn[:, t, k * P:(k + 1) * P], ident[:, :])
                        if k == 0 and t == 0:
                            last.then_inc(w_used, 1)
                    last.then_inc(full, 1)
                    job += 1
                pe.wait_ge(sem("xn_done"), NT + NC)
                for k in range(0, KD, 2):
                    b = bank()
                    for i in range(2):
                        for t in range(NC):
                            last = nc.tensor.transpose(b[:, i * CTX + t * P:i * CTX + (t + 1) * P], cn[:, t, (k + i) * P:(k + i + 1) * P], ident[:, :])
                    last.then_inc(full, 1)
                    job += 1
                w = chunk(pe, 4)
                pe.wait_ge(read, J_MOD + KD)
                for t in range(NT):
                    b = bank()
                    for k in range(KD):
                        last = nc.tensor.matmul(b[:, 0:Q_RANK + KV_RANK], hT[:, k, t * P:(t + 1) * P], w[:, k, 0:Q_RANK + KV_RANK], start=k == 0, stop=k == KD - 1)
                    last.then_inc(full, 1)
                    job += 1
                pe.wait_ge(read, J_MOD + KD + KD // 2)
                for t in range(NC):
                    b = bank()
                    for k in range(KD):
                        last = nc.tensor.matmul(b[:, 0:KV_RANK], hcT[:, k, t * P:(t + 1) * P], w[:, k, Q_RANK:Q_RANK + KV_RANK], start=k == 0, stop=k == KD - 1)
                    last.then_inc(full, 1)
                    job += 1
                pe.wait_ge(sem("krw_set"), 10)
                assert job == J_KR
                for kind, src, width in ((0, hT, SEQ), (1, hT, SEQ), (0, hcT, CTX)):
                    b = bank()
                    for k in range(KD):
                        last = nc.tensor.matmul(b[:, 0:width], krw[:, k, kind, :], src[:, k, :], start=k == 0, stop=k == KD - 1)
                    last.then_inc(full, 1)
                    job += 1
                assert job == J_V
                for s in range(2):
                    pe.wait_ge(read, job + NT - 8)
                    for half in range(2):
                        p = 2 * s + half
                        pe.wait_ge(v_high, p + 1)
                        pe.wait_ge(v_low, p + 1)
                        for t in range(NT):
                            for k in range(KD):
                                if p == 0 and t == 0:
                                    pe.wait_ge(h_low, k + 1)
                                for a, c_ in PARTS:
                                    last = nc.tensor.matmul(PS[:, (job + t) % 8, half * 2 * P:(half + 1) * 2 * P], h_hl[a][:, k, t * P:(t + 1) * P], v_piece[:, half, c_, k, :],
                                                            start=k == 0 and (a, c_) == PARTS[0], stop=k == KD - 1 and (a, c_) == PARTS[-1])
                            if half:
                                last.then_inc(full, 1)
                        if not half:
                            last.then_inc(v_used, 1)
                    job += NT
                pe.wait_ge(tab_in, 80)
                for h in range(2):
                    b = bank()
                    for g in range(4):
                        last = nc.tensor.transpose(b[:, g * P:(g + 1) * P], ws_sb[:, 4 * h + g, :], ident[:, :])
                    last.then_inc(full, 1)
                    job += 1
                pe.wait_ge(sem("zn_done"), 2 * NT + NC)
                for k in range(2):
                    b = bank()
                    for t in range(NT):
                        last = nc.tensor.transpose(b[:, t * P:(t + 1) * P], zq[:, t, k * P:(k + 1) * P], ident[:, :])
                    last.then_inc(full, 1)
                    job += 1
                for t0, n in ((0, NT), (NT, NC)):
                    b = bank()
                    for t in range(n):
                        last = nc.tensor.transpose(b[:, t * P:(t + 1) * P], zq[:, t0 + t, Q_RANK:], ident[:, :])
                    last.then_inc(full, 1)
                    job += 1
                assert job == J_U
                for m in range(8):
                    b = bank()
                    pe.wait_ge(u_high, m + 1)
                    pe.wait_ge(u_low, m + 1)
                    for k in range(KD):
                        for a, c_ in PARTS:
                            last = nc.tensor.matmul(b, u_piece[:, m % 4, a, k, :], h_hl[c_][:, k, :],
                                                    start=k == 0 and (a, c_) == PARTS[0], stop=k == KD - 1 and (a, c_) == PARTS[-1])
                    last.then_inc(full, 1)
                    job += 1
                assert job == J_SGU
                pe.wait_ge(sem("v_done"), NT)
                for g in range(GROUPS):
                    b = bank()
                    for t in range(NT):
                        last = nc.tensor.matmul(b[:, t * P:(t + 1) * P], xn[:, t, g * P:(g + 1) * P], wsT[:, g, :], start=True, stop=True)
                    last.then_inc(full, 1)
                    job += 1

        oT = sb("oT", [P, HEADS, SEQ], scope=late)
        with ExitStack() as here:
            def tmp(name, shape, dtype=F32):
                return sb(name, shape, dtype, scope=here)

            wqr = tmp("wqr", [P, 2, 2, P])
            rot = tmp("rot", [P, 2, SEQ])
            qn = tmp("qn", [P, 2, 2, SEQ], F32R)
            qr = tmp("qr", [P, 2, SEQ], F32R)
            kn = tmp("kn", [P, 2, 2, KEYS], F32R)
            kr = [tmp("kr_hi", [P, KEYS], F32R), over("kr_lo", "krT", [P, KEYS])]
            v_pt = tmp("v_pt", [P, 2, NKT, 2, VD], F32R)
            pT = over("pT", "w_ring", [P, 2, NKT, SEQ], 2 * SLOT)
            probs = tmp("probs", [P, 2, KEYS])
            top_s = tmp("top_s", [P, 2, 1])
            neg_s = tmp("neg_s", [P, 2, 1])
            den = tmp("den", [P, 2, 1])
            rden = tmp("rden", [P, 2, 1])
            acc = over("acc", "w_ring", [P, 2, CH], 2 * SLOT + 2 * NKT * SEQ * 4, F32)
            b_gate = over("b_gate", "w_ring", [P, D], 2 * SLOT + 2 * NKT * SEQ * 4 + 2 * CH * 4, F32)
            ones = tmp("ones", [P, P])
            rep_in, wqr_set = sem("rep_in"), sem("wqr_set")
            proj_full, proj_read, rope_full, rope_done = sem("proj_full"), sem("proj_read"), sem("rope_full"), sem("rope_done")
            scores_full, max_done, exp_done, probs_done = sem("scores_full"), sem("max_done"), sem("exp_done"), sem("probs_done")
            pt_full, pt_copied, o_full, o_copied = sem("pt_full"), sem("pt_copied"), sem("o_full"), sem("o_copied")
            acc_done, b_gate_in, mod_full, mod_read = sem("acc_done"), sem("b_gate_in"), sem("mod_full"), sem("mod_read")
            kr_high, kr_low, proj_low, pt_low = sem("kr_high"), sem("kr_low"), sem("proj_low"), sem("pt_low")
            HPAIRS, PER = HEADS // 2, 2 * NT
            PROJ = 7
            block = here.enter_context(nc.Block())

            def pt_bank(n):
                b = 4 + 2 * (n % 2)
                return PS[:, b:b + 2, :].rearrange("p b n -> p (b n)")[:, 0:KEYS].rearrange("p (k n) -> p k n", k=NKT)

            def proj_jobs():
                for i in range(2):
                    yield PS[:, i, :], lambda a, i=i: qn[:, a, i, :]
                for i in range(2):
                    yield PS[:, 4 + 2 * i:6 + 2 * i, :].rearrange("p b n -> p (b n)")[:, 0:KEYS], lambda a, i=i: kn[:, a, i, :]
                for b in range(3):
                    yield PS[:, b, :], lambda a, b=b: v_pt[:, a, 2 * b:2 * b + 2, :, :].rearrange("p t i v -> p (t i v)")

            @block.sync
            def _(sp):
                for g, gain in enumerate((g_post1, g_post2)):
                    sp.dma_start(gates[:, g, :], gain[0].partition_broadcast(P)).then_inc(rep_in, 16)
                for h in range(1, HPAIRS):
                    sp.wait_ge(proj_full, h * PROJ)
                    load_pair(sp, h)
                    for r in range(2):
                        sp.wait_ge(acc_done, 2 * h - 1 + r)
                        load_mod(sp, h, r)
                    if h >= 2:
                        if h == 3:
                            sp.wait_ge(mod_read, 2 * h + 1)
                        sp.dma_start(b_gate[:, :], b_mod[0][MOD_PART[h] * D:(MOD_PART[h] + 1) * D].partition_broadcast(P)).then_inc(b_gate_in, 16)
                for r in range(2):
                    sp.wait_ge(acc_done, 2 * HPAIRS - 1 + r)
                    load_merge(sp, r)

            @block.gpsimd
            def _(pool):
                nc.gpsimd.memset(ones[:, :], 1.0).then_inc(sem("ones_set"), 1)
                link, pool_turn = Link(pool, sem("pool_link2")), sem("pool_turn")
                with link.loop(HPAIRS, 6) as h:
                    for r in range(2):
                        pool.wait_ge(mod_in[r], h * 16 + 16)
                        pool.wait_ge(mod_full, h * 2 + (r + 1))
                        pool.sem_inc(pool_turn, 1)
                        w = w_ring[:, r]
                        for k in range(KD):
                            last = nc.gpsimd.tensor_scalar(w[:, k, :], w[:, k, :], silu_c[:, 0, k:k + 1], None, ALU.mult)
                        link(last, pool_turn)
                        link(nc.gpsimd.tensor_tensor(w[:, 0:4, :], w[:, 0:4, :], w[:, 4:8, :], ALU.add), pool_turn)
                        link(nc.gpsimd.tensor_tensor(w[:, 0:2, :], w[:, 0:2, :], w[:, 2:4, :], ALU.add), pool_turn)
                        nc.gpsimd.tensor_tensor(acc[:, r, :], w[:, 0, :], w[:, 1, :], ALU.add).then_inc(acc_done, 1)

            @block.tensor
            def _(pe):
                pe.sem_inc(pt_full, 1)
                pe.sem_inc(o_full, 1)
                pe.sem_inc(rope_full, 1)
                pe.sem_inc(mod_full, 2)
                pe.wait_ge(sem("ones_set"), 1)

                def heads(h, gate):
                    pe.wait_ge(pair_in, h * 32 + 32)
                    pe.wait_ge(exp_done, h * PER + 1)
                    pe.wait_ge(pt_copied, h * PER + 1)
                    pe.wait_ge(pt_low, h * PER + 1)
                    for i in range(2):
                        for k in range(2):
                            last = nc.tensor.matmul(PS[:, i, :], wq[:, k, i * (NOPE + ROPE):i * (NOPE + ROPE) + NOPE], cqT[:, k, :], start=k == 0, stop=k == 1)
                        last.then_inc(proj_full, 1)
                    pe.wait_ge(wqr_set, h * 6 + 6)
                    for kind in range(2):
                        for k in range(2):
                            last = nc.tensor.matmul(PS[:, 2 + kind, :], wqr[:, k, kind, :], cqT[:, k, :], start=k == 0, stop=k == 1)
                        last.then_inc(rope_full, 1)
                    pe.wait_ge(mod_read, h * 2 + 1)
                    for i in range(2):
                        if i:
                            pe.wait_ge(o_copied, h * 2 + 1)
                        nc.tensor.matmul(PS[:, 4 + 2 * i, :], wkv[:, i, 0:NOPE], ckvT[:, 0:SEQ], start=True, stop=True)
                        nc.tensor.matmul(PS[:, 5 + 2 * i, 0:CTX], wkv[:, i, 0:NOPE], ckvT[:, SEQ:KEYS], start=True, stop=True).then_inc(proj_full, 1)
                    for b in range(3):
                        if b < 2:
                            pe.wait_ge(proj_read, h * PROJ + (b + 1))
                            pe.wait_ge(proj_low, h * PROJ + (b + 1))
                        else:
                            pe.wait_ge(rope_done, h + 1)
                        for t in range(2):
                            last = nc.tensor.matmul(PS[:, b, t * 2 * VD:(t + 1) * 2 * VD], ckvT[:, (2 * b + t) * P:(2 * b + t + 1) * P],
                                                    wkv[:, :, NOPE:NOPE + VD], start=True, stop=True)
                        last.then_inc(proj_full, 1)

                    def scores(n):
                        i, t, b = n // NT, n % NT, 2 * (n % 2)
                        r = slice(i * ROPE, (i + 1) * ROPE)
                        for bb, k0, k1 in ((b, 0, SEQ), (b + 1, SEQ, KEYS)):
                            for a, c_ in PARTS:
                                nc.tensor.matmul(PS[:, bb, 0:k1 - k0], qn[:, a, i, t * P:(t + 1) * P], kn[:, c_, i, k0:k1], start=(a, c_) == PARTS[0], stop=False)
                            for a, c_ in PARTS:
                                last = nc.tensor.matmul(PS[:, bb, 0:k1 - k0], qr[r, a, t * P:(t + 1) * P], kr[c_][r, k0:k1], start=False, stop=(a, c_) == PARTS[-1])
                        last.then_inc(scores_full, 1)

                    def outputs(i):
                        pe.wait_ge(pt_low, h * PER + (NT * (i + 1) + 1))
                        pe.wait_ge(o_copied, h * 2 + (i + 1))
                        for kt in range(NKT):
                            for a, c_ in PARTS:
                                last = nc.tensor.matmul(PS[:, 7, :], v_pt[:, a, kt, i, :], pT[:, c_, kt, :],
                                                        start=kt == 0 and (a, c_) == PARTS[0], stop=kt == NKT - 1 and (a, c_) == PARTS[-1])
                        last.then_inc(o_full, 1)

                    pe.wait_ge(proj_read, h * PROJ + PROJ)
                    pe.wait_ge(proj_low, h * PROJ + PROJ)
                    pe.wait_ge(rope_done, h + 1)
                    pe.wait_ge(kr_low, 1)
                    scores(0)
                    for n in range(PER):
                        if n + 1 < PER:
                            if n:
                                pe.wait_ge(exp_done, h * PER + (n + 1))
                            scores(n + 1)
                        if n == NT + 1:
                            outputs(0)
                            pe.wait_ge(o_copied, h * 2 + 2)
                        pe.wait_ge(probs_done, h * PER + (n + 1))
                        if n >= 2:
                            pe.wait_ge(pt_copied, h * PER + n)
                            pe.wait_ge(pt_low, h * PER + n)
                        for kt in range(NKT):
                            last = nc.tensor.transpose(pt_bank(n)[:, kt, :], probs[:, n % 2, kt * P:(kt + 1) * P], ident[:, :])
                        last.then_inc(pt_full, 1)
                    pe.wait_ge(pt_copied, h * PER + PER)
                    pe.wait_ge(pt_low, h * PER + PER)
                    for r in range(2):
                        pe.wait_ge(acc_done, h * 2 + (r + 1))
                        if gate:
                            last = nc.tensor.matmul(PS[:, 4 + r, :], ones[:, :], acc[:, r, :], start=True, stop=True)
                        else:
                            for m in range(4):
                                last = nc.tensor.matmul(PS[:, 4 + r, m:m + 1], acc[:, r, m * P:(m + 1) * P], ones[:, 0:1], start=True, stop=True)
                        last.then_inc(mod_full, 1)
                    outputs(1)

                with pe.Fori(0, 2) as h:
                    heads(h, False)
                with pe.Fori(2, HPAIRS) as h:
                    heads(h, True)

            @block.scalar
            def _(act):
                act.sem_inc(exp_done, 1)
                act.sem_inc(pt_copied, 1)
                nc.scalar.copy(kr[0][:, :], krT[:, :]).then_inc(kr_high, 1)
                with act.Fori(0, HPAIRS) as h:
                    act.wait_ge(pair_in, h * 32 + 32)
                    act.wait_ge(rope_full, h * 2 + 1)
                    for i in range(2):
                        src = wq[:, :, i * (NOPE + ROPE) + NOPE:(i + 1) * (NOPE + ROPE)]
                        nc.scalar.copy(wqr[:, :, 0, i * ROPE:(i + 1) * ROPE], src).then_inc(wqr_set, 1)
                        for part in range(2):
                            dst_v = wqr[:, :, 1, i * ROPE:(i + 1) * ROPE].rearrange("p k (h x q) -> p k h x q", h=2, x=2)[:, :, :, part, :]
                            src_v = src.rearrange("p k (h x q) -> p k h x q", h=2, x=2)[:, :, :, 1 - part, :]
                            nc.scalar.copy(dst_v, src_v).then_inc(wqr_set, 1)
                    for job, (bank, part) in enumerate(proj_jobs()):
                        act.wait_ge(proj_full, h * PROJ + (job + 1))
                        nc.scalar.copy(part(0), bank).then_inc(proj_read, 1)

                    def exps(n):
                        act.wait_ge(max_done, h * PER + (n + 1))
                        if n:
                            act.wait_ge(pt_full, h * PER + n)
                        s = PS[:, 2 * (n % 2):2 * (n % 2) + 2, :].rearrange("p b n -> p (b n)")[:, 0:KEYS]
                        nc.scalar.activation(probs[:, n % 2, :], s, ACT.Exp, bias=neg_s[:, n % 2, :], scale=SCALE,
                                             accum_out=den[:, n % 2, :]).then_inc(exp_done, 1)

                    exps(0)
                    for n in range(PER):
                        if n + 1 < PER:
                            exps(n + 1)
                        act.wait_ge(pt_full, h * PER + (n + 2))
                        if n % NT == 0:
                            act.wait_ge(o_full, h * 2 + (n // NT + 1))
                        nc.scalar.copy(pT[:, 0, :, n % NT * P:(n % NT + 1) * P], pt_bank(n)).then_inc(pt_copied, 1)

            @block.vector
            def _(dve):
                link = Link(dve, sem("dve_link2"))
                dve.sem_inc(o_copied, 1)
                dve.sem_inc(pt_low, 1)
                dve.sem_inc(mod_read, 1)
                dve.wait_ge(kr_high, 1)
                nc.vector.tensor_tensor(kr[1][:, :], krT[:, :], kr[0][:, :].bitcast(F32), ALU.subtract).then_inc(kr_low, 1)

                def heads(h, gate):
                    for job, (bank, part) in enumerate(proj_jobs()):
                        if job == 2:
                            for kind, table in ((0, cos_sb), (1, sin_sb)):
                                dve.wait_ge(rope_full, h * 2 + (kind + 2))
                                link(nc.vector.tensor_tensor(rot[:, kind, :], PS[:, 2 + kind, :], table[:, :], ALU.mult))
                            link(nc.vector.tensor_tensor(rot[:, 0, :], rot[:, 0, :], rot[:, 1, :], ALU.add))
                            link(nc.vector.tensor_copy(qr[:, 0, :], rot[:, 0, :]))
                            nc.vector.tensor_tensor(qr[:, 1, :], rot[:, 0, :], qr[:, 0, :].bitcast(F32), ALU.subtract).then_inc(rope_done, 1)
                        dve.wait_ge(proj_read, h * PROJ + (job + 1))
                        nc.vector.tensor_tensor(part(1), bank, part(0).bitcast(F32), ALU.subtract).then_inc(proj_low, 1)

                    def largest(n):
                        b = n % 2
                        dve.wait_ge(scores_full, h * PER + (n + 1))
                        s = PS[:, 2 * b:2 * b + 2, :].rearrange("p b n -> p (b n)")[:, 0:KEYS]
                        link(nc.vector.reduce_max(top_s[:, b, :], s, AX.X))
                        nc.vector.tensor_scalar(neg_s[:, b, :], top_s[:, b, :], -SCALE, None, ALU.mult).then_inc(max_done, 1)

                    def low(n):
                        dve.wait_ge(pt_copied, h * PER + (n + 2))
                        at = slice(n % NT * P, (n % NT + 1) * P)
                        nc.vector.tensor_tensor(pT[:, 1, :, at], pt_bank(n), pT[:, 0, :, at].bitcast(F32), ALU.subtract).then_inc(pt_low, 1)

                    def output(i):
                        dve.wait_ge(o_full, h * 2 + (i + 2))
                        nc.vector.tensor_copy(oT[:, col(h * 2 + i), :].rearrange("p a n -> p (a n)"), PS[:, 7, :]).then_inc(o_copied, 1)

                    def normalise(n):
                        b = n % 2
                        dve.wait_ge(exp_done, h * PER + (n + 2))
                        link(nc.vector.reciprocal(rden[:, b, :], den[:, b, :]))
                        nc.vector.tensor_scalar(probs[:, b, :], probs[:, b, :], rden[:, b, :], None, ALU.mult).then_inc(probs_done, 1)

                    largest(0)
                    normalise(0)
                    for n in range(PER):
                        if n + 1 < PER:
                            largest(n + 1)
                        if n == NT + 1:
                            output(0)
                        if n:
                            low(n - 1)
                        if n + 1 < PER:
                            normalise(n + 1)
                    low(PER - 1)
                    for r in range(2):
                        dve.wait_ge(mod_full, h * 2 + (r + 3))
                        if gate:
                            half = slice(r * CH, (r + 1) * CH)
                            g = gates[:, bass.ds(h - 2, 1), half].rearrange("p a n -> p (a n)")
                            dve.wait_ge(b_gate_in, h * 16 - 16)
                            link(nc.vector.tensor_tensor(b_gate[:, half], PS[:, 4 + r, :], b_gate[:, half], ALU.add))
                            nc.vector.tensor_tensor(g, b_gate[:, half], g, ALU.mult).then_inc(mod_read, 1)
                        else:
                            nc.vector.tensor_copy(mod2[:, col(h), 4 * r:4 * r + 4].rearrange("p a k -> p (a k)"), PS[:, 4 + r, 0:4]).then_inc(mod_read, 1)
                    output(1)

                with link.loop(2, 4 + 2 * PER) as h:
                    heads(h, False)
                dve.wait_ge(mod_read, 5)
                link(nc.vector.tensor_tensor(mod2[:, :, :].rearrange("p a k -> p (a k)"), mod2[:, :, :].rearrange("p a k -> p (a k)"), cols[:, 3 * KD:5 * KD], ALU.add))
                link(nc.vector.scalar_tensor_tensor(out=mod2[:, 1, :], in0=mod2[:, 1, :], scalar=1.0, in1=cols[:, C_PRE2:C_PRE2 + KD], op0=ALU.add, op1=ALU.mult))
                dve.wait_ge(rep_in, 2 * 16)
                with link.loop(HPAIRS - 2, 6 + 2 * PER, first=2) as h:
                    heads(h, True)

        heads_w.close()

        full3 = sem("merge_full")
        with ExitStack() as here:
            def tmp(name, shape, dtype=F32):
                return sb(name, shape, dtype, scope=here)

            src_hi = [tmp(f"{n}_hi", [P, KD, SEQ], F32R) for n in ("hT", "o_aT", "oT")]
            src = [[hi, over(f"{n}_lo", n, [P, KD, SEQ])] for hi, n in zip(src_hi, ("hT", "o_aT", "oT"))]
            piece = over("piece", "w_ring", [P, 4, 2, KD, P], 2 * SLOT)
            wo = [over("wo_hi", "w_ring", [P, 2, KD, CH], 2 * SLOT), over("wo_lo", "w_ring", [P, 2, KD, CH])]
            mT = x_sb[:, :, :].rearrange("p t d -> p (t d)").rearrange("p (k n) -> p k n", k=KD)
            xn2 = over("xn2", "o_aT_hi", [P, NT, D], dtype=F32)
            m = src[0]
            sig = tmp("sig", [P, 2, 2, SEQ])
            prod = tmp("prod", [P, 2, SEQ])
            ysq = tmp("ysq", [P, 2, NT])
            yroot = tmp("yroot", [P, 2, NT])
            yrstd = tmp("yrstd", [P, 1, NT])
            src_high, src_low, piece_high, piece_low = sem("src_high"), sem("src_low"), sem("piece_high"), sem("piece_low")
            wo_in, wo_high, wo_low, m_high, m_low = [sem(f"wo_in{r}") for r in range(2)], sem("wo_high"), sem("wo_low"), sem("m_high"), sem("m_low")
            sig_done, prod_done, m_done, y_half, y_full, y_read = sem("sig_done"), sem("prod_done"), sem("m_done"), sem("y_half"), sem("y_full"), sem("y_read")
            ysq_done, root3, x1_done, x_again, xn2_done = sem("ysq_done"), sem("root3"), sem("x1_done"), sem("x_again"), sem("xn2_done")
            block = here.enter_context(nc.Block())

            @block.sync
            def _(sp):
                for n in range(2, 8):
                    sp.wait_ge(piece_low, 4 * (n - 1))
                    load_merge(sp, n)
                for h in range(2):
                    sp.wait_ge(piece_low, 4 * (7 + h))
                    sp.dma_start(w_ring[:, h], w_o_k[:, :, h * CH:(h + 1) * CH]).then_inc(wo_in[h], 16)
                sp.wait_ge(m_low, KD)
                sp.dma_start(x_sb[:, :, :], x[0].rearrange("(t p) d -> p t d", p=P)).then_inc(x_again, 16)
                for s in range(4):
                    if s % 2 == 0:
                        sp.wait_ge(y_full if s else y_half, NT)
                    sp.dma_start(w_ring[:, PQ_SLOT[s]], w_pq_k[:, :, s * CH:(s + 1) * CH]).then_inc(pq_in[s], 16)

            @block.tensor
            def _(pe):
                for n in range(8):
                    b = n % 2 * 4
                    if n >= 2:
                        pe.wait_ge(sig_done, 2 * (n - 1))
                        pe.wait_ge(prod_done, 2 * (n - 1))
                    for j, i in enumerate((0, 0, 1, 2)):
                        pe.wait_ge(piece_high, 4 * n + j + 1)
                        pe.wait_ge(piece_low, 4 * n + j + 1)
                        for k in range(KD):
                            if n == 0:
                                pe.wait_ge(src_low, i * KD + k + 1)
                            for a, c_ in PARTS:
                                last = nc.tensor.matmul(PS[:, b + j, :], piece[:, j, a, k, :], src[i][c_][:, k, :],
                                                        start=k == 0 and (a, c_) == PARTS[0], stop=k == KD - 1 and (a, c_) == PARTS[-1])
                        last.then_inc(full3, 1)
                for h in range(2):
                    pe.wait_ge(wo_high, h + 1)
                    pe.wait_ge(wo_low, h + 1)
                    for t in range(NT):
                        for k in range(KD):
                            if h == 0 and t == 0:
                                pe.wait_ge(m_low, k + 1)
                            for a, c_ in PARTS:
                                last = nc.tensor.matmul(PS[:, 2 * t + h, :], m[a][:, k, t * P:(t + 1) * P], wo[c_][:, h, k, :],
                                                        start=k == 0 and (a, c_) == PARTS[0], stop=k == KD - 1 and (a, c_) == PARTS[-1])
                        last.then_inc(y_full if h else y_half, 1)

            @block.scalar
            def _(act):
                def high(g):
                    n, j = g // 4, g % 4
                    act.wait_ge(m_in[n % 2], 64 * (n // 2 + 1))
                    if n:
                        act.wait_ge(full3, g - 3)
                    nc.scalar.copy(piece[:, j, 0, :, :], m_raw[:, n % 2, j, :, :]).then_inc(piece_high, 1)

                for j in range(4):
                    high(j)
                    if j != 1:
                        i = max(j - 1, 0)
                        for k in range(KD):
                            nc.scalar.copy(src_hi[i][:, k, :], (hT, o_aT, oT)[i][:, k, :]).then_inc(src_high, 1)
                for n in range(8):
                    for j in range(4):
                        if n < 7:
                            high(4 * (n + 1) + j)
                        if j < 2:
                            act.wait_ge(full3, 4 * n + j + 1)
                            if n >= 2:
                                act.wait_ge(prod_done, 2 * (n - 2) + j + 1)
                            nc.scalar.activation(sig[:, n % 2, j, :], PS[:, n % 2 * 4 + j, :], ACT.Sigmoid).then_inc(sig_done, 1)

                def wo_hi(h):
                    act.wait_ge(wo_in[h], 16)
                    act.wait_ge(full3, 30 + 2 * h)
                    nc.scalar.copy(wo[0][:, h, :, :], w_ring[:, h]).then_inc(wo_high, 1)

                wo_hi(0)
                for n in range(8):
                    act.wait_ge(m_done, n + 1)
                    nc.scalar.copy(m[0][:, n, :], mT[:, n, :]).then_inc(m_high, 1)
                wo_hi(1)
                for t in range(NT):
                    for kind in range(2):
                        act.wait_ge(x1_done if kind else y_full, t + 1)
                        vec = x_sb[:, t, :] if kind else PS[:, 2 * t:2 * t + 2, :].rearrange("p b n -> p (b n)")
                        scratch = sig[:, kind, :, :].rearrange("p a n -> p (a n)")
                        nc.scalar.activation(scratch, vec, ACT.Square, accum_out=ysq[:, kind, t:t + 1]).then_inc(ysq_done, 1)
                        act.wait_ge(ysq_done, 2 * t + kind + 1)
                        nc.scalar.activation(yroot[:, kind, t:t + 1], ysq[:, kind, t:t + 1], ACT.Sqrt, bias=eps[:, :], scale=1.0 / D).then_inc(root3, 1)

            @block.vector
            def _(dve):
                link = Link(dve, sem("dve_link3"))

                def low(g):
                    n, j = g // 4, g % 4
                    dve.wait_ge(piece_high, g + 1)
                    nc.vector.tensor_tensor(piece[:, j, 1, :, :], m_raw[:, n % 2, j, :, :], piece[:, j, 0, :, :].bitcast(F32), ALU.subtract).then_inc(piece_low, 1)

                def m_lo(n):
                    dve.wait_ge(m_high, n + 1)
                    nc.vector.tensor_tensor(m[1][:, n, :], mT[:, n, :], m[0][:, n, :].bitcast(F32), ALU.subtract).then_inc(m_low, 1)

                def wo_lo(h):
                    dve.wait_ge(wo_high, h + 1)
                    nc.vector.tensor_tensor(wo[1][:, h, :, :], w_ring[:, h], wo[0][:, h, :, :].bitcast(F32), ALU.subtract).then_inc(wo_low, 1)

                for j in range(4):
                    low(j)
                    if j != 1:
                        i = max(j - 1, 0)
                        for k in range(KD):
                            dve.wait_ge(src_high, i * KD + k + 1)
                            nc.vector.tensor_tensor(src[i][1][:, k, :], (hT, o_aT, oT)[i][:, k, :], src_hi[i][:, k, :].bitcast(F32), ALU.subtract).then_inc(src_low, 1)
                for n in range(8):
                    if n == 7:
                        wo_lo(0)
                        for k in range(7):
                            m_lo(k)
                    for j in range(4):
                        if n < 7:
                            low(4 * (n + 1) + j)
                        if j >= 2:
                            dve.wait_ge(full3, 4 * n + j + 1)
                            dve.wait_ge(sig_done, 2 * n + j - 1)
                            if n:
                                dve.wait_ge(m_done, n)
                            nc.vector.tensor_tensor(prod[:, j - 2, :], sig[:, n % 2, j - 2, :], PS[:, n % 2 * 4 + j, :], ALU.mult).then_inc(prod_done, 1)
                    dve.wait_ge(prod_done, 2 * n + 2)
                    nc.vector.tensor_tensor(mT[:, n, :], prod[:, 0, :], prod[:, 1, :], ALU.add).then_inc(m_done, 1)
                m_lo(7)
                wo_lo(1)
                dve.wait_ge(m_done, 8)
                dve.wait_ge(x_again, 16)
                for t in range(NT):
                    y = PS[:, 2 * t:2 * t + 2, :].rearrange("p b n -> p (b n)")
                    scaled = prod[:, :, :].rearrange("p b n -> p (b n)")
                    dve.wait_ge(root3, 2 * t + 1)
                    link(nc.vector.reciprocal(yrstd[:, 0, t:t + 1], yroot[:, 0, t:t + 1]))
                    if t:
                        dve.wait_ge(x1_done, t)
                    nc.vector.scalar_tensor_tensor(out=scaled, in0=y, scalar=yrstd[:, 0, t:t + 1], in1=gates[:, 0, :], op0=ALU.mult, op1=ALU.mult).then_inc(y_read, 1)
                    dve.wait_ge(y_read, t + 1)
                    nc.vector.tensor_tensor(x_sb[:, t, :], x_sb[:, t, :], scaled, ALU.add).then_inc(x1_done, 1)
                    dve.wait_ge(root3, 2 * t + 2)
                    link(nc.vector.reciprocal(rstd2[:, t:t + 1], yroot[:, 1, t:t + 1]))
                    nc.vector.tensor_scalar(xn2[:, t, :], x_sb[:, t, :], rstd2[:, t:t + 1], None, ALU.mult).then_inc(xn2_done, 1)
        late.close()

        act_dram = nc.dram_tensor("act_dram", (P, NK, SEQ), F32).ap()
        wgt_dram = nc.dram_tensor("wgt_dram", (P, SEQ // STAGE, NK, STAGE), F32).ap()
        hidden = top.enter_context(ExitStack())
        h2 = [sb(f"h2_{n}", [P, KD, SEQ], F32R, scope=hidden) for n in ("hi", "lo")]
        s_all = w_ring[:, 0:2].rearrange("p r k n -> p (r k n)").rearrange("p (t h k) -> p t h k", t=NT, h=2 * PH)
        u_raw = w_ring[:, 2:4].rearrange("p r k n -> p (r k n)").rearrange("p (r a d) -> p r a d", r=PAIRS, a=2)
        u_in = [sem(f"u_in{r}") for r in range(PAIRS)]
        u_v = u_exp[0].rearrange("(p b) d -> p b d", p=P)

        v_v = v_exp[0].rearrange("(p b) d -> p b d", p=P)
        v_raw = w_ring[:, 2:4].rearrange("p r k n -> p (r k n)").rearrange("p (r a d) -> p r a d", r=2, a=4)
        v_in, aw_in = [sem(f"v_in{r}") for r in range(2)], [sem(f"aw_in{r}") for r in range(2)]
        w_first, AHEAD = sem("wgt_first"), 8

        def load_v(sp, n, r):
            sp.dma_start(v_raw[:, r, :, :], v_v[:, bass.ds(n * 4, 4), :]).then_inc(v_in[r], 16)

        def load_u(sp, pair, q):
            sp.dma_start(u_raw[:, q, :, :], u_v[:, bass.ds(pair * 2, 2), :]).then_inc(u_in[q], 16)

        with ExitStack() as here:
            def tmp(name, shape, dtype=F32):
                return sb(name, shape, dtype, scope=here)

            w_hl = [tmp(f"w_{n}", [P, 4, KD, P], F32R) for n in ("hi", "lo")]
            qT = tmp("qT", [P, 2 * PH, SEQ])
            k_sb = tmp("k_sb", [P, 2, P])
            kT = tmp("kT", [P, 2, NK])
            h2_f = tmp("h2_f", [P, 4, SEQ])
            k_in, kt_full, kt_read = sem("k_in"), sem("kt_full"), sem("kt_read")
            h2_full, h2_hi, h2_read, h2_lo = sem("h2_full"), sem("h2_hi"), sem("h2_read"), sem("h2_lo")
            whi_done, wlo_done, wsplit_used = sem("whi_done"), sem("wlo_done"), sem("wsplit_used")
            q_full, q_read, key_full, key_read = sem("q_full"), sem("q_read"), sem("key_full"), sem("key_read")
            block = here.enter_context(nc.Block())

            @block.sync
            def _(sp):
                sp.dma_start(k_sb[:, 0, :], k1[0]).then_inc(k_in, 16)
                sp.dma_start(k_sb[:, 1, :], k2[0]).then_inc(k_in, 16)
                sp.wait_ge(wlo_done, 2 * PH)
                for q in range(PAIRS):
                    load_u(sp, q, q)

            @block.gpsimd
            def _(pool):
                for k in range(KD):
                    pool.wait_ge(h2_read, k + 1)
                    nc.gpsimd.tensor_tensor(h2[1][:, k, :], h2_f[:, k % 4, :], h2[0][:, k, :].bitcast(F32), ALU.subtract).then_inc(h2_lo, 1)

            @block.tensor
            def _(pe):
                pe.wait_ge(xn2_done, NT)
                for k in range(KD):
                    for t in range(NT):
                        last = nc.tensor.transpose(PS[:, k, t * P:(t + 1) * P], xn2[:, t, k * P:(k + 1) * P], ident[:, :])
                    last.then_inc(h2_full, 1)
                def products(n, k, parts):
                    for a, c_ in parts:
                        last = nc.tensor.matmul(PS[:, n % 8, :], w_hl[a][:, n % 4, k, :], h2[c_][:, k, :],
                                                start=k == 0 and (a, c_) == (0, 0), stop=k == KD - 1 and (a, c_) == (0, 1), skip_group_check=True)
                    return last

                for n in range(4):
                    pe.wait_ge(h2_read, n + 1)
                    pe.wait_ge(whi_done, n + 1)
                    pe.wait_ge(wlo_done, n + 1)
                    for k in range(KD):
                        if n == 0:
                            pe.wait_ge(h2_hi, k + 1)
                        products(n, k, ((0, 0), (1, 0)))
                for n in range(4):
                    for k in range(KD):
                        if n == 0:
                            pe.wait_ge(h2_lo, k + 1)
                        last = products(n, k, ((0, 1),))
                    last.then_inc(q_full, 1)
                for n in range(4, 2 * PH):
                    pe.wait_ge(whi_done, n + 1)
                    pe.wait_ge(wlo_done, n + 1)
                    if n >= 8:
                        pe.wait_ge(q_read, n - 7)
                    if n == 8:
                        pe.wait_ge(k_in, 32)
                        for i in range(2):
                            last = nc.tensor.transpose(PS[:, 0, i * P:(i + 1) * P], k_sb[:, i, :], ident[:, :])
                        last.then_inc(kt_full, 1)
                        pe.wait_ge(kt_read, 1)
                    for k in range(KD):
                        last = products(n, k, ((0, 0), (1, 0), (0, 1)))
                    last.then_inc(q_full, 1)
                pe.wait_ge(q_read, 2 * PH)
                for t in range(NT):
                    if t >= 2:
                        pe.wait_ge(key_read, t - 1)
                    for n in range(2 * PH):
                        last = nc.tensor.matmul(PS[:, t % 2 * 4 + n // 4, n % 4 * NK:(n % 4 + 1) * NK], qT[:, n, t * P:(t + 1) * P], kT[:, n % 2, :], start=True, stop=True)
                    last.then_inc(key_full, 1)

            @block.scalar
            def _(act):

                def w_high(n):
                    c_, m = n // 4, n % 4
                    act.wait_ge(pq_in[c_], 16)
                    nc.scalar.copy(w_hl[0][:, m, :, :], w_ring[:, PQ_SLOT[c_], :, m * P:(m + 1) * P]).then_inc(whi_done, 1)

                w_high(0)
                for k in range(KD):
                    act.wait_ge(h2_full, k + 1)
                    nc.scalar.activation(h2[0][:, k, :], PS[:, k, :], ACT.Identity, bias=mod2[:, 0, k:k + 1], scale=mod2[:, 1, k:k + 1]).then_inc(h2_hi, 1)
                for n in range(1, 4):
                    w_high(n)
                for n in range(2 * PH):
                    if n == 8:
                        act.wait_ge(kt_full, 1)
                        nc.scalar.copy(kT[:, :, :], PS[:, 0, 0:2 * P].rearrange("p (i n) -> p i n", i=2)).then_inc(kt_read, 1)
                    act.wait_ge(q_full, n + 1)
                    nc.scalar.copy(qT[:, n, :], PS[:, n % 8, :]).then_inc(q_read, 1)
                    if n + 4 < 2 * PH:
                        w_high(n + 4)
                act.wait_ge(wlo_done, 16)
                for t in range(NT):
                    act.wait_ge(key_full, t + 1)
                    nc.scalar.copy(s_all[:, t, :, :].rearrange("p h k -> p (h k)"), PS[:, t % 2 * 4:t % 2 * 4 + 4, :].rearrange("p b n -> p (b n)")).then_inc(key_read, 1)

            @block.vector
            def _(dve):
                def w_low(n):
                    c_, m = n // 4, n % 4
                    dve.wait_ge(whi_done, n + 1)
                    nc.vector.tensor_tensor(w_hl[1][:, m, :, :], w_ring[:, PQ_SLOT[c_], :, m * P:(m + 1) * P], w_hl[0][:, m, :, :].bitcast(F32), ALU.subtract).then_inc(wlo_done, 1)

                w_low(0)
                for k in range(KD):
                    dve.wait_ge(h2_hi, k + 1)
                    if k >= 4:
                        dve.wait_ge(h2_lo, k - 3)
                    nc.vector.tensor_scalar(h2_f[:, k % 4, :], PS[:, k, :], mod2[:, 1, k:k + 1], mod2[:, 0, k:k + 1], ALU.mult, ALU.add).then_inc(h2_read, 1)
                for n in range(1, 2 * PH):
                    w_low(n)

        with ExitStack() as here:
            def tmp(name, shape, dtype=F32):
                return sb(name, shape, dtype, scope=here)

            uT = [tmp(f"uT_{n}", [P, 2, KD, P], F32R) for n in ("hi", "lo")]
            a_out = tmp("a_out", [P, 2, 2, SEQ])
            s_cur = tmp("s_cur", [P, 2 * PH, NK])
            s_rest = tmp("s_rest", [P, 2 * PH, NK])
            best = tmp("best", [P, 2 * PH, TOP])
            best_i = tmp("best_i", [P, 2 * PH, TOP], U32)
            best_f = tmp("best_f", [P, 2 * PH, TOP])
            cand = s_cur[:, :, :].rearrange("p h k -> p (h k)").rearrange("p (h c) -> p h c", h=PH)
            cand_rest = s_rest[:, :, :].rearrange("p h k -> p (h k)").rearrange("p (h c) -> p h c", h=PH)
            picks = s_rest[:, :, :].rearrange("p h k -> p (h k)").rearrange("p (s a) -> p s a", a=TOP)
            top_v = tmp("top_v", [P, PH, TOP])
            top_p = tmp("top_p", [P, SLOTS], U32)
            part = tmp("part", [P, 2, SLOTS], U32)
            part_f = tmp("part_f", [P, 2, SLOTS])
            chosen = tmp("chosen", [P, NT, 3, SLOTS])
            expo = tmp("expo", [P, PH, TOP])
            total = tmp("total", [P, PH])
            iota_i = tmp("iota_i", [P, NK], I32)
            iota_f = tmp("iota_f", [P, TOP])
            iota_k = tmp("iota_k", [P, NK])
            slotT = s_cur[:, :, :].rearrange("p h k -> p (h k)").rearrange("p (a t) -> p a t", a=4)
            partT = s_rest[:, :, :].rearrange("p h k -> p (h k)").rearrange("p (a t) -> p a t", a=4).bitcast(F32R)
            tmp("a_space", [P, 4, SEQ])
            a_first = over("a_first", "a_space", [P, 4, SEQ], dtype=F32)
            w_low = s_rest[:, :, :].rearrange("p h k -> p (h k)")[:, 2 * SEQ:4 * SEQ].rearrange("p (r b t) -> p r b t", r=2, b=NK)
            hot1 = tmp("hot1", [P, HOTS, TOK, NK], F32R)
            hot2 = tmp("hot2", [P, HOTS, TOK, 2, NK], F32R)
            w_stage = w_ring[:, 0:2].rearrange("p r k n -> p (r k n)").rearrange("p (s b t) -> p s b t", s=2, b=NK)
            ut_full, ut_hi, ut_lo = sem("ut_full"), sem("ut_hi"), sem("ut_lo")
            a_full, a_done, a_stored = sem("a_full"), sem("a_done"), [sem(f"a_stored{r}") for r in range(2)]
            s_cur_set, s_used, soft_in, soft_out, chosen_done = sem("s_cur_set"), sem("s_used"), sem("soft_in"), sem("soft_out"), sem("chosen_done")
            slot_full, slot_read, hot_done, w_added = sem("slot_full"), sem("slot_read"), sem("hot_done"), sem("wgt_added")
            w_full, w_read, w_stored = sem("wgt_full"), sem("wgt_read"), [sem(f"wgt_stored{r}") for r in range(2)]
            iota_set, turn = sem("iota_set"), sem("turn")
            LOW = -3.0e38
            block = here.enter_context(nc.Block())

            def w_bank(n):
                b = 4 + 2 * (n % 2)
                return PS[:, b:b + 2, :].rearrange("p b n -> p (b n)").rearrange("p (t g k) -> p t g k", t=TOK, g=2)

            CREDIT = HOTS

            @block.sync
            def _(sp):
                def next_u(i, q):
                    sp.wait_ge(ut_full, i * (4 * PAIRS) + (4 * q + 4))
                    load_u(sp, i * PAIRS + (PAIRS + q), q)

                def store_w(n, s):
                    sp.wait_ge(w_added, n * 16 + (8 * s + 8 + 2))
                    sp.dma_start(wgt_dram[:, bass.ds(n * 2 + s, 1), :, :].rearrange("p a b t -> p (a b t)"),
                                 w_stage[:, s, :, :].rearrange("p b t -> p (b t)")).then_inc(w_stored[s], 16)

                H = HALF // 2 // PAIRS
                with sp.Fori(0, H) as i:
                    for q in range(PAIRS):
                        next_u(i, q)

                def dense(i, load=True, prior=True):
                    for q in range(PAIRS):
                        if load:
                            next_u(i, q)
                        if q == 1 and prior:
                            store_w(i - (H + 1), 1)
                        if q == 2:
                            store_w(i - H, 0)

                dense(H, prior=False)
                with sp.Fori(H + 1, 2 * H - 1) as i:
                    dense(i)
                dense(2 * H - 1, load=False)
                for r in range(2):
                    sp.wait_ge(a_stored[r], 16 + 16)
                sp.dma_start(a_first[:, :, :], act_dram[:, 0:4, :]).then_inc(aw_in[0], 16)
                for r in range(2):
                    sp.wait_ge(ut_full, 2 * NK - 4 * PAIRS + 8 * (r + 1))
                    load_v(sp, r, r)
                sp.wait_ge(w_added, SEQ // TOK + 2)
                sp.dma_start(wgt_dram[:, SEQ // STAGE - 1, 0:AHEAD, :], w_stage[:, 1, 0:AHEAD, :]).then_inc(w_first, 16)

            @block.gpsimd
            def _(pool):
                nc.gpsimd.iota(iota_i[:, :], pattern=[[1, NK]], base=0, channel_multiplier=0).then_inc(iota_set, 1)
                pool_turn = sem("pool_turn")
                pool.sem_inc(w_added, 2)
                with pool.Fori(0, (NK - HALF) // 8) as i:
                    for n in range(16):
                        pool.wait_ge(w_read, i * 16 + (n + 1 + CREDIT))
                        pool.sem_inc(pool_turn, 1)
                        w = w_stage[:, n // 8, :, n % 8 * TOK:(n % 8 + 1) * TOK]
                        nc.gpsimd.tensor_tensor(w, w, w_low[:, n % 2, :, :], ALU.add).then_inc(w_added, 1)

            @block.tensor
            def _(pe):
                pe.sem_inc(a_full, CREDIT)
                pe.sem_inc(w_full, CREDIT)

                def turn_u(i, q, r, first=False):
                    pe.wait_ge(u_in[q], i * 16 + 16)
                    for half in range(2):
                        if not first:
                            pe.wait_ge(ut_hi, i * (4 * PAIRS) + (4 * q + 2 * r + half - 1))
                            pe.wait_ge(ut_lo, i * (4 * PAIRS) + (4 * q + 2 * r + half - 1))
                        for k in range(4):
                            last = nc.tensor.transpose(PS[:, half, k * P:(k + 1) * P], u_raw[:, q, r, (4 * half + k) * P:(4 * half + k + 1) * P], ident[:, :])
                        last.then_inc(ut_full, 1)

                def activations(i, q, r):
                    pe.wait_ge(ut_hi, i * (4 * PAIRS) + (4 * q + 2 * r + 2))
                    pe.wait_ge(ut_lo, i * (4 * PAIRS) + (4 * q + 2 * r + 2))
                    pe.wait_ge(a_done, i * (2 * PAIRS) + (2 * q + r - 1 + CREDIT))
                    for k in range(KD):
                        for a, c_ in PARTS:
                            last = nc.tensor.matmul(PS[:, 2 + r, :], uT[a][:, r, k, :], h2[c_][:, k, :],
                                                    start=k == 0 and (a, c_) == PARTS[0], stop=k == KD - 1 and (a, c_) == PARTS[-1])
                    last.then_inc(a_full, 1)

                def weights(i, n):
                    pe.wait_ge(hot_done, i * (4 * PAIRS) + (n + 1))
                    pe.wait_ge(w_read, i * (4 * PAIRS) + (n - 1 + CREDIT))
                    for j in range(TOK):
                        last = nc.tensor.matmul(w_bank(n)[:, j, :, :], hot1[:, n % HOTS, j, :], hot2[:, n % HOTS, j, :, :], start=True, stop=True)
                    last.then_inc(w_full, 1)

                def pairs(i, dense=None, more=True):
                    for q in range(PAIRS):
                        turn_u(i, q, 1)
                        activations(i, q, 0)
                        if dense is not None:
                            weights(dense, 4 * q)
                            weights(dense, 4 * q + 1)
                        if q < PAIRS - 1:
                            turn_u(i, q + 1, 0)
                        elif more:
                            turn_u(i + 1, 0, 0)
                        activations(i, q, 1)
                        if dense is not None:
                            weights(dense, 4 * q + 2)
                            weights(dense, 4 * q + 3)

                turn_u(0, 0, 0, first=True)
                with pe.Fori(0, HALF // 2 // PAIRS) as i:
                    pairs(i)
                pe.wait_ge(chosen_done, NT)
                for a in range(3):
                    for t in range(NT):
                        last = nc.tensor.transpose(PS[:, 4 + a, t * P:(t + 1) * P], chosen[:, t, a, :], ident[:, :])
                last.then_inc(slot_full, 1)
                pe.wait_ge(slot_read, 1)
                with pe.Fori(HALF // 2 // PAIRS, NK // 2 // PAIRS - 1) as i:
                    pairs(i, dense=i - HALF // 2 // PAIRS)
                pairs(NK // 2 // PAIRS - 1, dense=(NK - HALF) // 2 // PAIRS - 1, more=False)

            @block.scalar
            def _(act):
                act.sem_inc(a_done, CREDIT)
                act.sem_inc(w_read, CREDIT)
                for r in range(2):
                    act.sem_inc(a_stored[r], 16)
                    act.sem_inc(w_stored[r], 16)

                def high(i, j):
                    r = j % 2
                    act.wait_ge(a_full, i * 16 + (j - 1 + CREDIT))
                    for half in range(2):
                        act.wait_ge(ut_full, i * 32 + (2 * j + half + 1))
                        nc.scalar.copy(uT[0][:, r, 4 * half:4 * half + 4, :].rearrange("p k n -> p (k n)"), PS[:, half, :]).then_inc(ut_hi, 1)

                def gelu(i, j):
                    s = j // 2 % 2
                    if j % 2 == 0:
                        act.wait_ge(a_stored[s], i * 64 + 16 * (j // 4) + 16)
                    act.wait_ge(a_full, i * 16 + (j + 1 + CREDIT))
                    nc.scalar.activation(a_out[:, s, j % 2, :], PS[:, 2 + j % 2, :], ACT.Gelu_apprx_tanh).then_inc(a_done, 1)
                    if j % 2:
                        act.wait_ge(a_done, i * 16 + (j + 1 + CREDIT))
                        act.dma_start(act_dram[:, bass.ds(i * 16 + (j - 1), 2), :], a_out[:, s, :, :]).then_inc(a_stored[s], 16)

                def scores_of(t):
                    nc.scalar.copy(s_cur[:, :, :], s_all[:, col(t), :, :].rearrange("p a h k -> p (a h) k")).then_inc(s_cur_set, 1)

                def choice(t, more):
                    for j in range(16):
                        high(t, j + 1)
                        gelu(t, j)
                        if j == EXP_AT:
                            act.wait_ge(soft_in, t + 1)
                            nc.scalar.activation(expo[:, :, :], expo[:, :, :], ACT.Exp).then_inc(soft_out, 1)
                            if more:
                                act.wait_ge(s_used, t + 1)
                                scores_of(t + 1)

                scores_of(0)
                high(0, 0)
                with act.Fori(0, NT - 1) as t:
                    choice(t, True)
                choice(NT - 1, False)

                def dense(i, more):
                    for j in range(16):
                        if j < 15 or more:
                            high(i, j + 1)
                        gelu(i, j)
                        s = j // 4 % 2
                        if j % 4 == 0:
                            act.wait_ge(w_stored[s], (i - NT) * 32 + 16 * (j // 8) + 16)
                        for n in range(2):
                            c0 = (2 * (j % 4) + n) * TOK
                            act.wait_ge(w_full, (i - NT) * 32 + (2 * j + n + 1 + CREDIT))
                            nc.scalar.copy(w_stage[:, s, :, c0:c0 + TOK], w_bank(n)[:, :, 0, :].rearrange("p t b -> p b t"))
                            act.wait_ge(w_added, (i - NT) * 32 + (2 * j + n + 1))
                            nc.scalar.copy(w_low[:, n, :, :], w_bank(n)[:, :, 1, :].rearrange("p t b -> p b t")).then_inc(w_read, 1)

                with act.Fori(NT, 2 * NT - 1) as i:
                    dense(i, True)
                dense(2 * NT - 1, False)

            @block.vector
            def _(dve):
                link = Link(dve, sem("dve_link5"))
                dve.wait_ge(iota_set, 1)
                nc.vector.tensor_copy(iota_k[:, :], iota_i[:, :])
                link(nc.vector.tensor_copy(iota_f[:, :], iota_i[:, 0:TOP]))

                def low(i, per, j):
                    r, half = j // 2 % 2, j % 2
                    dve.wait_ge(ut_hi, i * per + (j + 1))
                    part_of = slice(4 * half, 4 * half + 4)
                    nc.vector.tensor_tensor(uT[1][:, r, part_of, :].rearrange("p k n -> p (k n)"), PS[:, half, :],
                                            uT[0][:, r, part_of, :].rearrange("p k n -> p (k n)").bitcast(F32), ALU.subtract).then_inc(ut_lo, 1)

                with link.loop(NT, 20) as t:
                    done = [0, 0]

                    def beside(elements):
                        done[1] += elements + 60
                        while done[0] < 32 and done[1] * 32 >= CHOICE * (done[0] + 1):
                            low(t, 32, done[0])
                            done[0] += 1

                    def top16(values, indices, source, rest, count):
                        width = source.shape[2]
                        for n in range(count):
                            last = nc.vector.max(values(n)[:, 0:8], source[:, n, :])
                            if n < count - 1:
                                beside(width)
                        link(last, turn)
                        for n in range(count):
                            nc.vector.max_index(indices(n)[:, 0:8], values(n)[:, 0:8], source[:, n, :])
                            last = nc.vector.match_replace(rest[:, n, :], values(n)[:, 0:8], source[:, n, :], LOW)
                            if n < count - 1:
                                beside(2 * width + 60)
                        link(last, turn)
                        for n in range(count):
                            last = nc.vector.max(values(n)[:, 8:16], rest[:, n, :])
                            if n < count - 1:
                                beside(width)
                        link(last, turn)
                        for n in range(count):
                            last = nc.vector.max_index(indices(n)[:, 8:16], values(n)[:, 8:16], rest[:, n, :])
                            if n < count - 1:
                                beside(width)
                        link(last, turn)

                    dve.wait_ge(s_cur_set, t + 1)
                    dve.sem_inc(turn, 1)
                    top16(lambda n: best[:, n, :], lambda n: best_i[:, n, :], s_cur, s_rest, 2 * PH)
                    link(nc.vector.tensor_copy(best_f[:, :, :], best_i[:, :, :]))
                    pair = best[:, :, :].rearrange("p (h i) a -> p h i a", i=2)
                    link(nc.vector.tensor_tensor(cand.rearrange("p h (a b) -> p h a b", a=TOP),
                                                 pair[:, :, 0, :].unsqueeze(3).to_broadcast([P, PH, TOP, TOP]),
                                                 pair[:, :, 1, :].unsqueeze(2).to_broadcast([P, PH, TOP, TOP]), ALU.add), turn)
                    beside(2048)
                    dve.sem_inc(turn, 1)
                    top16(lambda n: top_v[:, n, :], lambda n: top_p[:, n * TOP:(n + 1) * TOP], cand, cand_rest, PH)
                    assert done[0] <= 2 * EXP_AT + 3, done
                    nc.vector.tensor_tensor(expo[:, :, :], top_v[:, :, :], top_v[:, :, 0:1].to_broadcast([P, PH, TOP]), ALU.subtract).then_inc(soft_in, 1)
                    nc.vector.tensor_scalar(part[:, 0, :], top_p[:, :], 4, None, ALU.logical_shift_right).then_inc(s_used, 1)
                    link(nc.vector.tensor_scalar(part[:, 1, :], top_p[:, :], 15, None, ALU.bitwise_and))
                    link(nc.vector.tensor_copy(part_f[:, :, :], part[:, :, :]))
                    index = best_f[:, :, :].rearrange("p (h i) a -> p h i a", i=2)
                    for i in range(2):
                        link(nc.vector.tensor_tensor(picks, part_f[:, i, :].unsqueeze(2).to_broadcast([P, SLOTS, TOP]),
                                                     iota_f[:, :].unsqueeze(1).to_broadcast([P, SLOTS, TOP]), ALU.is_equal))
                        beside(2048)
                        p4 = picks.rearrange("p (h k) a -> p h k a", h=PH)
                        link(nc.vector.tensor_tensor(p4, p4, index[:, :, i, :].unsqueeze(2).to_broadcast([P, PH, TOP, TOP]), ALU.mult))
                        beside(2048)
                        link(nc.vector.tensor_reduce(chosen[:, col(t), i, :].rearrange("p a s -> p (a s)"), picks, AX.X, ALU.add))
                        beside(2048)
                    for j in range(done[0], 32):
                        low(t, 32, j)
                    dve.wait_ge(soft_out, t + 1)
                    link(nc.vector.tensor_reduce(total[:, :], expo[:, :, :], AX.X, ALU.add))
                    link(nc.vector.reciprocal(total[:, :], total[:, :]))
                    nc.vector.tensor_tensor(chosen[:, col(t), 2, :].rearrange("p a (h k) -> p (a h) k", h=PH), expo[:, :, :],
                                            total[:, :].unsqueeze(2).to_broadcast([P, PH, TOP]), ALU.mult).then_inc(chosen_done, 1)

                dve.wait_ge(slot_full, 1)
                for a in range(3):
                    last = nc.vector.tensor_copy(slotT[:, a, :], PS[:, 4 + a, :])
                link(last)
                link(nc.vector.tensor_copy(partT[:, 0, :], slotT[:, 2, :]))
                nc.vector.tensor_tensor(partT[:, 1, :], slotT[:, 2, :], partT[:, 0, :].bitcast(F32), ALU.subtract).then_inc(slot_read, 1)
                dve.wait_ge(slot_read, 1)

                with dve.Fori(0, (NK - HALF) // 4) as i:
                    for j in range(8):
                        low(i + 2 * HALF // 8, 8, j)
                        r = j % HOTS
                        dve.wait_ge(w_full, i * 8 + (j + 1 - HOTS + CREDIT))
                        first = slotT[:, 0, bass.ds(i * (8 * TOK) + j * TOK, TOK)]
                        nc.vector.tensor_tensor(hot1[:, r, :, :], iota_k[:, :].unsqueeze(1).to_broadcast([P, TOK, NK]),
                                                first.unsqueeze(2).to_broadcast([P, TOK, NK]), ALU.is_equal)
                        for n in range(TOK):
                            at = bass.ds(i * (8 * TOK) + (j * TOK + n), 1)
                            for g in range(2):
                                last = nc.vector.tensor_scalar(hot2[:, r, n, g, :], iota_k[:, :], slotT[:, 1, at], partT[:, g, at].bitcast(F32), ALU.is_equal, ALU.mult)
                        last.then_inc(hot_done, 1)
        hidden.close()

        with ExitStack() as here:
            def tmp(name, shape, dtype=F32):
                return sb(name, shape, dtype, scope=here)

            a_raw = [a_first, tmp("a_raw1", [P, 4, SEQ])]
            w_raw = tmp("w_raw", [P, 2, SEQ // STAGE, 4, STAGE])
            v_hl = [tmp(f"v_{n}", [P, 2, D], F32R) for n in ("hi", "lo")]
            g_hl = [tmp(f"g_{n}", [P, 2, SEQ], F32R) for n in ("hi", "lo")]
            g_f = tmp("g_f", [P, 2, SEQ])
            zsq = tmp("zsq", [P, NT])
            zroot = tmp("zroot", [P, NT])
            zrstd = tmp("zrstd", [P, NT])
            zout = tmp("zout", [P, NT, D])
            v_hi, v_lo, g_done, g_hi, g_lo, pv_done = sem("v_hi"), sem("v_lo"), sem("g_done"), sem("g_hi"), sem("g_lo"), sem("pv_done")
            z_full, z_sq, z_root, z_out, out_done = sem("z_full"), sem("z_sq"), sem("z_root"), sem("z_out"), sem("out_done")
            block = here.enter_context(nc.Block())

            @block.sync
            def _(sp):
                def load_a(n, r):
                    sp.dma_start(a_raw[r][:, :, :], act_dram[:, bass.ds(n * 4, 4), :]).then_inc(aw_in[r], 16)

                def load_w(n, r):
                    sp.dma_start(w_raw[:, r, :, :, :], wgt_dram[:, :, bass.ds(n * 4, 4), :]).then_inc(aw_in[r], 16)

                for r in range(2):
                    sp.wait_ge(a_stored[r], 16 + 16 * NK // 4)
                sp.wait_ge(w_stored[0], 16 + 16 * SEQ // STAGE // 2)
                sp.wait_ge(w_stored[1], 16 + 16 * (SEQ // STAGE // 2 - 1))
                sp.wait_ge(w_first, 16)
                load_w(0, 0)
                sp.dma_start(wgt_dram[:, SEQ // STAGE - 1, AHEAD:NK, :], w_stage[:, 1, AHEAD:NK, :]).then_inc(w_stored[1], 16)
                load_a(1, 1)
                load_w(1, 1)
                sp.wait_ge(w_stored[1], 16 + 16 * SEQ // STAGE // 2)
                with sp.Fori(1, NK // 8) as i:
                    for r in range(2):
                        sp.wait_ge(v_lo, i * 8 + (4 * r - 4))
                        sp.wait_ge(g_done, i * 8 + (4 * r - 4))
                        load_v(sp, i * 2 + r, r)
                        load_a(i * 2 + r, r)
                        load_w(i * 2 + r, r)
                for t in range(NT):
                    sp.wait_ge(z_out, t + 1)
                    sp.dma_start(out[0, t * P:(t + 1) * P, :], x_sb[:, t, :]).then_inc(out_done, 16)
                sp.wait_ge(out_done, NT * 16)

            @block.tensor
            def _(pe):
                pe.sem_inc(pv_done, CREDIT)

                def parts_ready(i, j):
                    for s in (v_hi, v_lo, g_hi, g_lo):
                        pe.wait_ge(s, i * 4 + (j + 1))

                def products(j, t, start=False, stop=False):
                    for half in range(2):
                        for a, c_ in PARTS:
                            last = nc.tensor.matmul(PS[:, 2 * t + half, :], g_hl[a][:, j % 2, t * P:(t + 1) * P], v_hl[c_][:, j % 2, half * CH:(half + 1) * CH],
                                                    start=start and (a, c_) == PARTS[0], stop=stop and (a, c_) == PARTS[-1], skip_group_check=True)
                    return last

                def blocks(i, count=4, first=False):
                    for j in range(count):
                        parts_ready(i, j)
                        for t in range(NT):
                            last = products(j, t, start=first and j == 0)
                        last.then_inc(pv_done, 1)

                blocks(0, first=True)
                with pe.Fori(1, NK // 4 - 1) as i:
                    blocks(i)
                blocks(NK // 4 - 1, count=2)
                for j in (2, 3):
                    parts_ready(NK // 4 - 1, j)
                for t in range(NT):
                    products(2, t)
                    products(3, t, stop=True).then_inc(z_full, 1)

            @block.scalar
            def _(act):
                with act.Fori(0, NK // 8) as i:
                    for j in range(8):
                        if j % 4 == 0:
                            act.wait_ge(v_in[j // 4], i * 16 + 16)
                        act.wait_ge(pv_done, i * 8 + (j - 1 + CREDIT))
                        nc.scalar.copy(v_hl[0][:, j % 2, :], v_raw[:, j // 4, j % 4, :]).then_inc(v_hi, 1)
                        act.wait_ge(g_done, i * 8 + (j + 1))
                        nc.scalar.copy(g_hl[0][:, j % 2, :], g_f[:, j % 2, :]).then_inc(g_hi, 1)
                for t in range(NT):
                    act.wait_ge(z_full, t + 1)
                    y = PS[:, 2 * t:2 * t + 2, :].rearrange("p b n -> p (b n)")
                    nc.scalar.activation(zout[:, t, :], y, ACT.Square, accum_out=zsq[:, t:t + 1]).then_inc(z_sq, 1)
                    act.wait_ge(z_sq, t + 1)
                    nc.scalar.activation(zroot[:, t:t + 1], zsq[:, t:t + 1], ACT.Sqrt, bias=eps[:, :], scale=1.0 / D).then_inc(z_root, 1)

            @block.vector
            def _(dve):
                with dve.Fori(0, NK // 8) as i:
                    for j in range(8):
                        if j % 4 == 0:
                            dve.wait_ge(aw_in[j // 4], i * 32 + 32)
                        nc.vector.tensor_tensor(g_f[:, j % 2, :].rearrange("p (g t) -> p g t", t=STAGE), a_raw[j // 4][:, j % 4, :].rearrange("p (g t) -> p g t", t=STAGE),
                                                w_raw[:, j // 4, :, j % 4, :], ALU.mult).then_inc(g_done, 1)
                        dve.wait_ge(v_hi, i * 8 + (j + 1))
                        nc.vector.tensor_tensor(v_hl[1][:, j % 2, :], v_raw[:, j // 4, j % 4, :], v_hl[0][:, j % 2, :].bitcast(F32), ALU.subtract).then_inc(v_lo, 1)
                        dve.wait_ge(g_hi, i * 8 + (j + 1))
                        nc.vector.tensor_tensor(g_hl[1][:, j % 2, :], g_f[:, j % 2, :], g_hl[0][:, j % 2, :].bitcast(F32), ALU.subtract).then_inc(g_lo, 1)
                link = Link(dve, sem("dve_link6"))
                for t in range(NT):
                    dve.wait_ge(z_root, t + 1)
                    link(nc.vector.reciprocal(zrstd[:, t:t + 1], zroot[:, t:t + 1]))
                    y = PS[:, 2 * t:2 * t + 2, :].rearrange("p b n -> p (b n)")
                    link(nc.vector.scalar_tensor_tensor(out=zout[:, t, :], in0=y, scalar=zrstd[:, t:t + 1], in1=gates[:, 1, :], op0=ALU.mult, op1=ALU.mult))
                    nc.vector.tensor_tensor(x_sb[:, t, :], x_sb[:, t, :], zout[:, t, :], ALU.add).then_inc(z_out, 1)


_INS = ['x', 'c', 'ctx', 'c_ctx', 'w_mod', 'b_mod', 'g_pre1', 'g_post1', 'g_pre2', 'g_post2', 'w_in', 'g_q', 'g_kv', 'w_uq', 'w_ukv',
        'g_sgu', 'w_s', 'b_s', 'w_pa', 'w_pb', 'w_o', 'w_pq', 'k1', 'k2', 'u_exp', 'v_exp']


def rope_tables():
    quarter = ROPE // 4
    freqs = np.float32(10000.0) ** (-np.arange(quarter, dtype=np.float32) / np.float32(quarter))
    t = np.arange(SEQ)
    ang = [pos.astype(np.float32)[None, :] * freqs[:, None] for pos in (t // GRID_W, t % GRID_W)]
    cos = np.concatenate([np.cos(a) for a in ang for _ in range(2)])
    sin = np.concatenate([s * np.sin(a) for a in ang for s in (-1, 1)])
    return (np.ascontiguousarray(np.tile(z, (2, 1)).astype(np.float32)) for z in (cos, sin))


def kernel(**inputs):
    import concourse.bacc as bacc
    from concourse.bass_utils import run_bass_kernel_spmd

    nc = bacc.Bacc("TRN2", target_bir_lowering=False, num_devices=1)
    cos, sin = rope_tables()
    arrays, args = {}, []
    for name, a in [(n, inputs[n]) for n in _INS] + [("rope_cos", cos), ("rope_sin", sin)]:
        a = np.ascontiguousarray(a)
        arrays[f"in_{name}"] = a
        args.append(nc.dram_tensor(f"in_{name}", a.shape, mybir.dt.from_np(a.dtype), kind="ExternalInput").ap())
    args.append(nc.dram_tensor("out_0", (1, SEQ, D), F32, kind="ExternalOutput").ap())
    layer(nc, *args)
    r = run_bass_kernel_spmd(nc, [arrays], core_ids=[0])
    return r.results[0]["out_0"]
```
